# Optimizing a Trainium2 kernel written in Bass

```python
import math
import jax, jax.numpy as jnp
from jax import lax
import numpy as np

D_MODEL = 2048
BATCH = 1
SEQ = 256
DEPTH = 1

CHUNK = 64
D_MIX = D_MODEL
D_CONV = D_MIX // 2
D_MLSTM = D_MIX - D_CONV
CONV_K = 3
M_HEADS = 8
M_HEAD_DIM = D_MLSTM // M_HEADS
D_IN = 3 * D_CONV + 4 * D_MLSTM + 2 * M_HEADS
PEER_HEADS = 8
N_KEYS = 128
N_EXPERTS = N_KEYS * N_KEYS
PEER_TOPK = 16
PEER_QDIM = 256
PEER_HALF = PEER_QDIM // 2
PEER_BLOCK = 128
ALPHA = (2 * DEPTH) ** 0.25
BETA = (8 * DEPTH) ** -0.25
LN_EPS = 1e-5


def layernorm(x, g, b):
    xf = x.astype(jnp.float32)
    mu = jnp.mean(xf, axis=-1, keepdims=True)
    xc = xf - mu
    var = jnp.mean(xc * xc, axis=-1, keepdims=True)
    y = xc * lax.rsqrt(var + LN_EPS) * g.astype(jnp.float32) + b.astype(jnp.float32)
    return y.astype(x.dtype)

def causal_dwconv(z, w, b):
    S = z.shape[1]
    zp = jnp.pad(z, ((0, 0), (CONV_K - 1, 0), (0, 0)))
    y = b
    for j in range(CONV_K):
        y = y + w[j] * zp[:, j:j + S]
    return y

def mlstm_chunkwise(q, k, v, logi, logf):
    Bn, S, H, dh = q.shape
    L = CHUNK
    NC = S // L
    f32 = jnp.float32
    def to_chunks(t):
        return t.astype(f32).reshape(Bn, NC, L, H, dh).transpose(1, 0, 3, 2, 4)
    qc = to_chunks(q)
    kc = to_chunks(k) * (dh ** -0.5)
    vc = to_chunks(v)
    li = logi.astype(f32).reshape(Bn, NC, L, H).transpose(1, 0, 3, 2)
    lf = logf.astype(f32).reshape(Bn, NC, L, H).transpose(1, 0, 3, 2)
    mask = jnp.tril(jnp.ones((L, L), dtype=bool))

    def step(carry, inp):
        C, n, m = carry
        qb, kb, vb, lib, lfb = inp
        bcum = jnp.cumsum(lfb, axis=-1)
        Dm = bcum[..., :, None] - bcum[..., None, :] + lib[..., None, :]
        Dm = jnp.where(mask, Dm, -jnp.inf)
        inter = bcum + m[..., None]
        m_t = jnp.maximum(inter, jnp.max(Dm, axis=-1))
        w_intra = jnp.exp(Dm - m_t[..., None])
        w_inter = jnp.exp(inter - m_t)
        s = jnp.einsum('bhld,bhjd->bhlj', qb, kb) * w_intra
        num = (jnp.einsum('bhlj,bhjd->bhld', s, vb)
               + w_inter[..., None] * jnp.einsum('bhed,bhld->bhle', C, qb))
        den = jnp.sum(s, axis=-1) + w_inter * jnp.einsum('bhd,bhld->bhl', n, qb)
        h = num / jnp.maximum(jnp.abs(den), jnp.exp(-m_t))[..., None]
        bL = bcum[..., -1]
        g = bL[..., None] - bcum + lib
        m_new = jnp.maximum(bL + m, jnp.max(g, axis=-1))
        wk = jnp.exp(g - m_new[..., None])
        decay = jnp.exp(bL + m - m_new)
        C_new = decay[..., None, None] * C + jnp.einsum('bhl,bhle,bhld->bhed', wk, vb, kb)
        n_new = decay[..., None] * n + jnp.einsum('bhl,bhld->bhd', wk, kb)
        return (C_new, n_new, m_new), h

    init = (jnp.zeros((Bn, H, dh, dh), f32), jnp.zeros((Bn, H, dh), f32),
            jnp.zeros((Bn, H), f32))
    _, hs = lax.scan(step, init, (qc, kc, vc, li, lf))
    return hs.transpose(1, 0, 3, 2, 4).reshape(Bn, S, H, dh).astype(q.dtype)

def peer_ffn(h, wq, keys, u, v):
    Bn, S, D = h.shape
    xb = h.reshape(-1, PEER_BLOCK, D)

    def block(xt):
        q = (xt @ wq).reshape(-1, PEER_HEADS, 2, PEER_HALF)
        s = jnp.einsum('thpc,hpnc->thpn', q, keys)
        sv, si = lax.top_k(s, PEER_TOPK)
        cand = (sv[:, :, 0, :, None] + sv[:, :, 1, None, :]).reshape(-1, PEER_HEADS, PEER_TOPK * PEER_TOPK)
        cid = (si[:, :, 0, :, None] * N_KEYS + si[:, :, 1, None, :]).reshape(-1, PEER_HEADS, PEER_TOPK * PEER_TOPK)
        top_s, top_j = lax.top_k(cand, PEER_TOPK)
        eid = jnp.take_along_axis(cid, top_j, axis=-1)
        gate = jax.nn.softmax(top_s.astype(jnp.float32), axis=-1)
        ue = jnp.take(u, eid, axis=0)
        act = jax.nn.gelu(jnp.einsum('thkd,td->thk', ue, xt).astype(jnp.float32), approximate=False)
        ve = jnp.take(v, eid, axis=0)
        return jnp.einsum('thk,thkd->td', (gate * act).astype(xt.dtype), ve)

    return lax.map(block, xb).reshape(Bn, S, D)

def first_inputs(seed: int = 0) -> dict:
    key = jax.random.key(seed)
    ks = jax.random.split(key, 20)
    f32 = jnp.float32
    nrm = lambda k, shape: jax.random.normal(k, shape, f32)
    x = nrm(ks[0], (BATCH, SEQ, D_MODEL))
    ln_in_g = 1.0 + 0.05 * nrm(ks[1], (D_MODEL,))
    ln_in_b = 0.01 * nrm(ks[2], (D_MODEL,))
    col_scale = jnp.concatenate([
        jnp.ones((2 * D_CONV,), f32), jnp.full((D_CONV,), BETA, f32),
        jnp.ones((2 * D_MLSTM,), f32), jnp.full((D_MLSTM,), BETA, f32),
        jnp.ones((D_MLSTM + 2 * M_HEADS,), f32)])
    w_in = nrm(ks[3], (DEPTH, D_MODEL, D_IN)) * (D_MODEL ** -0.5) * col_scale
    b_i = 0.1 * nrm(ks[4], (DEPTH, M_HEADS))
    b_f = jnp.linspace(3.0, 6.0, M_HEADS, dtype=f32) + 0.1 * nrm(ks[5], (DEPTH, M_HEADS))
    b_gate = jnp.concatenate([b_i, b_f], axis=-1)
    conv_w = nrm(ks[6], (DEPTH, CONV_K, D_CONV)) * (CONV_K ** -0.5)
    conv_b = 0.01 * nrm(ks[7], (DEPTH, D_CONV))
    mh_norm_g = 1.0 + 0.05 * nrm(ks[8], (DEPTH, D_MLSTM))
    w_out = nrm(ks[9], (DEPTH, D_MIX, D_MODEL)) * (D_MIX ** -0.5) * BETA
    ln1_g = 1.0 + 0.05 * nrm(ks[10], (DEPTH, D_MODEL))
    ln1_b = 0.01 * nrm(ks[11], (DEPTH, D_MODEL))
    peer_wq = nrm(ks[12], (DEPTH, D_MODEL, PEER_HEADS * PEER_QDIM)) * (D_MODEL ** -0.5)
    peer_keys = nrm(ks[13], (DEPTH, PEER_HEADS, 2, N_KEYS, PEER_HALF)) * (PEER_HALF ** -0.5)
    peer_u = nrm(ks[14], (DEPTH, N_EXPERTS, D_MODEL)) * (D_MODEL ** -0.5) * BETA
    peer_v = nrm(ks[15], (DEPTH, N_EXPERTS, D_MODEL)) * (PEER_HEADS ** -0.5) * BETA
    ln2_g = 1.0 + 0.05 * nrm(ks[16], (DEPTH, D_MODEL))
    ln2_b = 0.01 * nrm(ks[17], (DEPTH, D_MODEL))
    return {"x": x, "ln_in_g": ln_in_g, "ln_in_b": ln_in_b, "w_in": w_in, "b_gate": b_gate,
            "conv_w": conv_w, "conv_b": conv_b, "mh_norm_g": mh_norm_g, "w_out": w_out,
            "ln1_g": ln1_g, "ln1_b": ln1_b, "peer_wq": peer_wq, "peer_keys": peer_keys,
            "peer_u": peer_u, "peer_v": peer_v, "ln2_g": ln2_g, "ln2_b": ln2_b}

def first_block(x, ln_in_g, ln_in_b, w_in, b_gate, conv_w, conv_b, mh_norm_g, w_out,
              ln1_g, ln1_b, peer_wq, peer_keys, peer_u, peer_v, ln2_g, ln2_b):
    Bn, S, D = x.shape
    split_at = np.cumsum([D_CONV, D_CONV, D_CONV, D_MLSTM, D_MLSTM, D_MLSTM, D_MLSTM, M_HEADS]).tolist()
    h = layernorm(x, ln_in_g, ln_in_b)
    for l in range(DEPTH):
        proj = h @ w_in[l]
        cB, cC, ch, q, k, v, o, gi, gf = jnp.split(proj, split_at, axis=-1)
        y_conv = cB * causal_dwconv(cC * ch, conv_w[l], conv_b[l])
        gates = (jnp.concatenate([gi, gf], axis=-1) + b_gate[l]).astype(jnp.float32)
        logi = gates[..., :M_HEADS]
        logf = jax.nn.log_sigmoid(gates[..., M_HEADS:])
        hd = lambda t: t.reshape(Bn, S, M_HEADS, M_HEAD_DIM)
        hm = mlstm_chunkwise(hd(q), hd(k), hd(v), logi, logf)
        hm = layernorm(hm, mh_norm_g[l].reshape(M_HEADS, M_HEAD_DIM),
                       jnp.zeros((M_HEADS, M_HEAD_DIM), hm.dtype))
        y_m = jax.nn.sigmoid(o) * hm.reshape(Bn, S, D_MLSTM)
        mix = jnp.concatenate([y_conv, y_m], axis=-1) @ w_out[l]
        h = layernorm(ALPHA * h + mix, ln1_g[l], ln1_b[l])
        ff = peer_ffn(h, peer_wq[l], peer_keys[l], peer_u[l], peer_v[l])
        h = layernorm(ALPHA * h + ff, ln2_g[l], ln2_b[l])
    return h


Q_BLOCK = 128
D_MIX_2 = D_MODEL
HGRN_WIDTH = D_MIX_2 // 2
HGRN_DK = 128
HGRN_HEADS = HGRN_WIDTH // HGRN_DK
HGRN_DV = HGRN_WIDTH // HGRN_HEADS
FOX_WIDTH = D_MIX_2 - HGRN_WIDTH
FOX_HEAD_DIM = 128
FOX_HEADS = FOX_WIDTH // FOX_HEAD_DIM
D_FF = ((8 * D_MODEL // 3 + 255) // 256) * 256
CONV_WIDTH = 3
EPS = 1e-6
FOX_GATE_BIAS_OFFSET = 2.0
IN_SIZES = (HGRN_HEADS * HGRN_DK, HGRN_HEADS * HGRN_DK, HGRN_WIDTH, HGRN_WIDTH,
            FOX_WIDTH, FOX_WIDTH, FOX_WIDTH, FOX_HEADS)
D_IN_2 = sum(IN_SIZES)


def rmsnorm(x, gain):
    x32 = x.astype(jnp.float32)
    y = x32 * lax.rsqrt(jnp.mean(x32 * x32, axis=-1, keepdims=True) + EPS) * gain.astype(jnp.float32)
    return y.astype(x.dtype)

def gla_chunkwise(q, k, v, logf):
    B, H, L, DK = q.shape
    DV = v.shape[-1]
    N = L // CHUNK
    r = lambda t: t.reshape(B, H, N, CHUNK, t.shape[-1])
    q, k, v, logf = r(q), r(k), r(v), r(logf)
    b = jnp.cumsum(logf, axis=-2)
    b_last = b[..., -1:, :]
    q_dec = q * jnp.exp(b)
    k_dec = k * jnp.exp(-b)
    k_end = k * jnp.exp(b_last - b)
    mask = jnp.tril(jnp.ones((CHUNK, CHUNK), dtype=bool))
    attn = jnp.einsum('bhnck,bhnsk->bhncs', q_dec, k_dec)
    attn = jnp.where(mask, attn, 0.0)
    o_intra = jnp.einsum('bhncs,bhnsv->bhncv', attn, v)
    chunk_decay = jnp.exp(b_last[..., 0, :])

    def step(S, xs):
        qd, ke, vv, dc = xs
        o = jnp.einsum('bhck,bhkv->bhcv', qd, S)
        S = dc[..., None] * S + jnp.einsum('bhck,bhcv->bhkv', ke, vv)
        return S, o

    xs = (jnp.moveaxis(q_dec, 2, 0), jnp.moveaxis(k_end, 2, 0),
          jnp.moveaxis(v, 2, 0), jnp.moveaxis(chunk_decay, 2, 0))
    S0 = jnp.zeros((B, H, DK, DV), jnp.float32)
    _, o_inter = lax.scan(step, S0, xs)
    o = o_intra + jnp.moveaxis(o_inter, 0, 2)
    return o.reshape(B, H, L, DV)

def hgrn2_mixer(q, f_logit, inp, g, lb, norm_gain):
    B, L, _ = q.shape
    dt = q.dtype
    heads = lambda t, d: t.reshape(B, L, HGRN_HEADS, d).transpose(0, 2, 1, 3).astype(jnp.float32)
    qh = heads(q, HGRN_DK) * (HGRN_DK ** -0.5)
    zh = heads(f_logit, HGRN_DK)
    vh = heads(inp, HGRN_DV)
    lbh = lb.astype(jnp.float32).reshape(HGRN_HEADS, HGRN_DK)[None, :, None, :]
    f = lbh + (1.0 - lbh) * jax.nn.sigmoid(zh)
    kh = 1.0 - f
    o = gla_chunkwise(qh, kh, vh, jnp.log(f))
    o = o * lax.rsqrt(jnp.mean(o * o, axis=-1, keepdims=True) + EPS) * norm_gain.astype(jnp.float32)
    o = o * jax.nn.silu(heads(g, HGRN_DV))
    return o.transpose(0, 2, 1, 3).reshape(B, L, HGRN_WIDTH).astype(dt)

def fox_mixer(q, k, v, f_logit, gate_bias):
    B, L, _ = q.shape
    dt = q.dtype
    heads = lambda t: t.reshape(B, L, FOX_HEADS, FOX_HEAD_DIM).transpose(0, 2, 1, 3)
    qh, kh, vh = heads(q), heads(k), heads(v)
    logf = jax.nn.log_sigmoid(f_logit.astype(jnp.float32) + gate_bias.astype(jnp.float32))
    c = jnp.cumsum(logf, axis=1).transpose(0, 2, 1)
    scale = FOX_HEAD_DIM ** -0.5
    kpos = jnp.arange(L)

    def one_block(blk):
        start = blk * Q_BLOCK
        qb = lax.dynamic_slice_in_dim(qh, start, Q_BLOCK, axis=2)
        cb = lax.dynamic_slice_in_dim(c, start, Q_BLOCK, axis=2)
        s = jnp.einsum('bhqd,bhkd->bhqk', qb, kh).astype(jnp.float32) * scale
        s = s + cb[..., :, None] - c[..., None, :]
        qpos = start + jnp.arange(Q_BLOCK)
        s = jnp.where(kpos[None, :] <= qpos[:, None], s, -jnp.inf)
        p = jax.nn.softmax(s, axis=-1)
        return jnp.einsum('bhqk,bhkd->bhqd', p.astype(vh.dtype), vh)

    out = lax.map(one_block, jnp.arange(L // Q_BLOCK))
    out = out.transpose(1, 0, 3, 2, 4).reshape(B, L, FOX_WIDTH)
    return out.astype(dt)

def conv_ffn(h, w_gate, w_up, conv_w, conv_b, w_down):
    L = h.shape[1]
    a = h @ w_gate
    a_pad = jnp.pad(a, ((0, 0), (CONV_WIDTH - 1, 0), (0, 0)))
    a = sum(conv_w[j] * a_pad[:, j:j + L] for j in range(CONV_WIDTH)) + conv_b
    return (jax.nn.silu(a) * (h @ w_up)) @ w_down

def second_inputs(seed: int = 0) -> dict:
    key = jax.random.key(seed)
    ks = jax.random.split(key, 16)
    nrm = lambda k, shape, s: jax.random.normal(k, shape, jnp.float32) * s
    return {
        'x': nrm(ks[0], (BATCH, SEQ, D_MODEL), 1.0),
        'norm1_gain': 1.0 + nrm(ks[1], (DEPTH, D_MODEL), 0.02),
        'w_in': nrm(ks[2], (DEPTH, D_MODEL, D_IN_2), D_MODEL ** -0.5),
        'hgrn_lb_param': nrm(ks[3], (DEPTH + 1, HGRN_HEADS * HGRN_DK), 0.5),
        'hgrn_norm_gain': 1.0 + nrm(ks[4], (DEPTH, HGRN_DV), 0.02),
        'fox_gate_bias': FOX_GATE_BIAS_OFFSET + nrm(ks[5], (DEPTH, FOX_HEADS), 0.1),
        'w_out': nrm(ks[6], (DEPTH, D_MIX_2, D_MODEL), D_MIX_2 ** -0.5),
        'norm2_gain': 1.0 + nrm(ks[7], (DEPTH, D_MODEL), 0.02),
        'w_ffn_gate': nrm(ks[8], (DEPTH, D_MODEL, D_FF), D_MODEL ** -0.5),
        'w_ffn_up': nrm(ks[9], (DEPTH, D_MODEL, D_FF), D_MODEL ** -0.5),
        'ffn_conv_w': nrm(ks[10], (DEPTH, CONV_WIDTH, D_FF), CONV_WIDTH ** -0.5),
        'ffn_conv_b': nrm(ks[11], (DEPTH, D_FF), 0.02),
        'w_ffn_down': nrm(ks[12], (DEPTH, D_FF, D_MODEL), D_FF ** -0.5),
        'final_norm_gain': 1.0 + nrm(ks[13], (D_MODEL,), 0.02),
    }

def second_block(x, norm1_gain, w_in, hgrn_lb_param, hgrn_norm_gain, fox_gate_bias, w_out,
              norm2_gain, w_ffn_gate, w_ffn_up, ffn_conv_w, ffn_conv_b, w_ffn_down,
              final_norm_gain):
    split_points = [int(v) for v in np.cumsum(IN_SIZES)[:-1]]
    lb_all = jnp.cumsum(jax.nn.softmax(hgrn_lb_param.astype(jnp.float32), axis=0), axis=0)
    for l in range(DEPTH):
        h = rmsnorm(x, norm1_gain[l])
        proj = h @ w_in[l]
        q_a, f_a, i_a, g_a, q_b, k_b, v_b, f_b = jnp.split(proj, split_points, axis=-1)
        o_a = hgrn2_mixer(q_a, f_a, i_a, g_a, lb_all[l], hgrn_norm_gain[l])
        o_b = fox_mixer(q_b, k_b, v_b, f_b, fox_gate_bias[l])
        x = x + jnp.concatenate([o_a, o_b], axis=-1) @ w_out[l]
        h = rmsnorm(x, norm2_gain[l])
        x = x + conv_ffn(h, w_ffn_gate[l], w_ffn_up[l], ffn_conv_w[l], ffn_conv_b[l], w_ffn_down[l])
    return rmsnorm(x, final_norm_gain)


def setup_inputs(seed=0):
    out = dict(first_inputs(seed))
    for name, value in second_inputs(seed + 1).items():
        if name != "x":
            out[name + "_2"] = value
    return out


def reference(
    x, ln_in_g, ln_in_b, w_in, b_gate, conv_w, conv_b, mh_norm_g, w_out, ln1_g, ln1_b, peer_wq,
    peer_keys, peer_u, peer_v, ln2_g, ln2_b, norm1_gain_2, w_in_2, hgrn_lb_param_2,
    hgrn_norm_gain_2, fox_gate_bias_2, w_out_2, norm2_gain_2, w_ffn_gate_2, w_ffn_up_2,
    ffn_conv_w_2, ffn_conv_b_2, w_ffn_down_2, final_norm_gain_2,
):
    x = first_block(
        x, ln_in_g, ln_in_b, w_in, b_gate, conv_w, conv_b, mh_norm_g, w_out, ln1_g, ln1_b,
        peer_wq, peer_keys, peer_u, peer_v, ln2_g, ln2_b,
    )
    return second_block(
        x, norm1_gain_2, w_in_2, hgrn_lb_param_2, hgrn_norm_gain_2, fox_gate_bias_2, w_out_2,
        norm2_gain_2, w_ffn_gate_2, w_ffn_up_2, ffn_conv_w_2, ffn_conv_b_2, w_ffn_down_2,
        final_norm_gain_2,
    )


_drawn_inputs = setup_inputs


def setup_inputs(seed=0):
    import zlib

    import numpy as np

    out = dict(_drawn_inputs(seed))
    spreads = {}
    factors = {'ln_in_b': 2.806,
     'conv_b': 8.0,
     'mh_norm_g': 4.107,
     'ln1_b': 3.117,
     'ln2_b': 3.267,
     'norm1_gain_2': 2.834,
     'hgrn_norm_gain_2': 7.79,
     'fox_gate_bias_2': 3.011,
     'norm2_gain_2': 11.127,
     'ffn_conv_b_2': 31.701,
     'final_norm_gain_2': 21.442}
    for name, (base, spread) in spreads.items():
        noise = np.random.default_rng([zlib.crc32(name.encode()), seed]).standard_normal(out[name].shape)
        drawn = base * np.exp(spread * noise) if base else spread * noise
        out[name] = __import__('jax').numpy.asarray(drawn.astype(out[name].dtype))
    for name, factor in factors.items():
        out[name] = (out[name] * factor).astype(out[name].dtype)
    return out
```

```python
from contextlib import ExitStack

import concourse.bass as bass
from concourse import mybir

F32 = mybir.dt.float32
F32R = mybir.dt.float32r
I32 = mybir.dt.int32
U32 = mybir.dt.uint32
ALU = mybir.AluOpType
ACT = mybir.ActivationFunctionType
AX = mybir.AxisListType.X
ds = bass.ds

P = 128
T = 256
TB = T // P
D = 2048
DC = D // P
W = 512
UC = 4
UNITS = DC // UC
H = 8
DH = 128
HW = H * DH
CHUNK = 64
NCH = T // CHUNK
FF = 5632
FC = FF // P
FPAIRS = FF // W
NEXP = 16384
NKEY = 128
TOPK = 16
ALPHA = 2.0 ** 0.25
LN_EPS = 1e-5
RMS_EPS = 1e-6
LOWEST = -3.0e38
SCALE = float(DH) ** -0.5
RING = 4

S_IN, S_OUT, S_WQ, S_IN2, S_OUT2, S_FF, S_DOWN = 0, 14, 18, 22, 36, 40, 62
NDOWN = FC // UC


def wait_alone(eng, sem, value, passed):
    eng.wait_ge(sem, value).then_inc(passed, 1)


class Chain:

    def __init__(self, eng, sem, passed):
        self.eng, self.sem, self.passed, self.n, self.reg, self.per = eng, sem, passed, 0, None, 0

    def __call__(self, instruction, *signals):
        self.n += 1
        instruction.then_inc(self.sem, 1)
        value = self.n if self.reg is None else self.reg * self.per + self.n
        for s in signals:
            self.eng.wait_ge(self.sem, value).then_inc(s, 1)
        if not signals and self.reg is None:
            self.eng.wait_ge(self.sem, value)
        elif not signals:
            wait_alone(self.eng, self.sem, value, self.passed)

    def enter(self, reg, first, per):
        self.reg, self.per, self.at = reg, per, self.n
        self.n -= first * per

    def leave(self, first, trips):
        made = self.n + first * self.per - self.at
        assert made == self.per, f"the loop's body makes {made} links"
        self.n = self.at + trips * self.per
        self.reg = None


def block_kernel(nc, inp, out):
    ctx = ExitStack()
    with ctx:
        build(nc, inp, out, ctx)


def build(nc, inp, out, ctx):
    def sem(name):
        return ctx.enter_context(nc.semaphore(name))

    class S:

        x_in = sem("x_in")
        norm_in = sem("norm_in")
        stage_clear = sem("stage_clear")
        stage_in = sem("stage_in")
        small_in = sem("small_in")
        wf_in = sem("wf_in")
        keys_in = sem("keys_in")
        stored = sem("stored")
        ident_ready = sem("ident_ready")
        consts = sem("consts")
        pool_chain = sem("pool_chain")
        pool_passed = sem("pool_passed")
        act_chain = sem("act_chain")
        act_passed = sem("act_passed")
        dve_chain = sem("dve_chain")
        dve_passed = sem("dve_passed")
        square_ready = sem("square_ready")
        root_ready = sem("root_ready")
        tm_ready = sem("tm_ready")
        xt_ps = sem("xt_ps")
        xt_hi = sem("xt_hi")
        xt_lo = sem("xt_lo")
        cols_ps = sem("cols_ps")
        cols_ready = sem("cols_ready")
        mix_y = sem("mix_y")
        mix_a = sem("mix_a")
        mix_hi = sem("mix_hi")
        mix_lo = sem("mix_lo")
        conv_done = sem("conv_done")
        wg_hi = sem("wg_hi")
        wg_lo = sem("wg_lo")
        wf_hi = sem("wf_hi")
        wf_lo = sem("wf_lo")
        gate_ps = sem("gate_ps")
        gate_abs = sem("gate_abs")
        gate_ln = sem("gate_ln")
        gates_tm = sem("gates_tm")
        gates_T = sem("gates_T")
        gates_cm = sem("gates_cm")
        gates_back = sem("gates_back")
        em_arg = sem("em_arg")
        em_ready = sem("em_ready")
        m_scores = sem("m_scores")
        m_arg = sem("m_arg")
        m_exp = sem("m_exp")
        m_prob = sem("m_prob")
        m_num = sem("m_num")
        m_numcp = sem("m_numcp")
        m_y = sem("m_y")
        m_turn = sem("m_turn")
        keyT_ps = sem("keyT_ps")
        keyT = sem("keyT")
        score_ps = sem("score_ps")
        scores_cp = sem("scores_cp")
        soft_arg = sem("soft_arg")
        soft_exp = sem("soft_exp")
        uidx_ready = sem("uidx_ready")
        dot_done = sem("dot_done")
        dots_ready = sem("dots_ready")
        gelu_ready = sem("gelu_ready")
        ew_ready = sem("ew_ready")
        diag_ready = sem("diag_ready")
        v_done = sem("v_done")
        acc_done = sem("acc_done")
        ffsum = sem("ffsum")
        ln2_done = sem("ln2_done")
        nrm = sem("nrm")
        nrm_used = sem("nrm_used")
        lb_arg = sem("lb_arg")
        lb_exp = sem("lb_exp")
        f_ready = sem("f_ready")
        lnf_ready = sem("lnf_ready")
        b_ready = sem("b_ready")
        expb_ready = sem("expb_ready")
        dcay_ready = sem("dcay_ready")
        ke_arg = sem("ke_arg")
        expe_ready = sem("expe_ready")
        q_decayed = sem("q_decayed")
        expnb_ready = sem("expnb_ready")
        k_decayed = sem("k_decayed")
        c_ready = sem("c_ready")
        g_keT = sem("g_keT")
        g_ke = sem("g_ke")
        g_attn = sem("g_attn")
        g_ds = sem("g_ds")
        g_state = sem("g_state")
        g_o = sem("g_o")
        g_ocp = sem("g_ocp")
        g_y = sem("g_y")
        g_turn = sem("g_turn")
        a_scores = sem("a_scores")
        a_max = sem("a_max")
        a_exp = sem("a_exp")
        a_prob = sem("a_prob")
        a_pT = sem("a_pT")
        a_pTcp = sem("a_pTcp")
        a_out = sem("a_out")
        ff_y = sem("ff_y")
        ff_conv = sem("ff_conv")
        ff_silu = sem("ff_silu")
        ff_up = sem("ff_up")
        ah_full = sem("ah_full")
        al_full = sem("al_full")
        down_done = sem("down_done")
        final = sem("final")

    base = (nc.sbuf_base + 63) // 64 * 64
    total = nc.sbuf_usable_end - base
    ctx.enter_context(nc.sbuf_tensor("arena", [P, total // 4 - 32], F32))
    K = 1024

    def at(name, kb, shape, dt=F32):
        return nc.alloc_sbuf_tensor_at(name, [P, *shape], dt, offset=base + int(kb * K))

    raw = [at(f"raw{k}", 8 * k, [UC, W]) for k in range(UNITS)]
    wh = [at(f"wh{k}", 32 + 8 * k, [UC, W], F32R) for k in range(2)]
    wl = [at(f"wl{k}", 48 + 8 * k, [UC, W], F32R) for k in range(2)]
    XH = at("XH", 64, [DC, T], F32R)
    XL = at("XL", 80, [DC, T], F32R)
    RES = at("RES", 96, [TB, D])
    MIX = at("MIX", 112, [DC, T])
    GAIN = at("GAIN", 112, [D])
    BIAS = at("BIAS", 120, [D])
    ident = at("ident", 128, [P])
    mask01 = at("mask01", 128.5, [384])
    maskneg = at("maskneg", 130, [384])
    hmask = at("hmask", 131.5, [P])
    smask = at("smask", 132, [T])
    ones = at("ones", 133, [T])
    iota_i = at("iota_i", 134, [TOPK], I32)
    iota_f = at("iota_f", 134.125, [TOPK])
    stage = at("stage", 134.25, [3, P])
    cols = at("cols", 135.75, [3, P])
    SM = 137.25
    bgate = at("bgate", SM, [16])
    fbias = at("fbias", SM + 0.0625, [H])
    hgain = at("hgain", SM + 0.125, [DH])
    stats = at("stats", SM + 0.625, [4, 6])
    mv = at("mv", SM + 0.75, [TB, 2])
    rstd = at("rstd", SM + 0.8125, [TB])
    msq = at("msq", SM + 0.84375, [TB])
    glog = at("glog", SM + 0.875, [TB, 16])
    gabs = at("gabs", SM + 1, [TB, 16])
    gln = at("gln", SM + 1.125, [TB, 16])
    lb0 = at("lb0", SM + 1.25, [H])
    lb1 = at("lb1", SM + 1.28125, [H])
    lbm = at("lbm", SM + 1.3125, [H])
    lbs = at("lbs", SM + 1.34375, [H])
    lb = at("lb", SM + 1.375, [H])
    omlb = at("omlb", SM + 1.40625, [H])
    dcay = at("dcay", SM + 1.4375, [H, NCH])
    PH = 139
    ZC = at("ZC", PH, [H, T + 2])
    QT = at("QT", PH + 8.25, [H, T])
    KT = at("KT", PH + 16.25, [H, T])
    VX = at("VX", PH + 24.25, [TB, H, DH + 2])
    OG = at("OG", PH + 33, [TB, HW])
    mhg = at("mhg", PH + 41, [HW])
    wg_raw = at("wg_raw", PH + 46, [DC, 16])
    wg_h = at("wg_h", PH + 47, [DC, 16], F32R)
    wg_l = at("wg_l", PH + 48, [DC, 16], F32R)
    GP = at("GP", 64, [TB, P])
    BP = at("BP", 65, [T])
    RA = at("RA", 66, [T])
    LF = at("LF", 67, [T])
    LI = at("LI", 68, [T])
    FS = at("FS", 69, [T])
    CM = at("CM", 70, [T])
    bcol = at("bcol", 71, [TB, H])
    emcol = at("emcol", 71.0625, [TB, H])
    den = at("den", 71.125, [TB, H])
    hstat = at("hstat", 71.25, [H, 6])
    hmv = at("hmv", 71.5, [H, 2])
    hr = at("hr", 71.625, [H])
    nmax = at("nmax", 71.75, [2, TB])
    psum_ = at("psum_", 71.8125, [2, TB])
    E = at("E", 72, [2, 384])
    PM = at("PM", 75, [2, 384])
    HN = at("HN", 78, [TB, H, DH + 2])
    AT = at("AT", 72, [2, TB, P])
    ST = at("ST", 74, [2, 3, P])
    KE = at("KE", 87, [2, NCH - 1, DH])
    G_F = at("G_F", PH, [H, T])
    G_B = at("G_B", PH + 8, [H, T])
    G_Q = at("G_Q", PH + 16, [H, T])
    G_E = at("G_E", PH + 24, [H, T])
    G_K = at("G_K", PH + 32, [H, T])
    G_V = at("G_V", PH + 40, [TB, HW])
    G_G = at("G_G", PH + 48, [TB, HW])
    FQ = at("FQ", PH, [H, T])
    FK = at("FK", PH + 8, [H, T])
    FV = at("FV", PH + 56, [TB, HW])
    wf_raw = at("wf_raw", PH + 64, [DC, H])
    wf_h = at("wf_h", PH + 64.5, [DC, H], F32R)
    wf_l = at("wf_l", PH + 65, [DC, H], F32R)
    PQ = at("PQ", 112, [DC, T])
    KR = at("KR", PH, [DC, P])
    KX = at("KX", PH + 8, [DC, P])
    SC = at("SC", 64, [TB, H + 1, 2, NKEY])
    TK = 90.5
    sc = at("sc", TK, [2, NKEY])
    sc2 = at("sc2", TK + 1, [2, NKEY])
    best = at("best", TK + 2, [2, TOPK])
    bidx = at("bidx", TK + 2.125, [2, TOPK], U32)
    bidf = at("bidf", TK + 2.25, [2, TOPK])
    tops = at("tops", TK + 2.375, [TOPK])
    topj = at("topj", TK + 2.4375, [TOPK], U32)
    tij = at("tij", TK + 2.5, [2, TOPK], U32)
    tijf = at("tijf", TK + 2.625, [2, TOPK])
    eids = at("eids", TK + 2.75, [2, TOPK])
    eidf = at("eidf", TK + 2.875, [TOPK])
    nmx = at("nmx", TK + 2.9375, [1])
    esum = at("esum", TK + 2.96875, [1])
    rsum = at("rsum", TK + 3, [1])
    eexp = at("eexp", TK + 3.0625, [TOPK])
    gate = at("gate", TK + 3.125, [2, TOPK])
    uidx = at("uidx", TK + 3.25, [2, TOPK], U32)
    vidx = at("vidx", TK + 3.375, [2, TOPK], U32)
    dots = at("dots", TK + 3.5, [2, TOPK])
    acts = at("acts", TK + 3.625, [2, TOPK])
    ew = at("ew", TK + 3.75, [2, TOPK])
    cand = at("cand", 112, [TOPK, TOPK])
    cand2 = at("cand2", 113, [TOPK, TOPK])
    hot = at("hot", 114, [2, TOPK, TOPK])
    diag = at("diag", 120, [TOPK, P])
    ub = [at(f"ub{k}", PH + 8 * k, [D]) for k in range(RING)]
    vb = [at(f"vb{k}", PH + 32 + 8 * k, [D]) for k in range(RING)]
    NRM = at("NRM", PH, [TB, D])
    FA = at("FA", PH, [FC, T])
    FY = at("FY", PH + 44, [4, T])
    ah = [at(f"ah{k}", PH + 48 + k, [T], F32R) for k in range(2)]
    al = [at(f"al{k}", PH + 50 + k, [T], F32R) for k in range(2)]

    PS = ctx.enter_context(nc.psum_tensor("PS", [P, 8, 512], F32))

    raw_full = [sem(f"raw_full{k}") for k in range(UNITS)]
    hi_full = [sem(f"hi_full{k}") for k in range(2)]
    lo_full = [sem(f"lo_full{k}") for k in range(2)]
    w_free = [sem(f"w_free{k}") for k in range(2)]
    evac = [sem(f"evac{k}") for k in range(2)]
    u_full = [sem(f"u_full{k}") for k in range(RING)]
    v_full = [sem(f"v_full{k}") for k in range(RING)]

    def w_view(w):
        return w[0].rearrange("(c p) n -> p c n", p=P)

    def load_unit(sp, s, u, src):
        if not (isinstance(s, int) and s == 0):
            sp.wait_ge(lo_full[u % 2], (s - 1) * 2 + u // 2 + 1)
        sp.dma_start(raw[u][:], src).then_inc(raw_full[u], 16)

    def split_hi(act, s, u):
        act.wait_ge(raw_full[u], (s + 1) * 16)
        if not (isinstance(s, int) and s == 0 and u < 2):
            act.wait_ge(w_free[u % 2], s * 2 + u // 2)
        act.copy(wh[u % 2][:], raw[u][:]).then_inc(hi_full[u % 2], 1)

    def split_lo(dve, s, u):
        dve.wait_ge(hi_full[u % 2], s * 2 + u // 2 + 1)
        dve.tensor_tensor(wl[u % 2][:], raw[u][:], wh[u % 2][:].bitcast(F32),
                          ALU.subtract).then_inc(lo_full[u % 2], 1)

    def slab_ready(eng, s):
        eng.wait_ge(w_free[1], s * 2 + 2)

    def run_slabs(eng, split, s0, evacs):
        for j in range(len(evacs)):
            split(eng, s0 + j, 0)
            split(eng, s0 + j, 1)
            if j and evacs[j - 1]:
                evacs[j - 1](s0 + j - 1)
            split(eng, s0 + j, 2)
            split(eng, s0 + j, 3)
        if evacs[-1]:
            evacs[-1](s0 + len(evacs) - 1)

    def cm_out(buf):
        return PS[:, 2 * buf:2 * buf + 2, :].rearrange("p b (t n) -> p (b t) n", n=T)

    def tm_out(buf):
        return PS[:, 2 * buf:2 * buf + 2, :]

    def pe_slab(pe, half, buf, cm):
        if not (isinstance(half, int) and half == 0):
            pe.wait_ge(evac[buf], half)
        for u in range(UNITS):
            pe.wait_ge(lo_full[u % 2], half * 4 + buf * 2 + u // 2 + 1)
            mm_unit(pe, u, buf, cm).then_inc(w_free[u % 2], 1)

    def mm_unit(pe, u, buf, cm):
        k = u % 2
        if cm:
            o = cm_out(buf)
            for t in range(4):
                for c in range(UC):
                    x = slice(t * P, t * P + P)
                    d = u * UC + c
                    first = u == 0 and c == 0 and t % 2 == 0
                    pe.matmul(o[:, t, :], wh[k][:, c, x], XH[:, d, :], start=first, stop=False,
                              skip_group_check=True)
                    pe.matmul(o[:, t, :], wh[k][:, c, x], XL[:, d, :], start=False, stop=False,
                              skip_group_check=True)
                    m = pe.matmul(o[:, t, :], wl[k][:, c, x], XH[:, d, :], start=False,
                                  stop=d == DC - 1, skip_group_check=True)
            return m
        o = tm_out(buf)
        for tb in range(TB):
            y = slice(tb * P, tb * P + P)
            for c in range(UC):
                d = u * UC + c
                pe.matmul(o[:, tb, :], XH[:, d, y], wh[k][:, c, :], start=d == 0, stop=False,
                          skip_group_check=True)
                pe.matmul(o[:, tb, :], XH[:, d, y], wl[k][:, c, :], start=False, stop=False,
                          skip_group_check=True)
                m = pe.matmul(o[:, tb, :], XL[:, d, y], wh[k][:, c, :], start=False,
                              stop=d == DC - 1, skip_group_check=True)
        return m

    def bank2(b):
        return PS[:, b, :].rearrange("p (c n) -> p c n", n=T)

    def turn_x(pe, n, src):
        pe.wait_ge(S.tm_ready, n + 1)
        for g in range(8):
            if g >= 4:
                pe.wait_ge(S.xt_lo, 8 * n + g - 3)
            for c in range(2):
                for tb in range(TB):
                    m = pe.transpose(bank2(4 + g % 4)[:, c, tb * P:tb * P + P],
                                     src[:, tb, (2 * g + c) * P:(2 * g + c + 1) * P], ident[:])
            m.then_inc(S.xt_ps, 1)

    def x_hi(act, n):
        for g in range(8):
            act.wait_ge(S.xt_ps, 8 * n + g + 1)
            act.copy(XH[:, 2 * g:2 * g + 2, :], bank2(4 + g % 4)).then_inc(S.xt_hi, 1)

    def x_lo(dve, n):
        for g in range(8):
            dve.wait_ge(S.xt_hi, 8 * n + g + 1)
            dve.tensor_tensor(XL[:, 2 * g:2 * g + 2, :], bank2(4 + g % 4),
                              XH[:, 2 * g:2 * g + 2, :].bitcast(F32), ALU.subtract).then_inc(S.xt_lo, 1)

    def mix_hi(act, n):
        for g in range(4):
            act.copy(XH[:, 4 * g:4 * g + 4, :], MIX[:, 4 * g:4 * g + 4, :]).then_inc(S.mix_hi, 1)

    def mix_lo(dve, n):
        for g in range(4):
            dve.wait_ge(S.mix_hi, 4 * n + g + 1)
            dve.tensor_tensor(XL[:, 4 * g:4 * g + 4, :], MIX[:, 4 * g:4 * g + 4, :],
                              XH[:, 4 * g:4 * g + 4, :].bitcast(F32), ALU.subtract).then_inc(S.mix_lo, 1)

    def bcast(v, shape):
        return v.to_broadcast([P, *shape])

    block = ctx.enter_context(nc.Block())

    @block.sync
    def _(sp):
        def row(v, n):
            return v.partition_broadcast(P)

        for tb in range(TB):
            sp.dma_start(RES[:, tb, :], inp["x"][0].rearrange("(b p) d -> b p d", p=P)[tb]).then_inc(S.x_in, 16)
        sp.dma_start(GAIN[:], row(inp["ln_in_g"], D)).then_inc(S.norm_in, 16)
        sp.dma_start(BIAS[:], row(inp["ln_in_b"], D)).then_inc(S.norm_in, 16)
        sp.wait_ge(S.stage_clear, 1)
        sp.dma_start(stage[0:24, 0, :], inp["conv_w"][0].rearrange("j (c p) -> (j c) p", p=P)).then_inc(S.stage_in, 16)
        sp.dma_start(stage[24:32, 0, :], inp["conv_b"][0].rearrange("(c p) -> c p", p=P)).then_inc(S.stage_in, 16)
        sp.dma_start(stage[32:48, 0, :], inp["hgrn_lb_param_2"].rearrange("l (c p) -> (l c) p", p=P)).then_inc(S.stage_in, 16)
        fw = inp["ffn_conv_w_2"][0].rearrange("j (c p) -> j c p", p=P)
        sp.dma_start(stage[0:FC, 1, :], fw[0]).then_inc(S.stage_in, 16)
        sp.dma_start(stage[FC:2 * FC, 1, :], fw[1]).then_inc(S.stage_in, 16)
        sp.dma_start(stage[0:FC, 2, :], fw[2]).then_inc(S.stage_in, 16)
        sp.dma_start(stage[FC:2 * FC, 2, :], inp["ffn_conv_b_2"][0].rearrange("(c p) -> c p", p=P)).then_inc(S.stage_in, 16)
        sp.dma_start(bgate[:], row(inp["b_gate"][0], 16)).then_inc(S.small_in, 16)
        sp.dma_start(fbias[:], row(inp["fox_gate_bias_2"][0], H)).then_inc(S.small_in, 16)
        sp.dma_start(hgain[:], row(inp["hgrn_norm_gain_2"][0], DH)).then_inc(S.small_in, 16)
        sp.dma_start(mhg[:], row(inp["mh_norm_g"][0], HW)).then_inc(S.small_in, 16)
        w_in = w_view(inp["w_in"])
        sp.dma_start(wg_raw[:], w_in[:, :, 14 * W:14 * W + 16]).then_inc(S.small_in, 16)

        def stream(s0, w, c0, n):
            if s0 == 0:
                for u in range(UNITS):
                    load_unit(sp, 0, u, w[:, u * UC:(u + 1) * UC, c0:c0 + W])
                s0, c0, n = 1, c0 + W, n - 1
            with sp.Fori(0, n) as i:
                for u in range(UNITS):
                    load_unit(sp, i + s0, u, w[:, u * UC:(u + 1) * UC, ds(i * W + c0, W)])

        stream(0, w_in, 2 * W, 4)
        stream(4, w_in, 0, 2)
        stream(6, w_in, 6 * W, 8)
        stream(S_OUT, w_view(inp["w_out"]), 0, 4)
        sp.wait_ge(S.mix_lo, 4)
        sp.dma_start(GAIN[:], row(inp["ln1_g"][0], D)).then_inc(S.norm_in, 16)
        sp.dma_start(BIAS[:], row(inp["ln1_b"][0], D)).then_inc(S.norm_in, 16)
        keys = inp["peer_keys"][0].rearrange("h q n c -> (h q) n c")
        for n in range(2 * H):
            sp.dma_start(KR[:, n, :], keys[n]).then_inc(S.keys_in, 16)
        stream(S_WQ, w_view(inp["peer_wq"]), 0, 4)
        w_in2 = w_view(inp["w_in_2"])
        for u in range(UNITS):
            load_unit(sp, S_IN2, u, w_in2[:, u * UC:(u + 1) * UC, 2 * W:3 * W])
        sp.wait_ge(S.ffsum, 8)
        sp.dma_start(GAIN[:], row(inp["ln2_g"][0], D)).then_inc(S.norm_in, 16)
        sp.dma_start(BIAS[:], row(inp["ln2_b"][0], D)).then_inc(S.norm_in, 16)
        sp.dma_start(wf_raw[:], w_in2[:, :, 14 * W:14 * W + H]).then_inc(S.wf_in, 16)
        sp.wait_ge(S.ln2_done, 1)
        sp.dma_start(GAIN[:], row(inp["norm1_gain_2"][0], D)).then_inc(S.norm_in, 16)
        with sp.Fori(0, 1) as i:
            for u in range(UNITS):
                load_unit(sp, i + S_IN2 + 1, u, w_in2[:, u * UC:(u + 1) * UC, ds(i * W + 3 * W, W)])
        stream(S_IN2 + 2, w_in2, 0, 2)
        stream(S_IN2 + 4, w_in2, 8 * W, 4)
        stream(S_IN2 + 8, w_in2, 4 * W, 4)
        stream(S_IN2 + 12, w_in2, 12 * W, 2)
        stream(S_OUT2, w_view(inp["w_out_2"]), 0, 4)
        sp.wait_ge(S.mix_lo, 8)
        sp.dma_start(GAIN[:], row(inp["norm2_gain_2"][0], D)).then_inc(S.norm_in, 16)
        wgt, wup = w_view(inp["w_ffn_gate_2"]), w_view(inp["w_ffn_up_2"])
        with sp.Fori(0, FPAIRS) as i:
            for k, w in enumerate((wgt, wup)):
                for u in range(UNITS):
                    load_unit(sp, i * 2 + S_FF + k, u, w[:, u * UC:(u + 1) * UC, ds(i * W, W)])
        wdn = inp["w_ffn_down_2"][0].rearrange("(c p) (b n) -> c p b n", p=P, n=W)
        with sp.Fori(0, NDOWN) as i:
            for u in range(UNITS):
                load_unit(sp, i + S_DOWN, u, wdn[ds(i * UNITS + u, 1)].rearrange("o p b n -> (o p) b n"))
        sp.wait_ge(S.tm_ready, 4)
        sp.dma_start(GAIN[:], row(inp["final_norm_gain_2"], D)).then_inc(S.norm_in, 16)
        for tb in range(TB):
            sp.wait_ge(S.final, tb + 1)
            sp.dma_start(out[0].rearrange("(b p) d -> b p d", p=P)[tb], RES[:, tb, :]).then_inc(S.stored, 16)
        sp.wait_ge(S.stored, 16 * TB)

    @block.gpsimd
    def _(pool):
        link = Chain(pool, S.pool_chain, S.pool_passed)
        pool.memset(stage[:], 0.0).then_inc(S.stage_clear, 1)
        link(pool.memset(ident[:], 0.0))
        pool.affine_select(ident[:], ident[:], [[1, P]], ALU.not_equal, 1.0, base=0,
                           channel_multiplier=-1).then_inc(S.ident_ready, 1)
        pool.memset(smask[:], 1.0)
        pool.memset(ones[:], 1.0)
        pool.memset(maskneg[:], 0.0)
        pool.memset(hmask[:], 1.0)
        link(pool.memset(mask01[:], 1.0))
        for a in (0, 256):
            pool.affine_select(mask01[:, a:a + P], mask01[:, a:a + P], [[1, P]], ALU.is_ge, 0.0, base=0,
                               channel_multiplier=-1)
            pool.affine_select(maskneg[:, a:a + P], maskneg[:, a:a + P], [[-1, P]], ALU.is_ge, LOWEST,
                               base=0, channel_multiplier=1)
        pool.memset(smask[:].rearrange("p (c n) -> p c n", n=CHUNK)[:, :, 0:1], 0.0)
        link(pool.affine_select(hmask[:], hmask[:], [[1, P]], ALU.is_ge, 0.0, base=0, channel_multiplier=-1))
        pool.memset(hmask[0:CHUNK, CHUNK:P], 0.0)
        pool.iota(iota_i[:], [[1, TOPK]], base=0, channel_multiplier=0).then_inc(S.consts, 1)

        pool.wait_ge(S.scores_cp, 8)

        def gather(buf, idx, k, table, sem):
            pool.indirect_dma_start(buf[:], None, table, bass.IndirectOffsetOnAxis(ap=idx[:, k:k + 1], axis=0),
                                    ).then_inc(sem, 16)

        def u_row(s, tb, k, first):
            if not (first and k < RING):
                wait_alone(pool, S.dot_done, s * TOPK + k - RING + 1, S.pool_passed)
            gather(ub[k % RING], uidx[:, tb, :], k, inp["peer_u"][0], u_full[k % RING])

        def v_row(s, tb, k, first):
            if not (first and k < RING):
                wait_alone(pool, S.v_done, s * TOPK + k - RING + 1, S.pool_passed)
            gather(vb[k % RING], vidx[:, tb, :], k, inp["peer_v"][0], v_full[k % RING])

        def step(s, tb, first=False):
            wait_alone(pool, S.uidx_ready, s + 1, S.pool_passed)
            for k in range(TOPK):
                u_row(s, tb, k, first)
                if not first:
                    v_row(s - 1, 1 - tb, k, isinstance(s, int) and s == 1)

        step(0, 0, True)
        step(1, 1)
        with pool.Fori(1, H) as i:
            for tb in range(TB):
                step(i * 2 + tb, tb)
        for k in range(TOPK):
            v_row(2 * H - 1, 1, k, False)

    @block.scalar
    def _(act):
        link = Chain(act, S.act_chain, S.act_passed)

        def root(n, x):
            act.wait_ge(S.square_ready, n + 1)
            act.activation(x, x, ACT.Sqrt).then_inc(S.root_ready, 1)

        root(0, rstd[:])
        act.wait_ge(S.small_in, 80)
        act.copy(wg_h[:], wg_raw[:]).then_inc(S.wg_hi, 1)
        x_hi(act, 0)

        def q_out(dst, scale):
            def f(s):
                slab_ready(act, s)
                act.activation(dst[:, 4 * (s % 2):4 * (s % 2) + 4, :], cm_out(s % 2), ACT.Copy,
                               scale=scale).then_inc(evac[s % 2], 1)
            return f

        def v_out(s):
            slab_ready(act, s)
            act.copy(VX[:, :, 4 * (s % 2):4 * (s % 2) + 4, 0:DH],
                     tm_out(s % 2).rearrange("p b (h d) -> p b h d", d=DH)).then_inc(evac[s % 2], 1)

        def o_out(s):
            slab_ready(act, s)
            act.activation(OG[:, :, W * (s % 2):W * (s % 2) + W], tm_out(s % 2),
                           ACT.Sigmoid).then_inc(evac[s % 2], 1)

        run_slabs(act, split_hi, S_IN, [None] * 6 + [q_out(QT, 1.0)] * 2 + [q_out(KT, SCALE)] * 2
                  + [v_out] * 2 + [o_out] * 2)
        act.wait_ge(S.gate_abs, 1)
        link(act.activation(gln[:], gabs[:], ACT.Exp, scale=-1.0))
        act.activation(gln[:], gln[:], ACT.Ln, bias=1.0).then_inc(S.gate_ln, 1)
        act.wait_ge(S.em_arg, 1)
        act.activation(emcol[:], emcol[:], ACT.Exp).then_inc(S.em_ready, 1)
        for h in range(H + 1):
            if h < H:
                act.wait_ge(S.m_arg, h + 1)
                act.activation(E[:, h % 2, :], E[:, h % 2, :], ACT.Exp).then_inc(S.m_exp, 1)
            if h >= 1:
                act.wait_ge(S.m_num, h)
                act.copy(HN[:, :, h - 1, 0:DH + 1],
                         PS[:, 4 + (h - 1) % 2, 0:TB * (DH + 1)].rearrange("p (b d) -> p b d", b=TB)
                         ).then_inc(S.m_numcp, 1)
        root(1, hr[:])
        root(2, hr[:])
        for n in range(4):
            act.wait_ge(S.m_turn, n + 1)
            act.copy(MIX[:, H + 4 * (n % 2):H + 4 * (n % 2) + 4, (n // 2) * P:(n // 2 + 1) * P],
                     PS[:, 6 + n % 2, :].rearrange("p (h t) -> p h t", t=P)).then_inc(S.mix_y, 1)
        act.wait_ge(S.mix_y, 4)
        act.wait_ge(S.conv_done, 2)
        mix_hi(act, 0)
        run_slabs(act, split_hi, S_OUT, [None] * 4)
        root(3, rstd[:])

        x_hi(act, 1)

        def pq_out(s):
            slab_ready(act, s)
            j = s - S_WQ
            act.copy(PQ[:, 4 * j:4 * j + 4, :], cm_out(s % 2)).then_inc(evac[s % 2], 1)

        act.wait_ge(S.tm_ready, 2)
        run_slabs(act, split_hi, S_WQ, [pq_out] * 4)
        for n in range(8):
            act.wait_ge(S.score_ps, n + 1)
            tb, q = n // 4, n % 4
            act.copy(SC[:, tb, 2 * q:2 * q + 2, :, :],
                     PS[:, 4 + n % 4, :].rearrange("p (h c k) -> p h c k", h=2, c=2)).then_inc(S.scores_cp, 1)

        def soft(n, par):
            act.wait_ge(S.soft_arg, n + 1)
            act.activation(eexp[:], tops[:], ACT.Exp, bias=nmx[:, 0:1], accum_out=esum[:]).then_inc(S.soft_exp, 1)

        def weigh(n, tb, first=False):
            act.wait_ge(S.dots_ready, n + 1)
            act.activation(acts[:, tb, :], dots[:, tb, :], ACT.Gelu).then_inc(S.gelu_ready, 1)
            act.wait_ge(S.ew_ready, n + 1)
            for k in range(TOPK):
                if not first:
                    act.wait_ge(S.v_done, (n - 1) * TOPK + k + 1)
                act.activation(diag[:, k, :], ident[:], ACT.Copy, scale=ew[:, tb, k:k + 1]).then_inc(S.diag_ready, 1)

        soft(0, 0)
        soft(1, 1)
        weigh(0, 0, True)
        soft(2, 0)
        weigh(1, 1)
        with act.Fori(1, H) as i:
            for tb in range(TB):
                soft(i * 2 + tb + 1, 1 - tb)
                weigh(i * 2 + tb, tb)

        root(4, rstd[:])
        root(5, rstd[:])
        act.wait_ge(S.lb_arg, 1)
        act.activation(lb0[:], lb0[:], ACT.Exp).then_inc(S.lb_exp, 1)
        act.activation(lb1[:], lb1[:], ACT.Exp).then_inc(S.lb_exp, 1)
        act.wait_ge(S.wf_in, 16)
        act.copy(wf_h[:], wf_raw[:]).then_inc(S.wf_hi, 1)
        x_hi(act, 2)

        def f_out(s):
            slab_ready(act, s)
            act.wait_ge(S.nrm_used, 1)
            j = s % 2
            act.activation(G_F[:, 4 * j:4 * j + 4, :], cm_out(j), ACT.Sigmoid).then_inc(evac[j], 1)
            if j == 1:
                act.wait_ge(S.f_ready, 1)
                act.activation(G_E[:], G_F[:], ACT.Ln).then_inc(S.lnf_ready, 1)

        def gq_out(s):
            slab_ready(act, s)
            j = s % 2
            act.activation(G_Q[:, 4 * j:4 * j + 4, :], cm_out(j), ACT.Copy, scale=SCALE).then_inc(evac[j], 1)
            if j == 1:
                act.wait_ge(S.b_ready, 1)
                act.activation(G_K[:], G_B[:], ACT.Exp).then_inc(S.expb_ready, 1)
                act.activation(dcay[:], G_B[:].rearrange("p h (c n) -> p h c n", n=CHUNK)[:, :, :, CHUNK - 1],
                               ACT.Exp).then_inc(S.dcay_ready, 1)
                act.wait_ge(S.ke_arg, 1)
                act.activation(G_E[:], G_E[:], ACT.Exp).then_inc(S.expe_ready, 1)
                act.wait_ge(S.q_decayed, 1)
                act.activation(G_K[:], G_B[:], ACT.Exp, scale=-1.0).then_inc(S.expnb_ready, 1)

        def fqk_out(dst, scale):
            def f(s):
                slab_ready(act, s)
                act.wait_ge(S.k_decayed, 1)
                act.activation(dst[:, 4 * (s % 2):4 * (s % 2) + 4, :], cm_out(s % 2), ACT.Copy,
                               scale=scale).then_inc(evac[s % 2], 1)
            return f

        def tm_copy(dst):
            def f(s):
                slab_ready(act, s)
                act.copy(dst[:, :, W * (s % 2):W * (s % 2) + W], tm_out(s % 2)).then_inc(evac[s % 2], 1)
            return f

        def g_out(s):
            slab_ready(act, s)
            act.activation(G_G[:, :, W * (s % 2):W * (s % 2) + W], tm_out(s % 2),
                           ACT.Silu).then_inc(evac[s % 2], 1)

        run_slabs(act, split_hi, S_IN2, [f_out] * 2 + [gq_out] * 2 + [fqk_out(FQ, SCALE)] * 2
                  + [fqk_out(FK, 1.0)] * 2 + [tm_copy(G_V)] * 2 + [g_out] * 2 + [tm_copy(FV)] * 2)
        act.wait_ge(S.gate_abs, 2)
        link(act.activation(gln[:, :, 0:H], gabs[:, :, 0:H], ACT.Exp, scale=-1.0))
        act.activation(gln[:, :, 0:H], gln[:, :, 0:H], ACT.Ln, bias=1.0).then_inc(S.gate_ln, 1)
        for h in range(H + 1):
            if h < H:
                act.wait_ge(S.g_keT, h + 1)
                if h >= 2:
                    act.wait_ge(S.g_ds, h - 1)
                kt = PS[:, 2 + h % 2, 0:T].rearrange("p (b d) -> p b d", b=TB)
                act.copy(KE[0:CHUNK, h % 2, 0:NCH - 1:2, :], kt[0:CHUNK])
                act.copy(KE[CHUNK:P, h % 2, 1, :], kt[CHUNK:P, 0, :]).then_inc(S.g_ke, 1)
            if h >= 1:
                act.wait_ge(S.g_o, h)
                act.copy(HN[:, :, h - 1, 0:DH], PS[:, 6 + (h - 1) % 2, 0:TB * DH].rearrange("p (b d) -> p b d", b=TB)
                         ).then_inc(S.g_ocp, 1)
        root(6, hr[:])
        root(7, hr[:])
        for n in range(4):
            act.wait_ge(S.g_turn, n + 1)
            act.copy(MIX[:, 4 * (n % 2):4 * (n % 2) + 4, (n // 2) * P:(n // 2 + 1) * P],
                     PS[:, 6 + n % 2, :].rearrange("p (h t) -> p h t", t=P)).then_inc(S.mix_y, 1)
        for h in range(H + 1):
            if h < H:
                act.wait_ge(S.a_max, h + 1)
                act.activation(E[:, h % 2, 0:P], E[:, h % 2, 0:P], ACT.Exp, bias=nmax[:, h % 2, 0:1],
                               accum_out=psum_[:, h % 2, 0:1])
                act.activation(E[:, h % 2, P:384], E[:, h % 2, P:384], ACT.Exp, bias=nmax[:, h % 2, 1:2],
                               accum_out=psum_[:, h % 2, 1:2]).then_inc(S.a_exp, 1)
            if h >= 1:
                act.wait_ge(S.a_pT, h)
                act.copy(PM[:, (h - 1) % 2, :], PS[:, 2 + (h - 1) % 2, 0:384]).then_inc(S.a_pTcp, 1)
        act.wait_ge(S.mix_a, H)
        act.wait_ge(S.mix_y, 8)
        mix_hi(act, 1)
        run_slabs(act, split_hi, S_OUT2, [None] * 4)
        root(8, rstd[:])

        x_hi(act, 3)

        def gate_conv(n, s):
            slab_ready(act, s)
            if not (isinstance(n, int) and n == 0):
                act.wait_ge(S.ff_up, n)
            for t in range(4):
                w2 = cols[:, 2, ds(n * 4 + t, 1)] if not isinstance(n, int) else cols[:, 2, 4 * n + t:4 * n + t + 1]
                b = cols[:, 2, ds(n * 4 + t + FC, 1)] if not isinstance(n, int) else cols[:, 2, FC + 4 * n + t:FC + 4 * n + t + 1]
                a = act.activation(FY[:, t, :], cm_out(0)[:, t, :], ACT.Identity, bias=b, scale=w2)
            a.then_inc(S.ff_y, 1)

        def gate_silu(n):
            act.wait_ge(S.ff_conv, n + 1)
            act.activation(FY[:], FY[:], ACT.Silu).then_inc(S.ff_silu, 1)

        def ff_pair(n, s):
            for u in range(UNITS):
                split_hi(act, s, u)
            split_hi(act, s + 1, 0)
            split_hi(act, s + 1, 1)
            gate_conv(n, s)
            split_hi(act, s + 1, 2)
            gate_silu(n)
            split_hi(act, s + 1, 3)

        ff_pair(0, S_FF)
        with act.Fori(1, FPAIRS) as i:
            ff_pair(i, i * 2 + S_FF)
        act.wait_ge(S.ff_up, FPAIRS)

        def down_hi(j, s):
            for u in range(UNITS):
                split_hi(act, s, u)
                act.copy(ah[u % 2][:], FA[:, ds(j * UNITS + u, 1), :].rearrange("p o n -> p (o n)")
                         if not isinstance(j, int) else FA[:, j * UNITS + u, :]).then_inc(S.ah_full, 1)

        down_hi(0, S_DOWN)
        with act.Fori(1, NDOWN) as i:
            down_hi(i, i + S_DOWN)
        root(9, rstd[:])

    @block.vector
    def _(dve):
        link = Chain(dve, S.dve_chain, S.dve_passed)

        def inverse_root(n, x, src, eps):
            dve.tensor_scalar(x, src, eps, None, ALU.add).then_inc(S.square_ready, 1)
            dve.wait_ge(S.root_ready, n + 1)
            link(dve.reciprocal(x, x))

        def moments():
            for tb in range(TB):
                if tb:
                    link(dve.engine_nop())
                for q in range(4):
                    b = dve.bn_stats(stats[:, q, :], RES[:, tb, q * W:(q + 1) * W])
                link(b)
                link(dve.bn_aggr(mv[:, tb, :], stats[:]))

        def layer_norm(n, norms_in):
            moments()
            inverse_root(n, rstd[:], mv[:, :, 1], LN_EPS)
            dve.wait_ge(S.norm_in, norms_in)
            for tb in range(TB):
                link(dve.scalar_tensor_tensor(RES[:, tb, :], RES[:, tb, :], mv[:, tb, 0:1], GAIN[:],
                                              ALU.subtract, ALU.mult))
                link(dve.scalar_tensor_tensor(RES[:, tb, :], RES[:, tb, :], rstd[:, tb:tb + 1], BIAS[:],
                                              ALU.mult, ALU.add))

        def rms_norm(n, dst, norms_in, ready):
            moments()
            link(dve.tensor_tensor(msq[:], mv[:, :, 0], mv[:, :, 0], ALU.mult))
            link(dve.tensor_tensor(msq[:], msq[:], mv[:, :, 1], ALU.add))
            inverse_root(n, rstd[:], msq[:], RMS_EPS)
            dve.wait_ge(S.norm_in, norms_in)
            for tb in range(TB):
                dve.scalar_tensor_tensor(dst[:, tb, :], RES[:, tb, :], rstd[:, tb:tb + 1], GAIN[:],
                                         ALU.mult, ALU.mult).then_inc(ready, 1)

        dve.wait_ge(S.x_in, 32)
        layer_norm(0, 32)
        dve.engine_nop().then_inc(S.tm_ready, 1)
        dve.wait_ge(S.consts, 1)
        dve.tensor_copy(iota_f[:], iota_i[:])
        dve.wait_ge(S.cols_ps, 1)
        link(dve.tensor_copy(cols[:], PS[:, 0, 0:384].rearrange("p (a n) -> p a n", n=P)), S.cols_ready)
        dve.wait_ge(S.wg_hi, 1)
        dve.tensor_tensor(wg_l[:], wg_raw[:], wg_h[:].bitcast(F32), ALU.subtract).then_inc(S.wg_lo, 1)
        dve.memset(ZC[:, :, 0:2], 0.0)
        link(dve.memset(VX[:, :, :, DH:DH + 1], 1.0))
        x_lo(dve, 0)

        def c_out(s):
            slab_ready(dve, s)
            link(dve.tensor_copy(ZC[:, 4 * (s % 2):4 * (s % 2) + 4, 2:], cm_out(s % 2)), evac[s % 2])

        def h_out(s):
            slab_ready(dve, s)
            j = s % 2
            z = ZC[:, 4 * j:4 * j + 4, :]
            link(dve.tensor_tensor(z[:, :, 2:], z[:, :, 2:], cm_out(j), ALU.mult), evac[j])
            for t in range(4 * j, 4 * j + 4):
                dve.tensor_scalar(MIX[:, t, :], ZC[:, t, 2:], cols[:, 0, 16 + t:17 + t], cols[:, 0, 24 + t:25 + t],
                                  ALU.mult, ALU.add)
            for tap in (1, 0):
                link(dve.engine_nop())
                for t in range(4 * j, 4 * j + 4):
                    dve.scalar_tensor_tensor(MIX[:, t, :], ZC[:, t, tap:tap + T],
                                             cols[:, 0, 8 * tap + t:8 * tap + t + 1], MIX[:, t, :],
                                             ALU.mult, ALU.add)
            link(dve.engine_nop())

        def b_out(s):
            slab_ready(dve, s)
            j = s % 2
            m = MIX[:, 4 * j:4 * j + 4, :]
            link(dve.tensor_tensor(m, m, cm_out(j), ALU.mult), evac[j], S.conv_done)

        run_slabs(dve, split_lo, S_IN, [c_out] * 2 + [h_out] * 2 + [b_out] * 2 + [None] * 8)
        dve.wait_ge(S.gate_ps, 1)
        link(dve.tensor_tensor(glog[:], PS[:, 6, 0:32].rearrange("p (b n) -> p b n", b=TB),
                               bcast(bgate[:].unsqueeze(1), [TB, 16]), ALU.add))
        dve.scalar_tensor_tensor(gabs[:], glog[:], -1.0, glog[:], ALU.mult, ALU.max).then_inc(S.gate_abs, 1)
        dve.memset(GP[:], 0.0)
        dve.memset(BP[:], 0.0)
        link(dve.memset(RA[:], 0.0))
        dve.wait_ge(S.gate_ln, 1)
        dve.tensor_copy(GP[:, :, 0:H], glog[:, :, 0:H])
        dve.scalar_tensor_tensor(GP[:, :, 32:32 + H], glog[:, :, H:16], 0.0, gln[:, :, H:16], ALU.min,
                                 ALU.subtract).then_inc(S.gates_tm, 1)
        dve.wait_ge(S.gates_T, 1)
        dve.tensor_copy(LI[0:H, :], PS[0:H, 7, 0:T])
        link(dve.tensor_copy(LF[0:H, :], PS[32:32 + H, 7, 0:T]))
        link(dve.tensor_tensor_scan(FS[0:H, :], ones[0:H, :], LF[0:H, :], 0.0, ALU.mult, ALU.add))
        link(dve.tensor_tensor(BP[0:H, :], LI[0:H, :], FS[0:H, :], ALU.subtract))
        link(dve.tensor_tensor_scan(CM[0:H, :], BP[0:H, :], BP[0:H, :], 0.0, ALU.max, ALU.max))
        link(dve.tensor_scalar(RA[0:H, :], CM[0:H, :], -1.0, None, ALU.mult))
        link(dve.tensor_tensor(LF[0:H, :], RA[0:H, :], FS[0:H, :], ALU.subtract))
        dve.tensor_copy(BP[32:32 + H, :], LF[0:H, :]).then_inc(S.gates_cm, 1)
        dve.wait_ge(S.gates_back, 1)
        bt = PS[:, 6, 0:T].rearrange("p (b n) -> p b n", b=TB)
        link(dve.tensor_copy(bcol[:], bt[:, :, 0:H]))
        dve.tensor_copy(emcol[:], bt[:, :, 32:32 + H]).then_inc(S.em_arg, 1)
        for h in range(H + 1):
            if h < H:
                e = h % 2
                dve.wait_ge(S.m_scores, h + 1)
                dve.tensor_scalar(E[:, e, 0:T], PS[:, 2 + e, 0:T], bcol[:, 0, h:h + 1], 0.0, ALU.add, ALU.min)
                dve.tensor_scalar(E[:, e, T:384], PS[:, 2 + e, P:T], bcol[:, 1, h:h + 1], 0.0, ALU.add,
                                  ALU.min).then_inc(S.m_arg, 1)
            if h >= 1:
                e = (h - 1) % 2
                dve.wait_ge(S.m_exp, h)
                link(dve.tensor_tensor(E[:, e, :], E[:, e, :], mask01[:], ALU.mult))
                if h >= 3:
                    dve.wait_ge(S.m_num, h - 2)
                dve.tensor_tensor(PM[:, e, :], E[:, e, :], PS[:, e, 0:384], ALU.mult).then_inc(S.m_prob, 1)
        dve.wait_ge(S.m_numcp, H)
        dve.wait_ge(S.em_ready, 1)
        link(dve.scalar_tensor_tensor(den[:], HN[:, :, :, DH], -1.0, HN[:, :, :, DH], ALU.mult, ALU.max))
        link(dve.tensor_tensor(den[:], den[:], emcol[:], ALU.max))
        link(dve.reciprocal(den[:], den[:]))
        for tb in range(TB):
            hh = HN[:, tb, :, 0:DH]
            og = OG[:, tb, :].rearrange("p (h d) -> p h d", d=DH)
            link(dve.tensor_tensor(hh, hh, bcast(den[:, tb, :].unsqueeze(2), [H, DH]), ALU.mult))
            for h in range(H):
                b = dve.bn_stats(hstat[:, h, :], HN[:, tb, h, 0:DH])
            link(b)
            for h in range(H):
                b = dve.bn_aggr(hmv[:, h, :], hstat[:, h, :])
            link(b)
            inverse_root(1 + tb, hr[:], hmv[:, :, 1], LN_EPS)
            link(dve.tensor_tensor(hh, hh, bcast(hmv[:, :, 0:1], [H, DH]), ALU.subtract))
            link(dve.tensor_tensor(hh, hh, bcast(hr[:].unsqueeze(2), [H, DH]), ALU.mult))
            link(dve.tensor_tensor(og, og, mhg[:].rearrange("p (h d) -> p h d", d=DH), ALU.mult))
            link(dve.tensor_tensor(hh, hh, og, ALU.mult), S.m_y)
        mix_lo(dve, 0)

        def res_add(scale):
            def f(s):
                slab_ready(dve, s)
                j = (s - (S_OUT if s < S_OUT2 else S_OUT2)) * W
                r = RES[:, :, j:j + W]
                link(dve.scalar_tensor_tensor(r, r, scale, tm_out(s % 2), ALU.mult, ALU.add), evac[s % 2])
            return f

        run_slabs(dve, split_lo, S_OUT, [res_add(ALPHA)] * 4)
        layer_norm(3, 64)
        dve.engine_nop().then_inc(S.tm_ready, 1)
        for n in range(4):
            dve.wait_ge(S.keyT_ps, n + 1)
            dve.tensor_copy(KX[:, 4 * n:4 * n + 4, :],
                            PS[:, n, :].rearrange("p (a k) -> p a k", k=P)).then_inc(S.keyT, 1)
        x_lo(dve, 1)
        run_slabs(dve, split_lo, S_WQ, [None] * 4)

        dve.wait_ge(S.scores_cp, 8)
        link(dve.memset(SC[:, :, H, :, :], 0.0))

        def top16(vals, spare, dst, idx):
            link(dve.max(dst[:, 0:8], vals))
            dve.max_index(idx[:, 0:8], dst[:, 0:8], vals)
            link(dve.match_replace(spare, dst[:, 0:8], vals, LOWEST))
            link(dve.max(dst[:, 8:16], spare))
            link(dve.max_index(idx[:, 8:16], dst[:, 8:16], spare))

        def route(n, tb, h):
            src = SC[:, tb, ds(h, 1), :, :].rearrange("p o a k -> p (o a) k") if not isinstance(h, int) else SC[:, tb, h, :, :]
            link(dve.tensor_copy(sc[:], src))
            for a in range(2):
                top16(sc[:, a, :], sc2[:, a, :], best[:, a, :], bidx[:, a, :])
            link(dve.tensor_copy(bidf[:], bidx[:]))
            link(dve.tensor_tensor(cand[:], bcast(best[:, 0, :].unsqueeze(2), [TOPK, TOPK]),
                                   bcast(best[:, 1, :].unsqueeze(1), [TOPK, TOPK]), ALU.add))
            if not (isinstance(n, int) and n == 0):
                wait_alone(dve, S.soft_exp, n, S.dve_passed)
            c1, c2 = cand[:].rearrange("p a b -> p (a b)"), cand2[:].rearrange("p a b -> p (a b)")
            top16(c1, c2, tops[:], topj[:])
            dve.tensor_scalar(nmx[:], tops[:, 0:1], -1.0, None, ALU.mult).then_inc(S.soft_arg, 1)
            dve.tensor_scalar(tij[:, 0, :], topj[:], 4, None, ALU.logical_shift_right)
            link(dve.tensor_scalar(tij[:, 1, :], topj[:], 15, None, ALU.bitwise_and))
            link(dve.tensor_copy(tijf[:], tij[:]))
            for a in range(2):
                link(dve.tensor_tensor(hot[:, a, :, :], bcast(iota_f[:].unsqueeze(1), [TOPK, TOPK]),
                                       bcast(tijf[:, a, :].unsqueeze(2), [TOPK, TOPK]), ALU.is_equal))
                link(dve.tensor_tensor(hot[:, a, :, :], hot[:, a, :, :],
                                       bcast(bidf[:, a, :].unsqueeze(1), [TOPK, TOPK]), ALU.mult))
            link(dve.tensor_reduce(eids[:], hot[:], AX, ALU.add))
            link(dve.scalar_tensor_tensor(eidf[:], eids[:, 0, :], float(NKEY), eids[:, 1, :], ALU.mult, ALU.add))
            dve.tensor_copy(uidx[:, tb, :], eidf[:]).then_inc(S.uidx_ready, 1)
            dve.wait_ge(S.soft_exp, n + 1)
            link(dve.reciprocal(rsum[:], esum[:]))
            link(dve.tensor_scalar(gate[:, tb, :], eexp[:], rsum[:, 0:1], None, ALU.mult))

        def dot_rows(n, tb):
            dve.tensor_copy(vidx[:, tb, :], uidx[:, tb, :])
            for k in range(TOPK):
                dve.wait_ge(u_full[k % RING], (n * (TOPK // RING) + k // RING + 1) * 16)
                dve.tensor_tensor_reduce(ub[k % RING][:], ub[k % RING][:], RES[:, tb, :], 1.0, 0.0, ALU.mult,
                                         ALU.add, dots[:, tb, k:k + 1]).then_inc(S.dot_done, 1)
            dve.wait_ge(S.dot_done, (n + 1) * TOPK).then_inc(S.dots_ready, 1)

        def weights(n, tb):
            dve.wait_ge(S.gelu_ready, n + 1)
            dve.tensor_tensor(ew[:, tb, :], acts[:, tb, :], gate[:, tb, :], ALU.mult).then_inc(S.ew_ready, 1)

        def expert_step(n, tb, h_next):
            route(n + 1, 1 - tb, h_next)
            dot_rows(n, tb)
            weights(n, tb)

        route(0, 0, 0)
        expert_step(0, 0, 0)
        expert_step(1, 1, 1)
        with dve.Fori(1, H) as i:
            link.enter(i, 1, 50)
            for tb in range(TB):
                expert_step(i * 2 + tb, tb, i + tb)
        link.leave(1, H - 1)
        dve.wait_ge(S.v_done, 2 * H * TOPK)
        dve.wait_ge(S.acc_done, 1)
        for tb in range(TB):
            for b in range(4):
                r = RES[:, tb, b * W:(b + 1) * W]
                dve.scalar_tensor_tensor(r, r, ALPHA, PS[:, 4 * tb + b, :], ALU.mult, ALU.add).then_inc(S.ffsum, 1)
        dve.wait_ge(S.ffsum, 8)
        layer_norm(4, 96)
        dve.engine_nop().then_inc(S.ln2_done, 1)
        rms_norm(5, NRM, 112, S.nrm)
        dve.wait_ge(S.nrm, 2)
        dve.engine_nop().then_inc(S.tm_ready, 1)

        link(dve.tensor_tensor(lbm[:], cols[:, 0, 32:40], cols[:, 0, 40:48], ALU.max))
        dve.tensor_tensor(lb0[:], cols[:, 0, 32:40], lbm[:], ALU.subtract)
        link(dve.tensor_tensor(lb1[:], cols[:, 0, 40:48], lbm[:], ALU.subtract), S.lb_arg)
        dve.wait_ge(S.lb_exp, 2)
        link(dve.tensor_tensor(lbs[:], lb0[:], lb1[:], ALU.add))
        link(dve.reciprocal(lbs[:], lbs[:]))
        link(dve.tensor_tensor(lb[:], lb0[:], lbs[:], ALU.mult))
        link(dve.tensor_scalar(omlb[:], lb[:], -1.0, 1.0, ALU.mult, ALU.add))
        dve.wait_ge(S.wf_hi, 1)
        dve.tensor_tensor(wf_l[:], wf_raw[:], wf_h[:].bitcast(F32), ALU.subtract).then_inc(S.wf_lo, 1)
        x_lo(dve, 2)
        dve.wait_ge(S.xt_lo, 24)
        dve.engine_nop().then_inc(S.nrm_used, 1)

        def f_fix(s):
            dve.wait_ge(evac[1], s // 2 + 1)
            dve.wait_ge(evac[0], s // 2 + 1)
            for h in range(H):
                a = dve.tensor_scalar(G_F[:, h, :], G_F[:, h, :], omlb[:, h:h + 1], lb[:, h:h + 1], ALU.mult, ALU.add)
            link(a, S.f_ready)
            dve.wait_ge(S.lnf_ready, 1)
            for h in range(H):
                a = dve.tensor_tensor_scan(G_B[:, h, :], smask[:], G_E[:, h, :], 0.0, ALU.mult, ALU.add)
            link(a, S.b_ready)

        def k_fix(s):
            dve.wait_ge(evac[1], s // 2 + 1)
            dve.wait_ge(evac[0], s // 2 + 1)
            bc = G_B[:].rearrange("p h (c n) -> p (h c) n", n=CHUNK)
            ec = G_E[:].rearrange("p h (c n) -> p (h c) n", n=CHUNK)
            last = bc[:, :, CHUNK - 1:CHUNK]
            link(dve.tensor_tensor(ec, bcast(last, [H * NCH, CHUNK]), bc, ALU.subtract), S.ke_arg)
            link(dve.tensor_scalar(G_F[:], G_F[:], -1.0, 1.0, ALU.mult, ALU.add))
            dve.wait_ge(S.expb_ready, 1)
            link(dve.tensor_tensor(G_Q[:], G_Q[:], G_K[:], ALU.mult), S.q_decayed)
            dve.wait_ge(S.expe_ready, 1)
            link(dve.tensor_tensor(G_E[:], G_E[:], G_F[:], ALU.mult))
            dve.wait_ge(S.expnb_ready, 1)
            link(dve.tensor_tensor(G_K[:], G_K[:], G_F[:], ALU.mult), S.k_decayed)

        run_slabs(dve, split_lo, S_IN2, [None, f_fix, None, k_fix] + [None] * 10)
        dve.wait_ge(S.gate_ps, 2)
        link(dve.tensor_tensor(glog[:, :, 0:H], PS[:, 6, 0:16].rearrange("p (b n) -> p b n", b=TB),
                               bcast(fbias[:].unsqueeze(1), [TB, H]), ALU.add))
        dve.scalar_tensor_tensor(gabs[:, :, 0:H], glog[:, :, 0:H], -1.0, glog[:, :, 0:H], ALU.mult, ALU.max).then_inc(S.gate_abs, 1)
        dve.memset(GP[:], 0.0)
        dve.memset(BP[:], 0.0)
        dve.memset(RA[:], 0.0)
        dve.memset(KE[:], 0.0)
        link(dve.memset(AT[:], 0.0))
        dve.wait_ge(S.gate_ln, 2)
        dve.scalar_tensor_tensor(GP[:, :, 0:H], glog[:, :, 0:H], 0.0, gln[:, :, 0:H], ALU.min,
                                 ALU.subtract).then_inc(S.gates_tm, 1)
        dve.wait_ge(S.gates_T, 2)
        link(dve.tensor_copy(LF[0:H, :], PS[0:H, 7, 0:T]))
        link(dve.tensor_tensor_scan(BP[0:H, :], ones[0:H, :], LF[0:H, :], 0.0, ALU.mult, ALU.add))
        dve.tensor_scalar(RA[0:H, :], BP[0:H, :], -1.0, None, ALU.mult).then_inc(S.gates_cm, 1)
        dve.wait_ge(S.gates_back, 2)
        link(dve.tensor_copy(bcol[:], bt[:, :, 0:H]), S.c_ready)

        for h in range(H):
            e = h % 2
            dve.wait_ge(S.g_keT, h + 1)
            if h >= 2:
                dve.wait_ge(S.g_o, h - 1)
            for tb in range(TB):
                dve.copy_predicated(AT[:, e, tb, :], hmask[:].bitcast(I32), PS[:, 4 + e, tb * P:tb * P + P])
            dve.engine_nop().then_inc(S.g_attn, 1)
            dve.wait_ge(S.g_ds, h + 1)
            dve.wait_ge(S.dcay_ready, 1)
            link(dve.tensor_copy(ST[:, e, 0, :], PS[:, e, 0:P]))
            for c in (1, 2):
                link(dve.scalar_tensor_tensor(ST[:, e, c, :], ST[:, e, c - 1, :], dcay[:, h, c:c + 1],
                                              PS[:, e, c * P:c * P + P], ALU.mult, ALU.add))
            dve.engine_nop().then_inc(S.g_state, 1)
        dve.wait_ge(S.g_ocp, H)
        for tb in range(TB):
            hh = HN[:, tb, :, 0:DH]
            gg = G_G[:, tb, :].rearrange("p (h d) -> p h d", d=DH)
            for h in range(H):
                b = dve.bn_stats(hstat[:, h, :], HN[:, tb, h, 0:DH])
            link(b)
            for h in range(H):
                b = dve.bn_aggr(hmv[:, h, :], hstat[:, h, :])
            link(b)
            link(dve.tensor_tensor(hr[:], hmv[:, :, 0], hmv[:, :, 0], ALU.mult))
            link(dve.tensor_tensor(hr[:], hr[:], hmv[:, :, 1], ALU.add))
            inverse_root(6 + tb, hr[:], hr[:], RMS_EPS)
            link(dve.tensor_tensor(hh, hh, bcast(hr[:].unsqueeze(2), [H, DH]), ALU.mult))
            link(dve.tensor_tensor(hh, hh, bcast(hgain[:].unsqueeze(1), [H, DH]), ALU.mult))
            link(dve.tensor_tensor(hh, hh, gg, ALU.mult), S.g_y)
        dve.wait_ge(S.g_turn, 4)

        def soft_arg(h):
            e = h % 2
            dve.wait_ge(S.a_scores, h + 1)
            if h >= 2:
                dve.wait_ge(S.a_pT, h - 1)
            dve.scalar_tensor_tensor(E[:, e, 0:P], PS[:, e, 0:P], bcol[:, 0, h:h + 1], maskneg[:, 0:P],
                                     ALU.add, ALU.add)
            dve.scalar_tensor_tensor(E[:, e, P:2 * P], PS[:, e, P:2 * P], bcol[:, 1, h:h + 1], maskneg[:, P:2 * P],
                                     ALU.add, ALU.add)
            link(dve.scalar_tensor_tensor(E[:, e, 2 * P:384], PS[:, e, 2 * P:384], bcol[:, 1, h:h + 1],
                                          maskneg[:, 2 * P:384], ALU.add, ALU.add))
            dve.tensor_reduce(nmax[:, e, 0:1], E[:, e, 0:P], AX, ALU.max, negate=True)
            link(dve.tensor_reduce(nmax[:, e, 1:2], E[:, e, P:384], AX, ALU.max, negate=True), S.a_max)

        def soft_norm(h):
            e = h % 2
            dve.wait_ge(S.a_exp, h + 1)
            link(dve.reciprocal(psum_[:, e, :], psum_[:, e, :]))
            dve.tensor_scalar(E[:, e, 0:P], E[:, e, 0:P], psum_[:, e, 0:1], None, ALU.mult)
            link(dve.tensor_scalar(E[:, e, P:384], E[:, e, P:384], psum_[:, e, 1:2], None, ALU.mult), S.a_prob)

        def attn_out(h):
            dve.wait_ge(S.a_out, h + 1)
            dve.tensor_copy(MIX[:, H + h, :], PS[:, 4 + h % 2, 0:T]).then_inc(S.mix_a, 1)

        for h in range(H + 2):
            if h < H:
                soft_arg(h)
            if 1 <= h <= H:
                soft_norm(h - 1)
            if h >= 2:
                attn_out(h - 2)
        mix_lo(dve, 1)
        run_slabs(dve, split_lo, S_OUT2, [res_add(1.0)] * 4)
        rms_norm(8, NRM, 128, S.nrm)
        dve.wait_ge(S.nrm, 4)
        dve.engine_nop().then_inc(S.tm_ready, 1)
        x_lo(dve, 3)

        def col(a, n, t):
            return cols[:, a[0], ds(n * 4 + (t + a[1]), 1)] if not isinstance(n, int) else \
                cols[:, a[0], 4 * n + t + a[1]:4 * n + t + a[1] + 1]

        def gate_taps(n):
            dve.wait_ge(S.ff_y, n + 1)
            for back, place in ((1, (1, FC)), (2, (1, 0))):
                for t in range(4):
                    a = dve.scalar_tensor_tensor(FY[:, t, back:], cm_out(0)[:, t, 0:T - back], col(place, n, t),
                                                 FY[:, t, back:], ALU.mult, ALU.add)
                link(a)
            dve.engine_nop().then_inc(S.ff_conv, 1)
            dve.engine_nop().then_inc(evac[0], 1)

        def up_out(n, s):
            slab_ready(dve, s)
            dve.wait_ge(S.ff_silu, n + 1)
            dst = FA[:, ds(n * 4, 4), :] if not isinstance(n, int) else FA[:, 4 * n:4 * n + 4, :]
            link(dve.tensor_tensor(dst, FY[:], cm_out(1), ALU.mult), evac[1], S.ff_up)

        def ff_pair(n, s, first=False):
            split_lo(dve, s, 0)
            split_lo(dve, s, 1)
            if not first:
                up_out(n - 1, s - 1)
            split_lo(dve, s, 2)
            split_lo(dve, s, 3)
            split_lo(dve, s + 1, 0)
            split_lo(dve, s + 1, 1)
            gate_taps(n)
            split_lo(dve, s + 1, 2)
            split_lo(dve, s + 1, 3)

        ff_pair(0, S_FF, True)
        with dve.Fori(1, FPAIRS) as i:
            link.enter(i, 1, 3)
            ff_pair(i, i * 2 + S_FF)
        link.leave(1, FPAIRS - 1)
        up_out(FPAIRS - 1, S_FF + 2 * FPAIRS - 1)

        def down_lo(j, s):
            for u in range(UNITS):
                split_lo(dve, s, u)
                dve.wait_ge(S.ah_full, j * UNITS + u + 1)
                dve.tensor_tensor(al[u % 2][:], FA[:, ds(j * UNITS + u, 1), :].rearrange("p o n -> p (o n)")
                                  if not isinstance(j, int) else FA[:, j * UNITS + u, :],
                                  ah[u % 2][:].bitcast(F32), ALU.subtract).then_inc(S.al_full, 1)

        down_lo(0, S_DOWN)
        with dve.Fori(1, NDOWN) as i:
            down_lo(i, i + S_DOWN)
        slab_ready(dve, S_DOWN + NDOWN - 1)
        dve.wait_ge(S.down_done, 1)
        for tb in range(TB):
            for b in range(4):
                r = RES[:, tb, b * W:(b + 1) * W]
                a = dve.tensor_tensor(r, r, PS[:, 4 * tb + b, :], ALU.add)
            link(a)
        rms_norm(9, RES, 144, S.final)

    @block.tensor
    def _(pe):
        pe.wait_ge(S.ident_ready, 1)
        pe.wait_ge(S.stage_in, 7 * 16)
        for a in range(3):
            m = pe.transpose(PS[:, 0, a * P:a * P + P], stage[:, a, :], ident[:])
        m.then_inc(S.cols_ps, 1)
        turn_x(pe, 0, RES)
        pe.wait_ge(S.xt_lo, 8)
        pe.wait_ge(S.cols_ready, 1)
        for s in range(10):
            pe_slab(pe, s // 2, s % 2, True)
        for s in range(10, 14):
            pe_slab(pe, s // 2, s % 2, False)

        def gates(n, width, h, l, ready):
            pe.wait_ge(ready, 1)
            for tb in range(TB):
                y = slice(tb * P, tb * P + P)
                o = PS[:, 6, tb * width:(tb + 1) * width]
                for d in range(DC):
                    pe.matmul(o, XH[:, d, y], h[:, d, :], start=d == 0, stop=False)
                    pe.matmul(o, XH[:, d, y], l[:, d, :], start=False, stop=False)
                    m = pe.matmul(o, XL[:, d, y], h[:, d, :], start=False, stop=d == DC - 1)
            m.then_inc(S.gate_ps, 1)
            pe.wait_ge(S.gates_tm, n + 1)
            for tb in range(TB):
                m = pe.transpose(PS[:, 7, tb * P:tb * P + P], GP[:, tb, :], ident[:])
            m.then_inc(S.gates_T, 1)
            pe.wait_ge(S.gates_cm, n + 1)
            for tb in range(TB):
                m = pe.transpose(PS[:, 6, tb * P:tb * P + P], BP[:, tb * P:tb * P + P], ident[:])
            m.then_inc(S.gates_back, 1)

        gates(0, 16, wg_h, wg_l, S.wg_lo)
        pe.wait_ge(evac[0], 7)
        pe.wait_ge(evac[1], 7)
        for h in range(H + 1):
            if h < H:
                e = h % 2
                if h >= 2:
                    pe.wait_ge(S.m_prob, h - 1)
                pe.matmul(PS[:, e, 0:T], KT[:, h, 0:P], QT[:, h, :], start=True, stop=True)
                pe.matmul(PS[:, e, T:384], KT[:, h, P:T], QT[:, h, P:T], start=True, stop=True)
                pe.matmul(PS[:, 2 + e, 0:T], bcast(ident[:, h:h + 1], [P]), RA[:], start=True,
                          stop=True).then_inc(S.m_scores, 1)
            if h >= 1:
                g = h - 1
                e = g % 2
                pe.wait_ge(S.m_prob, h)
                if g >= 2:
                    pe.wait_ge(S.m_numcp, g - 1)
                o = PS[:, 4 + e, 0:TB * (DH + 1)].rearrange("p (b d) -> p b d", b=TB)
                pe.matmul(o[:, 0, :], PM[:, e, 0:P], VX[:, 0, g, 0:DH + 1], start=True, stop=True)
                pe.matmul(o[:, 1, :], PM[:, e, P:T], VX[:, 0, g, 0:DH + 1], start=True, stop=False)
                pe.matmul(o[:, 1, :], PM[:, e, T:384], VX[:, 1, g, 0:DH + 1], start=False,
                          stop=True).then_inc(S.m_num, 1)

        def turn_heads(y, turned, copied, n0):
            for n in range(4):
                tb, half = n // 2, n % 2
                pe.wait_ge(y, tb + 1)
                if n >= 2:
                    pe.wait_ge(copied, n0 + n - 1)
                for k in range(4):
                    m = pe.transpose(PS[:, 6 + half, k * P:k * P + P], HN[:, tb, 4 * half + k, 0:DH], ident[:])
                m.then_inc(turned, 1)

        turn_heads(S.m_y, S.m_turn, S.mix_y, 0)
        pe.wait_ge(S.mix_lo, 4)
        for s in range(S_OUT, S_OUT + 4):
            pe_slab(pe, s // 2, s % 2, False)

        pe.wait_ge(S.keys_in, 16 * 2 * H)
        pe.wait_ge(evac[0], (S_OUT + 4) // 2)
        pe.wait_ge(evac[1], (S_OUT + 4) // 2)
        for n in range(4):
            for k in range(4):
                m = pe.transpose(PS[:, n, k * P:k * P + P], KR[:, 4 * n + k, :], ident[:])
            m.then_inc(S.keyT_ps, 1)
        turn_x(pe, 1, RES)
        pe.wait_ge(S.keyT, 4)
        pe.wait_ge(S.xt_lo, 16)
        for s in range(S_WQ, S_WQ + 4):
            pe_slab(pe, s // 2, s % 2, True)
        pe.wait_ge(evac[0], (S_WQ + 4) // 2)
        pe.wait_ge(evac[1], (S_WQ + 4) // 2)
        for n in range(8):
            if n >= 4:
                pe.wait_ge(S.scores_cp, n - 3)
            tb, q = n // 4, n % 4
            for k in range(4):
                m = pe.matmul(PS[:, 4 + n % 4, k * P:k * P + P], PQ[:, 4 * q + k, tb * P:tb * P + P],
                              KX[:, 4 * q + k, :], start=True, stop=True)
            m.then_inc(S.score_ps, 1)
        pe.wait_ge(S.scores_cp, 8)

        def v_rows(n, tb, start=False):
            for k in range(TOPK):
                pe.wait_ge(v_full[k % RING], (n * (TOPK // RING) + k // RING + 1) * 16)
                pe.wait_ge(S.diag_ready, n * TOPK + k + 1)
                for b in range(4):
                    m = pe.matmul(PS[:, 4 * tb + b, :], diag[:, k, :], vb[k % RING][:, b * W:(b + 1) * W],
                                  start=start and k == 0, stop=False, skip_group_check=True)
                m.then_inc(S.v_done, 1)

        v_rows(0, 0, True)
        v_rows(1, 1, True)
        with pe.Fori(1, H) as i:
            for tb in range(TB):
                v_rows(i * 2 + tb, tb)
        pe.wait_ge(S.v_done, 2 * H * TOPK)
        pe.nop().then_inc(S.acc_done, 1)

        pe.wait_ge(S.ffsum, 8)
        turn_x(pe, 2, NRM)
        pe.wait_ge(S.xt_lo, 24)
        for s in range(S_IN2, S_IN2 + 8):
            pe_slab(pe, s // 2, s % 2, True)
        for s in range(S_IN2 + 8, S_IN2 + 14):
            pe_slab(pe, s // 2, s % 2, False)
        gates(1, H, wf_h, wf_l, S.wf_lo)
        pe.wait_ge(evac[0], S_OUT2 // 2)
        pe.wait_ge(evac[1], S_OUT2 // 2)
        pe.wait_ge(S.c_ready, 1)
        for h in range(H + 1):
            if h < H:
                e = h % 2
                if h >= 2:
                    pe.wait_ge(S.g_attn, h - 1)
                    pe.wait_ge(S.g_ke, h - 1)
                for tb in range(TB):
                    y = slice(tb * P, tb * P + P)
                    pe.matmul(PS[:, 4 + e, tb * P:tb * P + P], G_K[:, h, y], G_Q[:, h, y], start=True, stop=True)
                for tb in range(TB):
                    y = slice(tb * P, tb * P + P)
                    m = pe.transpose(PS[:, 2 + e, y], G_E[:, h, y], ident[:])
                m.then_inc(S.g_keT, 1)
                pe.wait_ge(S.g_ke, h + 1)
                if h >= 2:
                    pe.wait_ge(S.g_state, h - 1)
                for c in range(NCH - 1):
                    m = pe.matmul(PS[:, e, c * P:c * P + P], KE[:, e, c, :],
                                  G_V[:, c // 2, h * DH:(h + 1) * DH], start=True, stop=True)
                m.then_inc(S.g_ds, 1)
            if h >= 1:
                g = h - 1
                e = g % 2
                pe.wait_ge(S.g_attn, h)
                pe.wait_ge(S.g_state, h)
                if g >= 2:
                    pe.wait_ge(S.g_ocp, g - 1)
                for tb in range(TB):
                    o = PS[:, 6 + e, tb * P:tb * P + P]
                    pe.matmul(o, AT[:, e, tb, :], G_V[:, tb, g * DH:(g + 1) * DH], start=True, stop=True,
                              skip_group_check=True)
                    for c in range(2 * tb, 2 * tb + 2):
                        if c == 0:
                            continue
                        r = slice((c % 2) * CHUNK, (c % 2) * CHUNK + CHUNK)
                        m = pe.matmul(o[r, :], G_Q[:, g, c * CHUNK:(c + 1) * CHUNK], ST[:, e, c - 1, :],
                                      start=False, stop=True, skip_group_check=True)
                m.then_inc(S.g_o, 1)
        turn_heads(S.g_y, S.g_turn, S.mix_y, 4)
        for h in range(H + 2):
            if h < H:
                e = h % 2
                if h >= 2:
                    pe.wait_ge(S.a_exp, h - 1)
                for tb, (a, b) in enumerate(((0, P), (P, 384))):
                    y = slice(tb * P, tb * P + P)
                    pe.matmul(PS[:, e, a:b], FQ[:, h, y], FK[:, h, 0:b - a], start=True, stop=False)
                    m = pe.matmul(PS[:, e, a:b], bcast(ident[:, h:h + 1], [P]), RA[:, 0:b - a], start=False, stop=True)
                m.then_inc(S.a_scores, 1)
            if 1 <= h <= H:
                g = h - 1
                e = g % 2
                pe.wait_ge(S.a_prob, g + 1)
                if g >= 2:
                    pe.wait_ge(S.a_pTcp, g - 1)
                for k in range(3):
                    m = pe.transpose(PS[:, 2 + e, k * P:k * P + P], E[:, e, k * P:k * P + P], ident[:])
                m.then_inc(S.a_pT, 1)
            if h >= 2:
                g = h - 2
                e = g % 2
                pe.wait_ge(S.a_pTcp, g + 1)
                if g >= 2:
                    pe.wait_ge(S.mix_a, g - 1)
                v = slice(g * DH, (g + 1) * DH)
                pe.matmul(PS[:, 4 + e, 0:T], FV[:, 0, v], PM[:, e, 0:T], start=True, stop=True)
                pe.matmul(PS[:, 4 + e, P:T], FV[:, 1, v], PM[:, e, T:384], start=False, stop=True,
                          skip_group_check=True).then_inc(S.a_out, 1)
        pe.wait_ge(S.mix_lo, 8)
        for s in range(S_OUT2, S_OUT2 + 4):
            pe_slab(pe, s // 2, s % 2, False)

        turn_x(pe, 3, NRM)
        pe.wait_ge(S.xt_lo, 32)
        with pe.Fori(0, FPAIRS) as i:
            for k in range(2):
                pe_slab(pe, i + S_FF // 2, k, True)

        def down(j, s, first=False):
            for u in range(UNITS):
                k = u % 2
                pe.wait_ge(lo_full[k], s * 2 + u // 2 + 1)
                pe.wait_ge(S.al_full, j * UNITS + u + 1)
                for tb in range(TB):
                    y = slice(tb * P, tb * P + P)
                    for b in range(4):
                        o = PS[:, 4 * tb + b, :]
                        for n, (x, w) in enumerate(((ah, wh), (ah, wl), (al, wh))):
                            m = pe.matmul(o, x[k][:, y], w[k][:, b, :], start=first and u == 0 and n == 0,
                                          stop=False, skip_group_check=True)
                m.then_inc(w_free[k], 1)

        pe.wait_ge(evac[0], S_DOWN // 2)
        pe.wait_ge(evac[1], S_DOWN // 2)
        down(0, S_DOWN, True)
        with pe.Fori(1, NDOWN) as i:
            down(i, i + S_DOWN)
        pe.wait_ge(w_free[1], 2 * (S_DOWN + NDOWN))
        pe.nop().then_inc(S.down_done, 1)


_INS = ["x", "ln_in_g", "ln_in_b", "w_in", "b_gate", "conv_w", "conv_b", "mh_norm_g", "w_out", "ln1_g", "ln1_b",
        "peer_wq", "peer_keys", "peer_u", "peer_v", "ln2_g", "ln2_b", "norm1_gain_2", "w_in_2", "hgrn_lb_param_2",
        "hgrn_norm_gain_2", "fox_gate_bias_2", "w_out_2", "norm2_gain_2", "w_ffn_gate_2", "w_ffn_up_2",
        "ffn_conv_w_2", "ffn_conv_b_2", "w_ffn_down_2", "final_norm_gain_2"]


def kernel(**inputs):
    import concourse.bacc as bacc
    import numpy as np
    from concourse.bass_utils import run_bass_kernel_spmd

    nc = bacc.Bacc("TRN2", target_bir_lowering=False, num_devices=1)
    arrays, aps = {}, {}
    for name in _INS:
        a = np.ascontiguousarray(inputs[name])
        arrays[f"in_{name}"] = a
        aps[name] = nc.dram_tensor(f"in_{name}", a.shape, mybir.dt.from_np(a.dtype), kind="ExternalInput").ap()
    out = nc.dram_tensor("out_y", (1, T, D), F32, kind="ExternalOutput").ap()
    block_kernel(nc, aps, out)
    r = run_bass_kernel_spmd(nc, [arrays], core_ids=[0])
    return r.results[0]["out_y"]
```

```python
from contextlib import ExitStack

import concourse.bass as bass
from concourse import mybir

F32 = mybir.dt.float32
F32R = mybir.dt.float32r
I32 = mybir.dt.int32
U32 = mybir.dt.uint32
ALU = mybir.AluOpType
ACT = mybir.ActivationFunctionType
AX = mybir.AxisListType.X
ds = bass.ds

P = 128
T = 256
TB = T // P
D = 2048
DC = D // P
W = 512
UC = 4
UNITS = DC // UC
H = 8
DH = 128
HW = H * DH
CHUNK = 64
NCH = T // CHUNK
FF = 5632
FC = FF // P
FPAIRS = FF // W
NEXP = 16384
NKEY = 128
TOPK = 16
ALPHA = 2.0 ** 0.25
LN_EPS = 1e-5
RMS_EPS = 1e-6
LOWEST = -3.0e38
SCALE = float(DH) ** -0.5
RING = 4

S_IN, S_OUT, S_WQ, S_IN2, S_OUT2, S_FF, S_DOWN = 0, 14, 18, 22, 36, 40, 62
NDOWN = FC // UC
GATES2, HEADS2, ATTN = 7, 11, 43


def wait_alone(eng, sem, value, passed):
    eng.wait_ge(sem, value).then_inc(passed, 1)


class Chain:

    def __init__(self, eng, sem, passed):
        self.eng, self.sem, self.passed, self.n, self.reg, self.per = eng, sem, passed, 0, None, 0

    def __call__(self, instruction, *signals):
        self.n += 1
        instruction.then_inc(self.sem, 1)
        value = self.n if self.reg is None else self.reg * self.per + self.n
        for s in signals:
            self.eng.wait_ge(self.sem, value).then_inc(s, 1)
        if not signals and self.reg is None:
            self.eng.wait_ge(self.sem, value)
        elif not signals:
            wait_alone(self.eng, self.sem, value, self.passed)

    def enter(self, reg, first, per):
        self.reg, self.per, self.at = reg, per, self.n
        self.n -= first * per

    def leave(self, first, trips):
        made = self.n + first * self.per - self.at
        assert made == self.per, f"the loop's body makes {made} links"
        self.n = self.at + trips * self.per
        self.reg = None


def block_kernel(nc, inp, out):
    ctx = ExitStack()
    with ctx:
        build(nc, inp, out, ctx)


def build(nc, inp, out, ctx):
    def sem(name):
        return ctx.enter_context(nc.semaphore(name))

    class S:

        x_in = sem("x_in")
        norm_in = sem("norm_in")
        stage_clear = sem("stage_clear")
        stage_in = sem("stage_in")
        small_in = sem("small_in")
        wf_in = sem("wf_in")
        keys_in = sem("keys_in")
        stored = sem("stored")
        ident_ready = sem("ident_ready")
        consts = sem("consts")
        pool_chain = sem("pool_chain")
        pool_passed = sem("pool_passed")
        act_chain = sem("act_chain")
        act_passed = sem("act_passed")
        dve_chain = sem("dve_chain")
        dve_passed = sem("dve_passed")
        square_ready = sem("square_ready")
        root_ready = sem("root_ready")
        tm_ready = sem("tm_ready")
        xt_ps = sem("xt_ps")
        xt_hi = sem("xt_hi")
        xt_lo = sem("xt_lo")
        cols_ps = sem("cols_ps")
        cols_ready = sem("cols_ready")
        mix_y = sem("mix_y")
        mix_a = sem("mix_a")
        mix_hi = sem("mix_hi")
        mix_lo = sem("mix_lo")
        conv_done = sem("conv_done")
        wg_hi = sem("wg_hi")
        wg_lo = sem("wg_lo")
        wf_hi = sem("wf_hi")
        wf_lo = sem("wf_lo")
        gate_ps = sem("gate_ps")
        gate_abs = sem("gate_abs")
        gate_ln = sem("gate_ln")
        gates_tm = sem("gates_tm")
        gates_T = sem("gates_T")
        gates_cm = sem("gates_cm")
        gates_back = sem("gates_back")
        em_arg = sem("em_arg")
        em_ready = sem("em_ready")
        m_scores = sem("m_scores")
        m_arg = sem("m_arg")
        m_exp = sem("m_exp")
        m_prob = sem("m_prob")
        m_num = sem("m_num")
        m_numcp = sem("m_numcp")
        m_y = sem("m_y")
        m_turn = sem("m_turn")
        keyT_ps = sem("keyT_ps")
        keyT = sem("keyT")
        score_ps = sem("score_ps")
        scores_cp = sem("scores_cp")
        soft_arg = sem("soft_arg")
        soft_exp = sem("soft_exp")
        uidx_ready = sem("uidx_ready")
        dot_done = sem("dot_done")
        dots_ready = sem("dots_ready")
        gelu_ready = sem("gelu_ready")
        ew_ready = sem("ew_ready")
        diag_ready = sem("diag_ready")
        v_done = sem("v_done")
        acc_done = sem("acc_done")
        ffsum = sem("ffsum")
        ln2_done = sem("ln2_done")
        nrm = sem("nrm")
        nrm_used = sem("nrm_used")
        lb_arg = sem("lb_arg")
        lb_exp = sem("lb_exp")
        f_ready = sem("f_ready")
        lnf_ready = sem("lnf_ready")
        b_ready = sem("b_ready")
        expb_ready = sem("expb_ready")
        dcay_ready = sem("dcay_ready")
        ke_arg = sem("ke_arg")
        expe_ready = sem("expe_ready")
        q_decayed = sem("q_decayed")
        expnb_ready = sem("expnb_ready")
        k_decayed = sem("k_decayed")
        c_ready = sem("c_ready")
        g_keT = sem("g_keT")
        g_ke = sem("g_ke")
        g_attn = sem("g_attn")
        g_ds = sem("g_ds")
        g_state = sem("g_state")
        g_o = sem("g_o")
        g_ocp = sem("g_ocp")
        g_y = sem("g_y")
        g_turn = sem("g_turn")
        a_scores = sem("a_scores")
        a_max = sem("a_max")
        a_exp = sem("a_exp")
        a_prob = sem("a_prob")
        a_pT = sem("a_pT")
        a_pTcp = sem("a_pTcp")
        a_out = sem("a_out")
        ff_y = sem("ff_y")
        ff_conv = sem("ff_conv")
        ff_silu = sem("ff_silu")
        ff_up = sem("ff_up")
        ah_full = sem("ah_full")
        al_full = sem("al_full")
        down_done = sem("down_done")
        final = sem("final")

    base = (nc.sbuf_base + 63) // 64 * 64
    total = nc.sbuf_usable_end - base
    ctx.enter_context(nc.sbuf_tensor("arena", [P, total // 4 - 32], F32))
    K = 1024

    def at(name, kb, shape, dt=F32):
        return nc.alloc_sbuf_tensor_at(name, [P, *shape], dt, offset=base + int(kb * K))

    raw = [at(f"raw{k}", 8 * k, [UC, W]) for k in range(UNITS)]
    wh = [at(f"wh{k}", 32 + 8 * k, [UC, W], F32R) for k in range(2)]
    wl = [at(f"wl{k}", 48 + 8 * k, [UC, W], F32R) for k in range(2)]
    XH = at("XH", 64, [DC, T], F32R)
    XL = at("XL", 80, [DC, T], F32R)
    RES = at("RES", 96, [TB, D])
    MIX = at("MIX", 112, [DC, T])
    GAIN = at("GAIN", 112, [D])
    BIAS = at("BIAS", 120, [D])
    ident = at("ident", 128, [P])
    mask01 = at("mask01", 128.5, [384])
    maskneg = at("maskneg", 130, [384])
    hmask = at("hmask", 131.5, [P])
    smask = at("smask", 132, [T])
    ones = at("ones", 133, [T])
    iota_i = at("iota_i", 134, [TOPK], I32)
    iota_f = at("iota_f", 134.125, [TOPK])
    stage = at("stage", 134.25, [3, P])
    cols = at("cols", 135.75, [3, P])
    SM = 137.25
    bgate = at("bgate", SM, [16])
    fbias = at("fbias", SM + 0.0625, [H])
    hgain = at("hgain", SM + 0.125, [DH])
    mv = at("mv", SM + 0.75, [TB, 2])
    rstd = at("rstd", SM + 0.8125, [TB])
    msq = at("msq", SM + 0.84375, [TB])
    glog = at("glog", SM + 0.875, [TB, 16])
    gabs = at("gabs", SM + 1, [TB, 16])
    gln = at("gln", SM + 1.125, [TB, 16])
    lb0 = at("lb0", SM + 1.25, [H])
    lb1 = at("lb1", SM + 1.28125, [H])
    lbm = at("lbm", SM + 1.3125, [H])
    lbs = at("lbs", SM + 1.34375, [H])
    lb = at("lb", SM + 1.375, [H])
    omlb = at("omlb", SM + 1.40625, [H])
    dcay = at("dcay", SM + 1.4375, [H, NCH])
    PH = 139
    ZC = at("ZC", PH, [H, T + 2])
    QT = at("QT", PH + 8.25, [H, T])
    KT = at("KT", PH + 16.25, [H, T])
    VX = at("VX", PH + 24.25, [TB, H, DH + 2])
    OG = at("OG", PH + 32.5, [TB, HW])
    mhg = at("mhg", PH + 40.5, [HW])
    wg_raw = at("wg_raw", PH + 44.5, [DC, 16])
    wg_h = at("wg_h", PH + 45.5, [DC, 16], F32R)
    wg_l = at("wg_l", PH + 46.5, [DC, 16], F32R)
    HN = at("HN", PH + 47.5, [TB, H, DH + 2])
    E1 = at("E1", PH + 55.75, [384])
    PM1 = at("PM1", PH + 57.25, [384])
    GP1 = at("GP1", PH + 58.75, [TB, P])
    BP1 = at("BP1", PH + 59.75, [T])
    RA1 = at("RA1", PH + 60.75, [T])
    LF1 = at("LF1", PH + 61.75, [T])
    LI = at("LI", PH + 62.75, [T])
    FS = at("FS", PH + 63.75, [T])
    CM = at("CM", PH + 64.75, [T])
    HS = PH + 66.5
    bcol = at("bcol", HS, [TB, H])
    emcol = at("emcol", HS + 0.0625, [TB, H])
    den = at("den", HS + 0.125, [TB, H])
    hstat = at("hstat", HS + 0.25, [H, 6])
    hmv = at("hmv", HS + 0.5, [H, 2])
    hr = at("hr", HS + 0.625, [H])
    nmax = at("nmax", HS + 0.75, [2, TB])
    psum_ = at("psum_", HS + 0.8125, [2, TB])
    stats = at("stats", HS + 0.875, [TB, 4, 6])
    G_F = at("G_F", PH, [H, T])
    G_B = at("G_B", PH + 8, [H, T])
    G_Q = at("G_Q", PH + 16, [H, T])
    GO = at("GO", PH + 16, [H, TB, DH])
    G_E = at("G_E", PH + 24, [H, T])
    G_K = at("G_K", PH + 32, [H, T])
    G_V = at("G_V", PH + 40, [TB, HW])
    G_G = at("G_G", PH + 48, [TB, HW])
    FQ = at("FQ", PH, [H, T])
    FK = at("FK", PH + 8, [H, T])
    FV = at("FV", PH + 56, [TB, HW])
    wf_raw = at("wf_raw", PH + 64, [DC, H])
    wf_h = at("wf_h", PH + 64.5, [DC, H], F32R)
    wf_l = at("wf_l", PH + 65, [DC, H], F32R)
    RA2 = at("RA2", PH + 65.5, [T])
    GP2 = at("GP2", PH + 48, [TB, P])
    BP2 = at("BP2", PH + 49, [T])
    LF2 = at("LF2", PH + 50, [T])
    AT = at("AT", PH + 51, [2, TB, P])
    ST = at("ST", PH + 53, [3, P])
    KE = at("KE", PH + 54.5, [NCH - 1, DH])
    E2 = at("E2", PH + 24, [2, 384])
    PM2 = at("PM2", PH + 27, [2, 384])
    PQ = at("PQ", 112, [DC, T])
    KR = at("KR", PH, [DC, P])
    KX = at("KX", PH + 50.5, [DC, P])
    SC = at("SC", PH + 32, [TB, H + 1, 2, NKEY])
    TK = PH + 58.5
    sc = at("sc", TK, [2, NKEY])
    sc2 = at("sc2", TK + 1, [2, NKEY])
    best = at("best", TK + 2, [2, TOPK])
    bidx = at("bidx", TK + 2.125, [2, TOPK], U32)
    bidf = at("bidf", TK + 2.25, [2, TOPK])
    tops = at("tops", TK + 2.375, [TOPK])
    topj = at("topj", TK + 2.4375, [TOPK], U32)
    tij = at("tij", TK + 2.5, [2, TOPK], U32)
    tijf = at("tijf", TK + 2.625, [2, TOPK])
    eids = at("eids", TK + 2.75, [2, TOPK])
    eidf = at("eidf", TK + 2.875, [TOPK])
    nmx = at("nmx", TK + 2.9375, [1])
    esum = at("esum", TK + 2.96875, [1])
    rsum = at("rsum", TK + 3, [1])
    eexp = at("eexp", TK + 3.0625, [TOPK])
    gate = at("gate", TK + 3.125, [2, TOPK])
    uidx = at("uidx", TK + 3.25, [2, TOPK], U32)
    vidx = at("vidx", TK + 3.375, [2, TOPK], U32)
    dots = at("dots", TK + 3.5, [2, TOPK])
    acts = at("acts", TK + 3.625, [2, TOPK])
    ew = at("ew", TK + 3.75, [2, TOPK])
    cand = at("cand", TK + 4, [TOPK, TOPK])
    cand2 = at("cand2", TK + 5, [TOPK, TOPK])
    hot = at("hot", TK + 6, [2, TOPK, TOPK])
    diag = at("diag", 120, [TOPK, P])
    ub = [at(f"ub{k}", PH + 8 * k, [D]) for k in range(RING)]
    vb = [at(f"vb{k}", 64 + 8 * k, [D]) for k in range(RING)]
    NRM = at("NRM", PH, [TB, D])
    FA = at("FA", PH, [FC, T])
    FY = at("FY", PH + 44, [4, T])
    ah = [at(f"ah{k}", PH + 48 + k, [T], F32R) for k in range(2)]
    al = [at(f"al{k}", PH + 50 + k, [T], F32R) for k in range(2)]

    PS = ctx.enter_context(nc.psum_tensor("PS", [P, 8, 512], F32))

    raw_full = [sem(f"raw_full{k}") for k in range(UNITS)]
    hi_full = [sem(f"hi_full{k}") for k in range(2)]
    lo_full = [sem(f"lo_full{k}") for k in range(2)]
    w_free = [sem(f"w_free{k}") for k in range(2)]
    evac = [sem(f"evac{k}") for k in range(2)]
    u_full = [sem(f"u_full{k}") for k in range(RING)]
    v_full = [sem(f"v_full{k}") for k in range(RING)]

    def w_view(w):
        return w[0].rearrange("(c p) n -> p c n", p=P)

    def load_unit(sp, s, u, src):
        if not (isinstance(s, int) and s == 0):
            sp.wait_ge(lo_full[u % 2], (s - 1) * 2 + u // 2 + 1)
        sp.dma_start(raw[u][:], src).then_inc(raw_full[u], 16)

    def split_hi(act, s, u):
        act.wait_ge(raw_full[u], (s + 1) * 16)
        if not (isinstance(s, int) and s == 0 and u < 2):
            act.wait_ge(w_free[u % 2], s * 2 + u // 2)
        act.copy(wh[u % 2][:], raw[u][:]).then_inc(hi_full[u % 2], 1)

    def split_lo(dve, s, u):
        dve.wait_ge(hi_full[u % 2], s * 2 + u // 2 + 1)
        dve.tensor_tensor(wl[u % 2][:], raw[u][:], wh[u % 2][:].bitcast(F32),
                          ALU.subtract).then_inc(lo_full[u % 2], 1)

    def slab_ready(eng, s):
        eng.wait_ge(w_free[1], s * 2 + 2)

    def lead(eng, split, s0):
        split(eng, s0, 0)
        split(eng, s0, 1)

    def run_slabs(eng, split, s0, n, events):
        for i in range(2, 4 * n + 2):
            if i < 4 * n:
                split(eng, s0 + i // 4, i % 4)
            for f in events.get(((i - 2) // 4, (i - 2) % 4), ()):
                f()

    def slot(n):
        return n // 2, 2 * (n % 2) + 1

    def plan(*parts):
        events = {}
        for part in parts:
            for slab, unit, f in part:
                events.setdefault((slab, unit), []).append(f)
        return events

    def each(f, s0, n):
        return [(j, 3, lambda j=j: f(s0 + j)) for j in range(n)]

    def cm_out(buf):
        return PS[:, 2 * buf:2 * buf + 2, :].rearrange("p b (t n) -> p (b t) n", n=T)

    def tm_out(buf):
        return PS[:, 2 * buf:2 * buf + 2, :]

    def pe_slab(pe, half, buf, cm, events=None, slab=None, x_in=None):
        if not (isinstance(half, int) and half == 0):
            pe.wait_ge(evac[buf], half)
        for u in range(UNITS):
            pe.wait_ge(lo_full[u % 2], half * 4 + buf * 2 + u // 2 + 1)
            if x_in:
                pe.wait_ge(x_in[0], x_in[1] + u)
            mm_unit(pe, u, buf, cm).then_inc(w_free[u % 2], 1)
            for f in (events or {}).get((slab, u), ()):
                f()

    def mm_unit(pe, u, buf, cm):
        k = u % 2
        if cm:
            o = cm_out(buf)
            for t in range(4):
                for c in range(UC):
                    x = slice(t * P, t * P + P)
                    d = u * UC + c
                    first = u == 0 and c == 0 and t % 2 == 0
                    pe.matmul(o[:, t, :], wh[k][:, c, x], XH[:, d, :], start=first, stop=False,
                              skip_group_check=True)
                    pe.matmul(o[:, t, :], wh[k][:, c, x], XL[:, d, :], start=False, stop=False,
                              skip_group_check=True)
                    m = pe.matmul(o[:, t, :], wl[k][:, c, x], XH[:, d, :], start=False,
                                  stop=d == DC - 1, skip_group_check=True)
            return m
        o = tm_out(buf)
        for tb in range(TB):
            y = slice(tb * P, tb * P + P)
            for c in range(UC):
                d = u * UC + c
                pe.matmul(o[:, tb, :], XH[:, d, y], wh[k][:, c, :], start=d == 0, stop=False,
                          skip_group_check=True)
                pe.matmul(o[:, tb, :], XH[:, d, y], wl[k][:, c, :], start=False, stop=False,
                          skip_group_check=True)
                m = pe.matmul(o[:, tb, :], XL[:, d, y], wh[k][:, c, :], start=False,
                              stop=d == DC - 1, skip_group_check=True)
        return m

    def bank4(b):
        return PS[:, b, :].rearrange("p (c n) -> p c n", n=P)

    def turn_x(pe, n, src):
        for g in range(8):
            tb, q = g // 4, g % 4
            pe.wait_ge(S.tm_ready, 2 * n + tb + 1)
            if g >= 4:
                pe.wait_ge(S.xt_lo, 8 * n + g - 3)
            for c in range(4):
                m = pe.transpose(bank4(4 + g % 4)[:, c, :], src[:, tb, (4 * q + c) * P:(4 * q + c + 1) * P], ident[:])
            m.then_inc(S.xt_ps, 1)

    def x_part(x, g):
        return x[:, 4 * (g % 4):4 * (g % 4) + 4, (g // 4) * P:(g // 4 + 1) * P]

    def x_hi(act, n):
        for g in range(8):
            act.wait_ge(S.xt_ps, 8 * n + g + 1)
            act.copy(x_part(XH, g), bank4(4 + g % 4)).then_inc(S.xt_hi, 1)

    def x_lo(dve, n, g0=0, g1=8):
        for g in range(g0, g1):
            dve.wait_ge(S.xt_hi, 8 * n + g + 1)
            dve.tensor_tensor(x_part(XL, g), bank4(4 + g % 4), x_part(XH, g).bitcast(F32),
                              ALU.subtract).then_inc(S.xt_lo, 1)

    def mix_hi(act, g):
        act.copy(XH[:, 4 * g:4 * g + 4, :], MIX[:, 4 * g:4 * g + 4, :]).then_inc(S.mix_hi, 1)

    def mix_lo(dve, n, g):
        dve.wait_ge(S.mix_hi, 4 * n + g + 1)
        dve.tensor_tensor(XL[:, 4 * g:4 * g + 4, :], MIX[:, 4 * g:4 * g + 4, :],
                          XH[:, 4 * g:4 * g + 4, :].bitcast(F32), ALU.subtract).then_inc(S.mix_lo, 1)

    def bcast(v, shape):
        return v.to_broadcast([P, *shape])

    block = ctx.enter_context(nc.Block())

    @block.sync
    def _(sp):
        def row(v, n):
            return v.partition_broadcast(P)

        for tb in range(TB):
            sp.dma_start(RES[:, tb, :], inp["x"][0].rearrange("(b p) d -> b p d", p=P)[tb]).then_inc(S.x_in, 16)
        sp.dma_start(GAIN[:], row(inp["ln_in_g"], D)).then_inc(S.norm_in, 16)
        sp.dma_start(BIAS[:], row(inp["ln_in_b"], D)).then_inc(S.norm_in, 16)
        sp.wait_ge(S.stage_clear, 1)
        sp.dma_start(stage[0:24, 0, :], inp["conv_w"][0].rearrange("j (c p) -> (j c) p", p=P)).then_inc(S.stage_in, 16)
        sp.dma_start(stage[24:32, 0, :], inp["conv_b"][0].rearrange("(c p) -> c p", p=P)).then_inc(S.stage_in, 16)
        sp.dma_start(stage[32:48, 0, :], inp["hgrn_lb_param_2"].rearrange("l (c p) -> (l c) p", p=P)).then_inc(S.stage_in, 16)
        fw = inp["ffn_conv_w_2"][0].rearrange("j (c p) -> j c p", p=P)
        sp.dma_start(stage[0:FC, 1, :], fw[0]).then_inc(S.stage_in, 16)
        sp.dma_start(stage[FC:2 * FC, 1, :], fw[1]).then_inc(S.stage_in, 16)
        sp.dma_start(stage[0:FC, 2, :], fw[2]).then_inc(S.stage_in, 16)
        sp.dma_start(stage[FC:2 * FC, 2, :], inp["ffn_conv_b_2"][0].rearrange("(c p) -> c p", p=P)).then_inc(S.stage_in, 16)
        sp.dma_start(bgate[:], row(inp["b_gate"][0], 16)).then_inc(S.small_in, 16)
        sp.dma_start(fbias[:], row(inp["fox_gate_bias_2"][0], H)).then_inc(S.small_in, 16)
        sp.dma_start(hgain[:], row(inp["hgrn_norm_gain_2"][0], DH)).then_inc(S.small_in, 16)
        sp.dma_start(mhg[:], row(inp["mh_norm_g"][0], HW)).then_inc(S.small_in, 16)
        w_in = w_view(inp["w_in"])
        sp.dma_start(wg_raw[:], w_in[:, :, 14 * W:14 * W + 16]).then_inc(S.small_in, 16)

        def stream(s0, w, c0, n):
            if s0 == 0:
                for u in range(UNITS):
                    load_unit(sp, 0, u, w[:, u * UC:(u + 1) * UC, c0:c0 + W])
                s0, c0, n = 1, c0 + W, n - 1
            with sp.Fori(0, n) as i:
                for u in range(UNITS):
                    load_unit(sp, i + s0, u, w[:, u * UC:(u + 1) * UC, ds(i * W + c0, W)])

        stream(0, w_in, 6 * W, 6)
        stream(6, w_in, 2 * W, 4)
        stream(10, w_in, 0, 2)
        stream(12, w_in, 12 * W, 2)
        stream(S_OUT, w_view(inp["w_out"]), 0, 2)
        sp.wait_ge(S.mix_lo, 4)
        sp.dma_start(GAIN[:], row(inp["ln1_g"][0], D)).then_inc(S.norm_in, 16)
        sp.dma_start(BIAS[:], row(inp["ln1_b"][0], D)).then_inc(S.norm_in, 16)
        keys = inp["peer_keys"][0].rearrange("h q n c -> (h q) n c")
        for n in range(2 * H):
            sp.dma_start(KR[:, n, :], keys[n]).then_inc(S.keys_in, 16)
        stream(S_OUT + 2, w_view(inp["w_out"]), 2 * W, 2)
        stream(S_WQ, w_view(inp["peer_wq"]), 0, 4)
        w_in2 = w_view(inp["w_in_2"])
        for u in range(UNITS):
            load_unit(sp, S_IN2, u, w_in2[:, u * UC:(u + 1) * UC, 2 * W:3 * W])
        sp.wait_ge(S.ffsum, 8)
        sp.dma_start(GAIN[:], row(inp["ln2_g"][0], D)).then_inc(S.norm_in, 16)
        sp.dma_start(BIAS[:], row(inp["ln2_b"][0], D)).then_inc(S.norm_in, 16)
        sp.dma_start(wf_raw[:], w_in2[:, :, 14 * W:14 * W + H]).then_inc(S.wf_in, 16)
        sp.wait_ge(S.ln2_done, 2)
        sp.dma_start(GAIN[:], row(inp["norm1_gain_2"][0], D)).then_inc(S.norm_in, 16)
        with sp.Fori(0, 1) as i:
            for u in range(UNITS):
                load_unit(sp, i + S_IN2 + 1, u, w_in2[:, u * UC:(u + 1) * UC, ds(i * W + 3 * W, W)])
        stream(S_IN2 + 2, w_in2, 0, 2)
        stream(S_IN2 + 4, w_in2, 4 * W, 2)
        stream(S_IN2 + 6, w_in2, 8 * W, 6)
        stream(S_IN2 + 12, w_in2, 6 * W, 2)
        w_out2 = w_view(inp["w_out_2"])

        def load_out(j):
            for u in range(UNITS):
                r = (u + UNITS // 2) % UNITS * UC
                load_unit(sp, S_OUT2 + j, u, w_out2[:, r:r + UC, j * W:(j + 1) * W])

        load_out(0)
        load_out(1)
        sp.wait_ge(S.mix_lo, 8)
        sp.dma_start(GAIN[:], row(inp["norm2_gain_2"][0], D)).then_inc(S.norm_in, 16)
        load_out(2)
        load_out(3)
        wgt, wup = w_view(inp["w_ffn_gate_2"]), w_view(inp["w_ffn_up_2"])
        with sp.Fori(0, FPAIRS) as i:
            for k, w in enumerate((wgt, wup)):
                for u in range(UNITS):
                    load_unit(sp, i * 2 + S_FF + k, u, w[:, u * UC:(u + 1) * UC, ds(i * W, W)])
        wdn = inp["w_ffn_down_2"][0].rearrange("(c p) (b n) -> c p b n", p=P, n=W)
        with sp.Fori(0, NDOWN) as i:
            for u in range(UNITS):
                load_unit(sp, i + S_DOWN, u, wdn[ds(i * UNITS + u, 1)].rearrange("o p b n -> (o p) b n"))
        sp.wait_ge(S.tm_ready, 8)
        sp.dma_start(GAIN[:], row(inp["final_norm_gain_2"], D)).then_inc(S.norm_in, 16)
        for tb in range(TB):
            sp.wait_ge(S.final, tb + 1)
            sp.dma_start(out[0].rearrange("(b p) d -> b p d", p=P)[tb], RES[:, tb, :]).then_inc(S.stored, 16)
        sp.wait_ge(S.stored, 16 * TB)

    @block.gpsimd
    def _(pool):
        link = Chain(pool, S.pool_chain, S.pool_passed)
        pool.memset(stage[:], 0.0).then_inc(S.stage_clear, 1)
        link(pool.memset(ident[:], 0.0))
        pool.affine_select(ident[:], ident[:], [[1, P]], ALU.not_equal, 1.0, base=0,
                           channel_multiplier=-1).then_inc(S.ident_ready, 1)
        pool.memset(smask[:], 1.0)
        pool.memset(ones[:], 1.0)
        pool.memset(maskneg[:], 0.0)
        pool.memset(hmask[:], 1.0)
        link(pool.memset(mask01[:], 1.0))
        for a in (0, 256):
            pool.affine_select(mask01[:, a:a + P], mask01[:, a:a + P], [[1, P]], ALU.is_ge, 0.0, base=0,
                               channel_multiplier=-1)
            pool.affine_select(maskneg[:, a:a + P], maskneg[:, a:a + P], [[-1, P]], ALU.is_ge, LOWEST,
                               base=0, channel_multiplier=1)
        pool.memset(smask[:].rearrange("p (c n) -> p c n", n=CHUNK)[:, :, 0:1], 0.0)
        link(pool.affine_select(hmask[:], hmask[:], [[1, P]], ALU.is_ge, 0.0, base=0, channel_multiplier=-1))
        pool.memset(hmask[0:CHUNK, CHUNK:P], 0.0)
        pool.iota(iota_i[:], [[1, TOPK]], base=0, channel_multiplier=0).then_inc(S.consts, 1)


        def gather(buf, idx, k, table, sem):
            pool.indirect_dma_start(buf[:], None, table, bass.IndirectOffsetOnAxis(ap=idx[:, k:k + 1], axis=0),
                                    ).then_inc(sem, 16)

        def u_row(s, tb, k, first):
            if not (first and k < RING):
                wait_alone(pool, S.dot_done, s * TOPK + k - RING + 1, S.pool_passed)
            gather(ub[k % RING], uidx[:, tb, :], k, inp["peer_u"][0], u_full[k % RING])

        def v_row(s, tb, k, first):
            if first and k == 0:
                pool.wait_ge(w_free[1], 2 * S_WQ + 8)
            if not (first and k < RING):
                wait_alone(pool, S.v_done, s * TOPK + k - RING + 1, S.pool_passed)
            gather(vb[k % RING], vidx[:, tb, :], k, inp["peer_v"][0], v_full[k % RING])

        def step(s, tb, first=False):
            wait_alone(pool, S.uidx_ready, s + 1, S.pool_passed)
            for k in range(TOPK):
                u_row(s, tb, k, first)
                if not first:
                    v_row(s - 1, 1 - tb, k, isinstance(s, int) and s == 1)

        step(0, 0, True)
        step(1, 1)
        with pool.Fori(1, H) as i:
            for tb in range(TB):
                step(i * 2 + tb, tb)
        for k in range(TOPK):
            v_row(2 * H - 1, 1, k, False)

    @block.scalar
    def _(act):
        link = Chain(act, S.act_chain, S.act_passed)

        def root(n, x):
            act.wait_ge(S.square_ready, n + 1)
            act.activation(x, x, ACT.Sqrt).then_inc(S.root_ready, 1)

        root(0, rstd[:])
        act.wait_ge(S.small_in, 80)
        act.copy(wg_h[:], wg_raw[:]).then_inc(S.wg_hi, 1)
        lead(act, split_hi, S_IN)
        x_hi(act, 0)

        def q_out(dst, scale):
            def f(s):
                slab_ready(act, s)
                act.activation(dst[:, 4 * (s % 2):4 * (s % 2) + 4, :], cm_out(s % 2), ACT.Copy,
                               scale=scale).then_inc(evac[s % 2], 1)
            return f

        def v_out(s):
            slab_ready(act, s)
            act.copy(VX[:, :, 4 * (s % 2):4 * (s % 2) + 4, 0:DH],
                     tm_out(s % 2).rearrange("p b (h d) -> p b h d", d=DH)).then_inc(evac[s % 2], 1)

        def o_out(s):
            slab_ready(act, s)
            act.activation(OG[:, :, W * (s % 2):W * (s % 2) + W], tm_out(s % 2),
                           ACT.Sigmoid).then_inc(evac[s % 2], 1)

        def m_gates():
            act.wait_ge(S.gate_abs, 1)
            link(act.activation(gln[:], gabs[:], ACT.Exp, scale=-1.0))
            act.activation(gln[:], gln[:], ACT.Ln, bias=1.0).then_inc(S.gate_ln, 1)

        def m_floor():
            act.wait_ge(S.em_arg, 1)
            act.activation(emcol[:], emcol[:], ACT.Exp).then_inc(S.em_ready, 1)

        def m_head(h):
            if h < H:
                act.wait_ge(S.m_arg, h + 1)
                act.activation(E1[:], E1[:], ACT.Exp).then_inc(S.m_exp, 1)
            if h >= 1:
                act.wait_ge(S.m_num, h)
                act.copy(HN[:, :, h - 1, 0:DH + 1],
                         PS[:, 7, 0:TB * (DH + 1)].rearrange("p (b d) -> p b d", b=TB)).then_inc(S.m_numcp, 1)

        def turned_out(turned, half):
            act.wait_ge(turned, half + 1)
            for tb in range(TB):
                a = act.copy(MIX[:, H + 4 * half:H + 4 * half + 4, tb * P:(tb + 1) * P],
                             PS[:, 6 + tb, :].rearrange("p (h t) -> p h t", t=P))
            a.then_inc(S.mix_y, 1)

        outs = [q_out(QT, 1.0)] * 2 + [q_out(KT, SCALE)] * 2 + [v_out] * 2 + [None] * 6 + [o_out]
        run_slabs(act, split_hi, S_IN, 14, plan(
            [(j, 3, lambda j=j: outs[j](S_IN + j)) for j in range(13) if outs[j]],
            [(*slot(11), m_gates), (*slot(13), m_floor)],
            [(*slot(14 + h), lambda h=h: m_head(h)) for h in range(H + 1)],
            [(11, 3, lambda: root(1, hr[:])), (12, 1, lambda: root(2, hr[:]))],
            [(13, 2, lambda: turned_out(S.m_turn, 0))]))
        split_hi(act, S_OUT, 0)
        slab_ready(act, S_OUT - 1)
        act.wait_ge(S.conv_done, 2)
        mix_hi(act, 0)
        split_hi(act, S_OUT, 1)
        o_out(S_OUT - 1)
        mix_hi(act, 1)
        act.wait_ge(S.mix_y, 1)
        mix_hi(act, 2)
        turned_out(S.m_turn, 1)
        act.wait_ge(S.mix_y, 2)
        mix_hi(act, 3)

        def keys_turned():
            for n in range(4):
                act.wait_ge(S.keyT_ps, n + 1)
                act.copy(KX[:, 4 * n:4 * n + 4, :],
                         PS[:, 4 + n, :].rearrange("p (a k) -> p a k", k=P)).then_inc(S.keyT, 1)

        def bound_exp():
            act.wait_ge(S.lb_arg, 1)
            act.activation(lb0[:], lb0[:], ACT.Exp).then_inc(S.lb_exp, 1)
            act.activation(lb1[:], lb1[:], ACT.Exp).then_inc(S.lb_exp, 1)

        run_slabs(act, split_hi, S_OUT, 4, plan([(1, 2, bound_exp), (3, 2, keys_turned)]))
        lead(act, split_hi, S_WQ)
        root(3, rstd[:])

        x_hi(act, 1)

        def pq_out(s):
            slab_ready(act, s)
            j = s - S_WQ
            act.copy(PQ[:, 4 * j:4 * j + 4, :], cm_out(s % 2)).then_inc(evac[s % 2], 1)

        act.wait_ge(S.tm_ready, 4)
        run_slabs(act, split_hi, S_WQ, 4, plan(each(pq_out, S_WQ, 4)))
        for n in range(8):
            act.wait_ge(S.score_ps, n + 1)
            tb, q = n // 4, n % 4
            act.copy(SC[:, tb, 2 * q:2 * q + 2, :, :],
                     PS[:, 4 + n % 4, :].rearrange("p (h c k) -> p h c k", h=2, c=2)).then_inc(S.scores_cp, 1)

        def soft(n, par):
            act.wait_ge(S.soft_arg, n + 1)
            act.activation(eexp[:], tops[:], ACT.Exp, bias=nmx[:, 0:1], accum_out=esum[:]).then_inc(S.soft_exp, 1)

        def weigh(n, tb, first=False):
            act.wait_ge(S.dots_ready, n + 1)
            act.activation(acts[:, tb, :], dots[:, tb, :], ACT.Gelu).then_inc(S.gelu_ready, 1)
            act.wait_ge(S.ew_ready, n + 1)
            for k in range(TOPK):
                if not first:
                    act.wait_ge(S.v_done, (n - 1) * TOPK + k + 1)
                act.activation(diag[:, k, :], ident[:], ACT.Copy, scale=ew[:, tb, k:k + 1]).then_inc(S.diag_ready, 1)

        soft(0, 0)
        soft(1, 1)
        weigh(0, 0, True)
        soft(2, 0)
        weigh(1, 1)
        with act.Fori(1, H) as i:
            for tb in range(TB):
                soft(i * 2 + tb + 1, 1 - tb)
                weigh(i * 2 + tb, tb)

        lead(act, split_hi, S_IN2)
        root(4, rstd[:])
        root(5, rstd[:])
        x_hi(act, 2)

        def wf_split():
            act.wait_ge(S.wf_in, 16)
            act.copy(wf_h[:], wf_raw[:]).then_inc(S.wf_hi, 1)

        def part(x, j):
            return x[:, 4 * j:4 * j + 4, :]

        def f_out(s):
            slab_ready(act, s)
            act.wait_ge(S.nrm_used, 1)
            act.activation(part(G_F, s % 2), cm_out(s % 2), ACT.Sigmoid).then_inc(evac[s % 2], 1)

        def f_log(j):
            act.wait_ge(S.f_ready, j + 1)
            act.activation(part(G_E, j), part(G_F, j), ACT.Ln).then_inc(S.lnf_ready, 1)

        def b_exp(j):
            act.wait_ge(S.b_ready, j + 1)
            act.activation(part(G_K, j), part(G_B, j), ACT.Exp).then_inc(S.expb_ready, 1)
            act.activation(dcay[:, 4 * j:4 * j + 4, :],
                           part(G_B, j).rearrange("p h (c n) -> p h c n", n=CHUNK)[:, :, :, CHUNK - 1],
                           ACT.Exp).then_inc(S.dcay_ready, 1)

        def gq_out(s):
            slab_ready(act, s)
            j = s % 2
            act.activation(part(G_Q, j), cm_out(j), ACT.Copy, scale=SCALE).then_inc(evac[j], 1)
            act.wait_ge(S.ke_arg, j + 1)
            act.activation(part(G_E, j), part(G_E, j), ACT.Exp).then_inc(S.expe_ready, 1)

        def nb_exp(j):
            act.wait_ge(S.q_decayed, j + 1)
            act.activation(part(G_K, j), part(G_B, j), ACT.Exp, scale=-1.0).then_inc(S.expnb_ready, 1)

        def fqk_out(dst, scale):
            def f(s):
                slab_ready(act, s)
                act.wait_ge(S.k_decayed, 2)
                act.activation(part(dst, s % 2), cm_out(s % 2), ACT.Copy, scale=scale).then_inc(evac[s % 2], 1)
            return f

        def tm_copy(dst):
            def f(s):
                slab_ready(act, s)
                act.copy(dst[:, :, W * (s % 2):W * (s % 2) + W], tm_out(s % 2)).then_inc(evac[s % 2], 1)
            return f

        def g_out(s):
            slab_ready(act, s)
            act.wait_ge(S.g_ocp, H)
            act.activation(G_G[:, :, W * (s % 2):W * (s % 2) + W], tm_out(s % 2),
                           ACT.Silu).then_inc(evac[s % 2], 1)

        def a_gates():
            act.wait_ge(S.gate_abs, 2)
            link(act.activation(gln[:, :, 0:H], gabs[:, :, 0:H], ACT.Exp, scale=-1.0))
            act.activation(gln[:, :, 0:H], gln[:, :, 0:H], ACT.Ln, bias=1.0).then_inc(S.gate_ln, 1)

        def g_step(n):
            if n < H:
                act.wait_ge(S.g_keT, n + 1)
                if n >= 1:
                    act.wait_ge(S.g_ds, n)
                kt = PS[:, 5, 0:T].rearrange("p (b d) -> p b d", b=TB)
                act.copy(KE[0:CHUNK, 0:NCH - 1:2, :], kt[0:CHUNK])
                act.copy(KE[CHUNK:P, 1, :], kt[CHUNK:P, 0, :]).then_inc(S.g_ke, 1)
            if n >= 2:
                act.wait_ge(S.g_o, n - 1)
                act.copy(GO[:, n - 2, :, :], PS[:, 7, 0:T].rearrange("p (b d) -> p b d", b=TB)).then_inc(S.g_ocp, 1)

        def a_step(n):
            if 2 <= n < H + 2:
                g = n - 2
                act.wait_ge(S.a_pT, g + 1)
                if g >= 2:
                    act.wait_ge(S.a_out, g - 1)
                act.copy(PM2[:, g % 2, :], PS[:, 5, 0:384]).then_inc(S.a_pTcp, 1)
            if n < H:
                e = n % 2
                act.wait_ge(S.a_max, n + 1)
                act.activation(E2[:, e, 0:P], E2[:, e, 0:P], ACT.Exp, bias=nmax[:, e, 0:1],
                               accum_out=psum_[:, e, 0:1])
                act.activation(E2[:, e, P:384], E2[:, e, P:384], ACT.Exp, bias=nmax[:, e, 1:2],
                               accum_out=psum_[:, e, 1:2]).then_inc(S.a_exp, 1)

        outs2 = [f_out] * 2 + [gq_out] * 2 + [tm_copy(G_V)] * 2 + [fqk_out(FQ, SCALE)] * 2 \
            + [fqk_out(FK, 1.0)] * 2 + [tm_copy(FV)] * 2 + [g_out]
        run_slabs(act, split_hi, S_IN2, 14, plan(
            [(j, 3, lambda j=j: outs2[j](S_IN2 + j)) for j in range(13)],
            [(0, 1, wf_split), (*slot(GATES2), a_gates)],
            [(1 + j, 0, lambda j=j: f_log(j)) for j in range(2)],
            [(2 + j, 1, lambda j=j: b_exp(j)) for j in range(2)],
            [(3 + j, 0, lambda j=j: nb_exp(j)) for j in range(2)],
            [(*slot(HEADS2 + n), lambda n=n: g_step(n)) for n in range(H + 2)],
            [(10, 2, lambda: root(6, hr[:])), (10, 3, lambda: root(7, hr[:]))],
            [(*divmod(ATTN + n, UNITS), lambda n=n: a_step(n)) for n in range(H + 2)],
            [(13, 2, lambda: turned_out(S.g_turn, 0))]))
        split_hi(act, S_OUT2, 0)
        slab_ready(act, S_OUT2 - 1)
        act.wait_ge(S.mix_a, H)
        mix_hi(act, 0)
        split_hi(act, S_OUT2, 1)
        g_out(S_OUT2 - 1)
        mix_hi(act, 1)
        act.wait_ge(S.mix_y, 3)
        mix_hi(act, 2)
        turned_out(S.g_turn, 1)
        act.wait_ge(S.mix_y, 4)
        mix_hi(act, 3)
        run_slabs(act, split_hi, S_OUT2, 4, {})
        lead(act, split_hi, S_FF)
        root(8, rstd[:])

        x_hi(act, 3)

        def gate_conv(n, s):
            slab_ready(act, s)
            if not (isinstance(n, int) and n == 0):
                act.wait_ge(S.ff_up, n)
            for t in range(4):
                w2 = cols[:, 2, ds(n * 4 + t, 1)] if not isinstance(n, int) else cols[:, 2, 4 * n + t:4 * n + t + 1]
                b = cols[:, 2, ds(n * 4 + t + FC, 1)] if not isinstance(n, int) else cols[:, 2, FC + 4 * n + t:FC + 4 * n + t + 1]
                a = act.activation(FY[:, t, :], cm_out(0)[:, t, :], ACT.Identity, bias=b, scale=w2)
            a.then_inc(S.ff_y, 1)

        def gate_silu(n):
            act.wait_ge(S.ff_conv, n + 1)
            act.activation(FY[:], FY[:], ACT.Silu).then_inc(S.ff_silu, 1)

        def ff_pair(n, s, first=False):
            for u in range(2 if first else 0, UNITS):
                split_hi(act, s, u)
            split_hi(act, s + 1, 0)
            split_hi(act, s + 1, 1)
            gate_conv(n, s)
            split_hi(act, s + 1, 2)
            gate_silu(n)
            split_hi(act, s + 1, 3)

        ff_pair(0, S_FF, True)
        with act.Fori(1, FPAIRS) as i:
            ff_pair(i, i * 2 + S_FF)
        act.wait_ge(S.ff_up, FPAIRS)

        def down_hi(j, s):
            for u in range(UNITS):
                split_hi(act, s, u)
                act.copy(ah[u % 2][:], FA[:, ds(j * UNITS + u, 1), :].rearrange("p o n -> p (o n)")
                         if not isinstance(j, int) else FA[:, j * UNITS + u, :]).then_inc(S.ah_full, 1)

        down_hi(0, S_DOWN)
        with act.Fori(1, NDOWN) as i:
            down_hi(i, i + S_DOWN)
        root(9, rstd[:])

    @block.vector
    def _(dve):
        link = Chain(dve, S.dve_chain, S.dve_passed)

        def inverse_root(n, x, src, eps):
            dve.tensor_scalar(x, src, eps, None, ALU.add).then_inc(S.square_ready, 1)
            dve.wait_ge(S.root_ready, n + 1)
            link(dve.reciprocal(x, x))

        def row_stats(tb, q):
            return dve.bn_stats(stats[:, tb, q, :], RES[:, tb, q * W:(q + 1) * W])

        def moments():
            for tb in range(TB):
                a = dve.bn_aggr(mv[:, tb, :], stats[:, tb, :, :])
            link(a)

        def layer_norm(n, norms_in, ready, again=False):
            moments()
            inverse_root(n, rstd[:], mv[:, :, 1], LN_EPS)
            dve.wait_ge(S.norm_in, norms_in)
            for tb in range(TB):
                link(dve.scalar_tensor_tensor(RES[:, tb, :], RES[:, tb, :], mv[:, tb, 0:1], GAIN[:],
                                              ALU.subtract, ALU.mult))
                link(dve.scalar_tensor_tensor(RES[:, tb, :], RES[:, tb, :], rstd[:, tb:tb + 1], BIAS[:],
                                              ALU.mult, ALU.add), ready)
                if again:
                    dve.wait_ge(ready, tb + 1)
                    for q in range(4):
                        a = row_stats(tb, q)
            if again:
                link(a)

        def rms_norm(n, dst, norms_in, ready):
            moments()
            link(dve.tensor_tensor(msq[:], mv[:, :, 0], mv[:, :, 0], ALU.mult))
            link(dve.tensor_tensor(msq[:], msq[:], mv[:, :, 1], ALU.add))
            inverse_root(n, rstd[:], msq[:], RMS_EPS)
            dve.wait_ge(S.norm_in, norms_in)
            for tb in range(TB):
                dve.scalar_tensor_tensor(dst[:, tb, :], RES[:, tb, :], rstd[:, tb:tb + 1], GAIN[:],
                                         ALU.mult, ALU.mult).then_inc(ready, 1)

        def x_lead(n, s0):
            split_lo(dve, s0, 0)
            x_lo(dve, n, 0, 5)
            split_lo(dve, s0, 1)
            x_lo(dve, n, 5, 8)

        for tb in range(TB):
            dve.wait_ge(S.x_in, 32)
            for q in range(4):
                a = row_stats(tb, q)
        link(a)
        layer_norm(0, 32, S.tm_ready)
        dve.wait_ge(S.consts, 1)
        dve.tensor_copy(iota_f[:], iota_i[:])
        dve.wait_ge(S.wg_hi, 1)
        dve.tensor_tensor(wg_l[:], wg_raw[:], wg_h[:].bitcast(F32), ALU.subtract).then_inc(S.wg_lo, 1)
        x_lead(0, S_IN)
        dve.wait_ge(S.cols_ps, 1)
        link(dve.tensor_copy(cols[:], PS[:, 3, 0:384].rearrange("p (a n) -> p a n", n=P)), S.cols_ready)
        dve.memset(ZC[:, :, 0:2], 0.0)
        dve.memset(GP1[:], 0.0)
        dve.memset(BP1[:], 0.0)
        dve.memset(RA1[:], 0.0)
        link(dve.memset(VX[:, :, :, DH:DH + 1], 1.0))

        def c_out(s):
            slab_ready(dve, s)
            link(dve.tensor_copy(ZC[:, 4 * (s % 2):4 * (s % 2) + 4, 2:], cm_out(s % 2)), evac[s % 2])

        def h_out(s):
            slab_ready(dve, s)
            j = s % 2
            z = ZC[:, 4 * j:4 * j + 4, :]
            link(dve.tensor_tensor(z[:, :, 2:], z[:, :, 2:], cm_out(j), ALU.mult), evac[j])
            for t in range(4 * j, 4 * j + 4):
                dve.tensor_scalar(MIX[:, t, :], ZC[:, t, 2:], cols[:, 0, 16 + t:17 + t], cols[:, 0, 24 + t:25 + t],
                                  ALU.mult, ALU.add)
            for tap in (1, 0):
                link(dve.engine_nop())
                for t in range(4 * j, 4 * j + 4):
                    dve.scalar_tensor_tensor(MIX[:, t, :], ZC[:, t, tap:tap + T],
                                             cols[:, 0, 8 * tap + t:8 * tap + t + 1], MIX[:, t, :],
                                             ALU.mult, ALU.add)
            link(dve.engine_nop())

        def b_out(s):
            slab_ready(dve, s)
            j = s % 2
            m = MIX[:, 4 * j:4 * j + 4, :]
            link(dve.tensor_tensor(m, m, cm_out(j), ALU.mult), evac[j], S.conv_done)

        bt = PS[:, 6, 0:T].rearrange("p (b n) -> p b n", b=TB)

        def m_gates():
            dve.wait_ge(S.gate_ps, 1)
            link(dve.tensor_tensor(glog[:], PS[:, 6, 0:32].rearrange("p (b n) -> p b n", b=TB),
                                   bcast(bgate[:].unsqueeze(1), [TB, 16]), ALU.add))
            dve.scalar_tensor_tensor(gabs[:], glog[:], -1.0, glog[:], ALU.mult, ALU.max).then_inc(S.gate_abs, 1)
            dve.tensor_copy(GP1[:, :, 0:H], glog[:, :, 0:H])
            dve.wait_ge(S.gate_ln, 1)
            dve.scalar_tensor_tensor(GP1[:, :, 32:32 + H], glog[:, :, H:16], 0.0, gln[:, :, H:16], ALU.min,
                                     ALU.subtract).then_inc(S.gates_tm, 1)

        def m_cumulate():
            dve.wait_ge(S.gates_T, 1)
            dve.tensor_copy(LI[0:H, :], PS[0:H, 7, 0:T])
            link(dve.tensor_copy(LF1[0:H, :], PS[32:32 + H, 7, 0:T]))
            link(dve.tensor_tensor_scan(FS[0:H, :], ones[0:H, :], LF1[0:H, :], 0.0, ALU.mult, ALU.add))
            link(dve.tensor_tensor(BP1[0:H, :], LI[0:H, :], FS[0:H, :], ALU.subtract))
            link(dve.tensor_tensor_scan(CM[0:H, :], BP1[0:H, :], BP1[0:H, :], 0.0, ALU.max, ALU.max))
            link(dve.tensor_scalar(RA1[0:H, :], CM[0:H, :], -1.0, None, ALU.mult))
            link(dve.tensor_tensor(LF1[0:H, :], RA1[0:H, :], FS[0:H, :], ALU.subtract))
            dve.tensor_copy(BP1[32:32 + H, :], LF1[0:H, :]).then_inc(S.gates_cm, 1)

        def m_columns():
            dve.wait_ge(S.gates_back, 1)
            link(dve.tensor_copy(bcol[:], bt[:, :, 0:H]))
            dve.tensor_copy(emcol[:], bt[:, :, 32:32 + H]).then_inc(S.em_arg, 1)

        def m_head(h):
            dve.wait_ge(S.m_scores, h + 1)
            if h >= 1:
                dve.wait_ge(S.m_prob, h)
            dve.tensor_scalar(E1[:, 0:T], PS[:, 5, 0:T], bcol[:, 0, h:h + 1], 0.0, ALU.add, ALU.min)
            dve.tensor_scalar(E1[:, T:384], PS[:, 5, P:T], bcol[:, 1, h:h + 1], 0.0, ALU.add,
                              ALU.min).then_inc(S.m_arg, 1)
            dve.wait_ge(S.m_exp, h + 1)
            link(dve.tensor_tensor(E1[:], E1[:], mask01[:], ALU.mult))
            if h >= 1:
                dve.wait_ge(S.m_num, h)
            dve.tensor_tensor(PM1[:], E1[:], PS[:, 4, 0:384], ALU.mult).then_inc(S.m_prob, 1)

        def m_norm(tb):
            if tb == 0:
                dve.wait_ge(S.m_numcp, H)
                dve.wait_ge(S.em_ready, 1)
                link(dve.scalar_tensor_tensor(den[:], HN[:, :, :, DH], -1.0, HN[:, :, :, DH], ALU.mult, ALU.max))
                link(dve.tensor_tensor(den[:], den[:], emcol[:], ALU.max))
                link(dve.reciprocal(den[:], den[:]))
            hh = HN[:, tb, :, 0:DH]
            link(dve.tensor_tensor(hh, hh, bcast(den[:, tb, :].unsqueeze(2), [H, DH]), ALU.mult))
            for h in range(H):
                b = dve.bn_stats(hstat[:, h, :], HN[:, tb, h, 0:DH])
            link(b)
            for h in range(H):
                b = dve.bn_aggr(hmv[:, h, :], hstat[:, h, :])
            link(b)
            inverse_root(1 + tb, hr[:], hmv[:, :, 1], LN_EPS)
            link(dve.tensor_tensor(hh, hh, bcast(hmv[:, :, 0:1], [H, DH]), ALU.subtract))
            link(dve.tensor_tensor(hh, hh, bcast(hr[:].unsqueeze(2), [H, DH]), ALU.mult))
            link(dve.tensor_tensor(hh, hh, mhg[:].rearrange("p (h d) -> p h d", d=DH), ALU.mult))

        def m_gate(half):
            dve.wait_ge(evac[half], 7)
            for tb in range(TB):
                hh = HN[:, tb, 4 * half:4 * half + 4, 0:DH]
                og = OG[:, tb, half * W:(half + 1) * W].rearrange("p (h d) -> p h d", d=DH)
                a = dve.tensor_tensor(hh, hh, og, ALU.mult)
            link(a, S.m_y)

        run_slabs(dve, split_lo, S_IN, 14, plan(
            [(6 + j, 3, lambda j=j: (c_out, h_out, b_out)[j // 2](6 + j)) for j in range(6)],
            [(*slot(11), m_gates), (*slot(12), m_cumulate), (*slot(13), m_columns)],
            [(*slot(14 + h), lambda h=h: m_head(h)) for h in range(H)],
            [(11, 3, lambda: m_norm(0)), (12, 1, lambda: m_norm(1)), (13, 1, lambda: m_gate(0))]))
        split_lo(dve, S_OUT, 0)
        mix_lo(dve, 0, 0)
        split_lo(dve, S_OUT, 1)
        m_gate(1)
        mix_lo(dve, 0, 1)
        mix_lo(dve, 0, 2)
        mix_lo(dve, 0, 3)

        def res_add(scale):
            def f(s):
                slab_ready(dve, s)
                q = s - (S_OUT if s < S_OUT2 else S_OUT2)
                r = RES[:, :, q * W:(q + 1) * W]
                link(dve.scalar_tensor_tensor(r, r, scale, tm_out(s % 2), ALU.mult, ALU.add), evac[s % 2])
                dve.wait_ge(evac[s % 2], s // 2 + 1)
                for tb in range(TB):
                    a = row_stats(tb, q)
                if q == 3:
                    link(a)
            return f

        def bound_arg():
            link(dve.tensor_tensor(lbm[:], cols[:, 0, 32:40], cols[:, 0, 40:48], ALU.max))
            dve.tensor_tensor(lb0[:], cols[:, 0, 32:40], lbm[:], ALU.subtract)
            link(dve.tensor_tensor(lb1[:], cols[:, 0, 40:48], lbm[:], ALU.subtract), S.lb_arg)

        def bound():
            dve.wait_ge(S.lb_exp, 2)
            link(dve.tensor_tensor(lbs[:], lb0[:], lb1[:], ALU.add))
            link(dve.reciprocal(lbs[:], lbs[:]))
            link(dve.tensor_tensor(lb[:], lb0[:], lbs[:], ALU.mult))
            link(dve.tensor_scalar(omlb[:], lb[:], -1.0, 1.0, ALU.mult, ALU.add))

        run_slabs(dve, split_lo, S_OUT, 4, plan(each(res_add(ALPHA), S_OUT, 4), [(1, 1, bound_arg), (2, 1, bound)]))
        layer_norm(3, 64, S.tm_ready)
        x_lead(1, S_WQ)
        run_slabs(dve, split_lo, S_WQ, 4, {})

        dve.wait_ge(S.scores_cp, 8)
        link(dve.memset(SC[:, :, H, :, :], 0.0))

        def top16(vals, spare, dst, idx):
            link(dve.max(dst[:, 0:8], vals))
            dve.max_index(idx[:, 0:8], dst[:, 0:8], vals)
            link(dve.match_replace(spare, dst[:, 0:8], vals, LOWEST))
            link(dve.max(dst[:, 8:16], spare))
            link(dve.max_index(idx[:, 8:16], dst[:, 8:16], spare))

        def route(n, tb, h):
            src = SC[:, tb, ds(h, 1), :, :].rearrange("p o a k -> p (o a) k") if not isinstance(h, int) else SC[:, tb, h, :, :]
            link(dve.tensor_copy(sc[:], src))
            for a in range(2):
                top16(sc[:, a, :], sc2[:, a, :], best[:, a, :], bidx[:, a, :])
            link(dve.tensor_copy(bidf[:], bidx[:]))
            link(dve.tensor_tensor(cand[:], bcast(best[:, 0, :].unsqueeze(2), [TOPK, TOPK]),
                                   bcast(best[:, 1, :].unsqueeze(1), [TOPK, TOPK]), ALU.add))
            if not (isinstance(n, int) and n == 0):
                wait_alone(dve, S.soft_exp, n, S.dve_passed)
            c1, c2 = cand[:].rearrange("p a b -> p (a b)"), cand2[:].rearrange("p a b -> p (a b)")
            top16(c1, c2, tops[:], topj[:])
            dve.tensor_scalar(nmx[:], tops[:, 0:1], -1.0, None, ALU.mult).then_inc(S.soft_arg, 1)
            dve.tensor_scalar(tij[:, 0, :], topj[:], 4, None, ALU.logical_shift_right)
            link(dve.tensor_scalar(tij[:, 1, :], topj[:], 15, None, ALU.bitwise_and))
            link(dve.tensor_copy(tijf[:], tij[:]))
            for a in range(2):
                link(dve.tensor_tensor(hot[:, a, :, :], bcast(iota_f[:].unsqueeze(1), [TOPK, TOPK]),
                                       bcast(tijf[:, a, :].unsqueeze(2), [TOPK, TOPK]), ALU.is_equal))
                link(dve.tensor_tensor(hot[:, a, :, :], hot[:, a, :, :],
                                       bcast(bidf[:, a, :].unsqueeze(1), [TOPK, TOPK]), ALU.mult))
            link(dve.tensor_reduce(eids[:], hot[:], AX, ALU.add))
            link(dve.scalar_tensor_tensor(eidf[:], eids[:, 0, :], float(NKEY), eids[:, 1, :], ALU.mult, ALU.add))
            dve.tensor_copy(uidx[:, tb, :], eidf[:]).then_inc(S.uidx_ready, 1)
            dve.wait_ge(S.soft_exp, n + 1)
            link(dve.reciprocal(rsum[:], esum[:]))
            link(dve.tensor_scalar(gate[:, tb, :], eexp[:], rsum[:, 0:1], None, ALU.mult))

        def dot_rows(n, tb):
            dve.tensor_copy(vidx[:, tb, :], uidx[:, tb, :])
            for k in range(TOPK):
                dve.wait_ge(u_full[k % RING], (n * (TOPK // RING) + k // RING + 1) * 16)
                dve.tensor_tensor_reduce(ub[k % RING][:], ub[k % RING][:], RES[:, tb, :], 1.0, 0.0, ALU.mult,
                                         ALU.add, dots[:, tb, k:k + 1]).then_inc(S.dot_done, 1)
            dve.wait_ge(S.dot_done, (n + 1) * TOPK).then_inc(S.dots_ready, 1)

        def weights(n, tb):
            dve.wait_ge(S.gelu_ready, n + 1)
            dve.tensor_tensor(ew[:, tb, :], acts[:, tb, :], gate[:, tb, :], ALU.mult).then_inc(S.ew_ready, 1)

        def expert_step(n, tb, h_next):
            route(n + 1, 1 - tb, h_next)
            dot_rows(n, tb)
            weights(n, tb)

        route(0, 0, 0)
        expert_step(0, 0, 0)
        expert_step(1, 1, 1)
        with dve.Fori(1, H) as i:
            link.enter(i, 1, 50)
            for tb in range(TB):
                expert_step(i * 2 + tb, tb, i + tb)
        link.leave(1, H - 1)
        dve.wait_ge(S.v_done, 2 * H * TOPK)
        dve.wait_ge(S.acc_done, 1)
        for tb in range(TB):
            for b in range(4):
                r = RES[:, tb, b * W:(b + 1) * W]
                dve.scalar_tensor_tensor(r, r, ALPHA, PS[:, 4 * tb + b, :], ALU.mult, ALU.add).then_inc(S.ffsum, 1)
            dve.wait_ge(S.ffsum, 4 * tb + 4)
            for b in range(4):
                a = row_stats(tb, b)
        link(a)
        layer_norm(4, 96, S.ln2_done, True)
        rms_norm(5, NRM, 112, S.tm_ready)

        x_lead(2, S_IN2)
        dve.wait_ge(S.xt_lo, 24)
        dve.engine_nop().then_inc(S.nrm_used, 1)

        def wf_split():
            dve.wait_ge(S.wf_hi, 1)
            dve.tensor_tensor(wf_l[:], wf_raw[:], wf_h[:].bitcast(F32), ALU.subtract).then_inc(S.wf_lo, 1)

        def clear():
            dve.memset(GP2[:], 0.0)
            dve.memset(BP2[:], 0.0)
            dve.memset(RA2[:], 0.0)
            dve.memset(KE[:], 0.0)
            link(dve.memset(AT[:], 0.0))

        def f_fix(j):
            dve.wait_ge(evac[j], S_IN2 // 2 + 1)
            for h in range(4 * j, 4 * j + 4):
                a = dve.tensor_scalar(G_F[:, h, :], G_F[:, h, :], omlb[:, h:h + 1], lb[:, h:h + 1], ALU.mult, ALU.add)
            link(a, S.f_ready)

        def f_cumulate(j):
            dve.wait_ge(S.lnf_ready, j + 1)
            for h in range(4 * j, 4 * j + 4):
                a = dve.tensor_tensor_scan(G_B[:, h, :], smask[:], G_E[:, h, :], 0.0, ALU.mult, ALU.add)
            link(a, S.b_ready)

        def q_fix(j):
            hs = slice(4 * j, 4 * j + 4)
            bc = G_B[:, hs, :].rearrange("p h (c n) -> p (h c) n", n=CHUNK)
            ec = G_E[:, hs, :].rearrange("p h (c n) -> p (h c) n", n=CHUNK)
            last = bc[:, :, CHUNK - 1:CHUNK]
            dve.wait_ge(S.b_ready, j + 1)
            link(dve.tensor_tensor(ec, bcast(last, [4 * NCH, CHUNK]), bc, ALU.subtract), S.ke_arg)
            link(dve.tensor_scalar(G_F[:, hs, :], G_F[:, hs, :], -1.0, 1.0, ALU.mult, ALU.add))
            dve.wait_ge(evac[j], S_IN2 // 2 + 2)
            dve.wait_ge(S.expb_ready, j + 1)
            link(dve.tensor_tensor(G_Q[:, hs, :], G_Q[:, hs, :], G_K[:, hs, :], ALU.mult), S.q_decayed)

        def k_fix(j):
            hs = slice(4 * j, 4 * j + 4)
            dve.wait_ge(S.expe_ready, j + 1)
            link(dve.tensor_tensor(G_E[:, hs, :], G_E[:, hs, :], G_F[:, hs, :], ALU.mult))
            dve.wait_ge(S.expnb_ready, j + 1)
            link(dve.tensor_tensor(G_K[:, hs, :], G_K[:, hs, :], G_F[:, hs, :], ALU.mult), S.k_decayed)

        def a_gates():
            dve.wait_ge(S.gate_ps, 2)
            link(dve.tensor_tensor(glog[:, :, 0:H], PS[:, 6, 0:16].rearrange("p (b n) -> p b n", b=TB),
                                   bcast(fbias[:].unsqueeze(1), [TB, H]), ALU.add))
            dve.scalar_tensor_tensor(gabs[:, :, 0:H], glog[:, :, 0:H], -1.0, glog[:, :, 0:H], ALU.mult,
                                     ALU.max).then_inc(S.gate_abs, 1)
            dve.wait_ge(S.gate_ln, 2)
            dve.scalar_tensor_tensor(GP2[:, :, 0:H], glog[:, :, 0:H], 0.0, gln[:, :, 0:H], ALU.min,
                                     ALU.subtract).then_inc(S.gates_tm, 1)

        def a_cumulate():
            dve.wait_ge(S.gates_T, 2)
            link(dve.tensor_copy(LF2[0:H, :], PS[0:H, 7, 0:T]))
            link(dve.tensor_tensor_scan(BP2[0:H, :], ones[0:H, :], LF2[0:H, :], 0.0, ALU.mult, ALU.add))
            dve.tensor_scalar(RA2[0:H, :], BP2[0:H, :], -1.0, None, ALU.mult).then_inc(S.gates_cm, 1)

        def a_columns():
            dve.wait_ge(S.gates_back, 2)
            link(dve.tensor_copy(bcol[:], bt[:, :, 0:H]), S.c_ready)

        def g_step(n):
            if n >= 1:
                h = n - 1
                dve.wait_ge(S.g_ds, h + 1)
                dve.wait_ge(S.dcay_ready, 2)
                if h >= 1:
                    dve.wait_ge(S.g_o, h)
                link(dve.tensor_copy(ST[:, 0, :], PS[:, 6, 0:P]))
                for c in (1, 2):
                    link(dve.scalar_tensor_tensor(ST[:, c, :], ST[:, c - 1, :], dcay[:, h, c:c + 1],
                                                  PS[:, 6, c * P:c * P + P], ALU.mult, ALU.add))
                dve.engine_nop().then_inc(S.g_state, 1)
            if n < H:
                dve.wait_ge(S.g_keT, n + 1)
                for tb in range(TB):
                    a = dve.copy_predicated(AT[:, n % 2, tb, :], hmask[:].bitcast(I32), PS[:, 4, tb * P:tb * P + P])
                link(a, S.g_attn)

        def g_norm(tb):
            dve.wait_ge(S.g_ocp, H)
            hh = GO[:, :, tb, :]
            for h in range(H):
                b = dve.bn_stats(hstat[:, h, :], GO[:, h, tb, :])
            link(b)
            for h in range(H):
                b = dve.bn_aggr(hmv[:, h, :], hstat[:, h, :])
            link(b)
            link(dve.tensor_tensor(hr[:], hmv[:, :, 0], hmv[:, :, 0], ALU.mult))
            link(dve.tensor_tensor(hr[:], hr[:], hmv[:, :, 1], ALU.add))
            inverse_root(6 + tb, hr[:], hr[:], RMS_EPS)
            link(dve.tensor_tensor(hh, hh, bcast(hr[:].unsqueeze(2), [H, DH]), ALU.mult))
            link(dve.tensor_tensor(hh, hh, bcast(hgain[:].unsqueeze(1), [H, DH]), ALU.mult))

        def g_gate(half):
            dve.wait_ge(evac[half], S_OUT2 // 2)
            for tb in range(TB):
                hh = GO[:, 4 * half:4 * half + 4, tb, :]
                gg = G_G[:, tb, half * W:(half + 1) * W].rearrange("p (h d) -> p h d", d=DH)
                a = dve.tensor_tensor(hh, hh, gg, ALU.mult)
            link(a, S.g_y)

        def a_step(n):
            if n < H:
                h, e = n, n % 2
                dve.wait_ge(S.a_scores, h + 1)
                if h >= 2:
                    dve.wait_ge(S.a_pT, h - 1)
                for a, tb in ((0, 0), (P, 1), (2 * P, 1)):
                    b = dve.scalar_tensor_tensor(E2[:, e, a:a + P], PS[:, 4, a:a + P], bcol[:, tb, h:h + 1],
                                                 maskneg[:, a:a + P], ALU.add, ALU.add)
                link(b)
                dve.tensor_reduce(nmax[:, e, 0:1], E2[:, e, 0:P], AX, ALU.max, negate=True)
                link(dve.tensor_reduce(nmax[:, e, 1:2], E2[:, e, P:384], AX, ALU.max, negate=True), S.a_max)
            if 1 <= n <= H:
                e = (n - 1) % 2
                dve.wait_ge(S.a_exp, n)
                link(dve.reciprocal(psum_[:, e, :], psum_[:, e, :]))
                dve.tensor_scalar(E2[:, e, 0:P], E2[:, e, 0:P], psum_[:, e, 0:1], None, ALU.mult)
                link(dve.tensor_scalar(E2[:, e, P:384], E2[:, e, P:384], psum_[:, e, 1:2], None, ALU.mult), S.a_prob)
            if n >= 3:
                dve.wait_ge(S.a_out, n - 2)
                dve.tensor_copy(MIX[:, n - 3, :], PS[:, 6, 0:T]).then_inc(S.mix_a, 1)

        run_slabs(dve, split_lo, S_IN2, 14, plan(
            [(0, 1, wf_split), (0, 2, clear)],
            [(j, 3, lambda j=j: f_fix(j)) for j in range(2)],
            [(1 + j, 1, lambda j=j: f_cumulate(j)) for j in range(2)],
            [(2 + j, 3, lambda j=j: q_fix(j)) for j in range(2)],
            [(3 + j, 1, lambda j=j: k_fix(j)) for j in range(2)],
            [(*slot(GATES2), a_gates), (*slot(GATES2 + 1), a_cumulate), (*slot(GATES2 + 2), a_columns)],
            [(*slot(HEADS2 + n), lambda n=n: g_step(n)) for n in range(H + 1)],
            [(10, 2, lambda: g_norm(0)), (10, 3, lambda: g_norm(1))],
            [(*divmod(ATTN + n, UNITS), lambda n=n: a_step(n)) for n in range(H + 3)],
            [(13, 1, lambda: g_gate(0))]))
        split_lo(dve, S_OUT2, 0)
        mix_lo(dve, 1, 0)
        split_lo(dve, S_OUT2, 1)
        g_gate(1)
        mix_lo(dve, 1, 1)
        mix_lo(dve, 1, 2)
        mix_lo(dve, 1, 3)
        run_slabs(dve, split_lo, S_OUT2, 4, plan(each(res_add(1.0), S_OUT2, 4)))
        rms_norm(8, NRM, 128, S.tm_ready)
        x_lead(3, S_FF)

        def col(a, n, t):
            return cols[:, a[0], ds(n * 4 + (t + a[1]), 1)] if not isinstance(n, int) else \
                cols[:, a[0], 4 * n + t + a[1]:4 * n + t + a[1] + 1]

        def gate_taps(n):
            dve.wait_ge(S.ff_y, n + 1)
            for back, place in ((1, (1, FC)), (2, (1, 0))):
                for t in range(4):
                    a = dve.scalar_tensor_tensor(FY[:, t, back:], cm_out(0)[:, t, 0:T - back], col(place, n, t),
                                                 FY[:, t, back:], ALU.mult, ALU.add)
                link(a)
            dve.engine_nop().then_inc(S.ff_conv, 1)
            dve.engine_nop().then_inc(evac[0], 1)

        def up_out(n, s):
            slab_ready(dve, s)
            dve.wait_ge(S.ff_silu, n + 1)
            dst = FA[:, ds(n * 4, 4), :] if not isinstance(n, int) else FA[:, 4 * n:4 * n + 4, :]
            link(dve.tensor_tensor(dst, FY[:], cm_out(1), ALU.mult), evac[1], S.ff_up)

        def ff_pair(n, s, first=False):
            if not first:
                split_lo(dve, s, 0)
                split_lo(dve, s, 1)
                up_out(n - 1, s - 1)
            split_lo(dve, s, 2)
            split_lo(dve, s, 3)
            split_lo(dve, s + 1, 0)
            split_lo(dve, s + 1, 1)
            gate_taps(n)
            split_lo(dve, s + 1, 2)
            split_lo(dve, s + 1, 3)

        ff_pair(0, S_FF, True)
        with dve.Fori(1, FPAIRS) as i:
            link.enter(i, 1, 3)
            ff_pair(i, i * 2 + S_FF)
        link.leave(1, FPAIRS - 1)
        up_out(FPAIRS - 1, S_FF + 2 * FPAIRS - 1)

        def down_lo(j, s):
            for u in range(UNITS):
                split_lo(dve, s, u)
                dve.wait_ge(S.ah_full, j * UNITS + u + 1)
                dve.tensor_tensor(al[u % 2][:], FA[:, ds(j * UNITS + u, 1), :].rearrange("p o n -> p (o n)")
                                  if not isinstance(j, int) else FA[:, j * UNITS + u, :],
                                  ah[u % 2][:].bitcast(F32), ALU.subtract).then_inc(S.al_full, 1)

        down_lo(0, S_DOWN)
        with dve.Fori(1, NDOWN) as i:
            down_lo(i, i + S_DOWN)
        slab_ready(dve, S_DOWN + NDOWN - 1)
        dve.wait_ge(S.down_done, 1)
        for tb in range(TB):
            for b in range(4):
                r = RES[:, tb, b * W:(b + 1) * W]
                a = dve.tensor_tensor(r, r, PS[:, 4 * tb + b, :], ALU.add)
            link(a)
            for b in range(4):
                a = row_stats(tb, b)
        link(a)
        rms_norm(9, RES, 144, S.final)

    @block.tensor
    def _(pe):
        pe.wait_ge(S.ident_ready, 1)
        pe.wait_ge(S.stage_in, 7 * 16)
        for a in range(3):
            m = pe.transpose(PS[:, 3, a * P:a * P + P], stage[:, a, :], ident[:])
        m.then_inc(S.cols_ps, 1)
        turn_x(pe, 0, RES)

        def gate_logits(width, h, l, ready):
            pe.wait_ge(ready, 1)
            for tb in range(TB):
                y = slice(tb * P, tb * P + P)
                o = PS[:, 6, tb * width:(tb + 1) * width]
                for d in range(DC):
                    pe.matmul(o, XH[:, d, y], h[:, d, :], start=d == 0, stop=False)
                    pe.matmul(o, XH[:, d, y], l[:, d, :], start=False, stop=False)
                    m = pe.matmul(o, XL[:, d, y], h[:, d, :], start=False, stop=d == DC - 1)
            m.then_inc(S.gate_ps, 1)

        def gates_turn(n, src):
            pe.wait_ge(S.gates_tm, n + 1)
            for tb in range(TB):
                m = pe.transpose(PS[:, 7, tb * P:tb * P + P], src[:, tb, :], ident[:])
            m.then_inc(S.gates_T, 1)

        def gates_return(n, src):
            pe.wait_ge(S.gates_cm, n + 1)
            for tb in range(TB):
                m = pe.transpose(PS[:, 6, tb * P:tb * P + P], src[:, tb * P:tb * P + P], ident[:])
            m.then_inc(S.gates_back, 1)

        def m_head(h):
            if h >= 1:
                pe.wait_ge(S.m_prob, h)
            if h < H:
                if h == 0:
                    pe.wait_ge(evac[0], 3)
                    pe.wait_ge(evac[1], 3)
                pe.matmul(PS[:, 4, 0:T], KT[:, h, 0:P], QT[:, h, :], start=True, stop=True)
                pe.matmul(PS[:, 4, T:384], KT[:, h, P:T], QT[:, h, P:T], start=True, stop=True)
                pe.matmul(PS[:, 5, 0:T], bcast(ident[:, h:h + 1], [P]), RA1[:], start=True,
                          stop=True).then_inc(S.m_scores, 1)
            if h >= 1:
                g = h - 1
                if g >= 1:
                    pe.wait_ge(S.m_numcp, g)
                o = PS[:, 7, 0:TB * (DH + 1)].rearrange("p (b d) -> p b d", b=TB)
                pe.matmul(o[:, 0, :], PM1[:, 0:P], VX[:, 0, g, 0:DH + 1], start=True, stop=True)
                pe.matmul(o[:, 1, :], PM1[:, P:T], VX[:, 0, g, 0:DH + 1], start=True, stop=False)
                pe.matmul(o[:, 1, :], PM1[:, T:384], VX[:, 1, g, 0:DH + 1], start=False,
                          stop=True).then_inc(S.m_num, 1)

        def turn_heads(half, src, y, turned, mix):
            pe.wait_ge(y, half + 1)
            if half == 1:
                pe.wait_ge(S.mix_y, mix + 1)
            for tb in range(TB):
                for k in range(4):
                    m = pe.transpose(PS[:, 6 + tb, k * P:k * P + P], src(tb, 4 * half + k), ident[:])
            m.then_inc(turned, 1)

        def m_turn(half):
            pe.wait_ge(S.m_numcp, H)
            turn_heads(half, lambda tb, h: HN[:, tb, h, 0:DH], S.m_y, S.m_turn, 0)

        def g_turn(half):
            pe.wait_ge(S.mix_a, H)
            turn_heads(half, lambda tb, h: GO[:, h, tb, :], S.g_y, S.g_turn, 2)

        def turn_keys():
            pe.wait_ge(S.keys_in, 16 * 2 * H)
            pe.wait_ge(S.mix_y, 2)
            for n in range(4):
                for k in range(4):
                    m = pe.transpose(PS[:, 4 + n, k * P:k * P + P], KR[:, 4 * n + k, :], ident[:])
                m.then_inc(S.keyT_ps, 1)

        m_events = plan(
            [(*slot(11), lambda: gate_logits(16, wg_h, wg_l, S.wg_lo)), (*slot(12), lambda: gates_turn(0, GP1)),
             (*slot(13), lambda: gates_return(0, BP1))],
            [(*slot(14 + h), lambda h=h: m_head(h)) for h in range(H + 1)],
            [(13, 2, lambda: m_turn(0))])
        for s in range(S_IN, S_OUT):
            if s == 1:
                pe.wait_ge(S.cols_ready, 1)
            pe_slab(pe, s // 2, s % 2, s not in (4, 5, 12, 13), m_events, s, (S.xt_lo, 5) if s == 0 else None)
        out_events = plan([(0, 0, lambda: m_turn(1)), (3, 2, turn_keys)])
        for s in range(S_OUT, S_OUT + 4):
            pe_slab(pe, s // 2, s % 2, False, out_events, s - S_OUT, (S.mix_lo, 1) if s == S_OUT else None)

        pe.wait_ge(S.keyT, 4)
        turn_x(pe, 1, RES)
        for s in range(S_WQ, S_WQ + 4):
            pe_slab(pe, s // 2, s % 2, True, x_in=(S.xt_lo, 13) if s == S_WQ else None)
        pe.wait_ge(evac[0], (S_WQ + 4) // 2)
        pe.wait_ge(evac[1], (S_WQ + 4) // 2)
        for n in range(8):
            if n >= 4:
                pe.wait_ge(S.scores_cp, n - 3)
            tb, q = n // 4, n % 4
            for k in range(4):
                m = pe.matmul(PS[:, 4 + n % 4, k * P:k * P + P], PQ[:, 4 * q + k, tb * P:tb * P + P],
                              KX[:, 4 * q + k, :], start=True, stop=True)
            m.then_inc(S.score_ps, 1)
        pe.wait_ge(S.scores_cp, 8)

        def v_rows(n, tb, start=False):
            for k in range(TOPK):
                pe.wait_ge(v_full[k % RING], (n * (TOPK // RING) + k // RING + 1) * 16)
                pe.wait_ge(S.diag_ready, n * TOPK + k + 1)
                for b in range(4):
                    m = pe.matmul(PS[:, 4 * tb + b, :], diag[:, k, :], vb[k % RING][:, b * W:(b + 1) * W],
                                  start=start and k == 0, stop=False, skip_group_check=True)
                m.then_inc(S.v_done, 1)

        v_rows(0, 0, True)
        v_rows(1, 1, True)
        with pe.Fori(1, H) as i:
            for tb in range(TB):
                v_rows(i * 2 + tb, tb)
        pe.wait_ge(S.v_done, 2 * H * TOPK)
        pe.nop().then_inc(S.acc_done, 1)

        pe.wait_ge(S.ffsum, 8)
        turn_x(pe, 2, NRM)
        def g_step(n):
            if 1 <= n <= H:
                h = n - 1
                pe.wait_ge(S.g_ke, h + 1)
                if h == 0:
                    pe.wait_ge(S.c_ready, 1)
                    pe.wait_ge(evac[0], S_IN2 // 2 + 3)
                    pe.wait_ge(evac[1], S_IN2 // 2 + 3)
                else:
                    pe.wait_ge(S.g_state, h)
                for c in range(NCH - 1):
                    m = pe.matmul(PS[:, 6, c * P:c * P + P], KE[:, c, :],
                                  G_V[:, c // 2, h * DH:(h + 1) * DH], start=True, stop=True)
                m.then_inc(S.g_ds, 1)
            if n >= 2:
                g = n - 2
                pe.wait_ge(S.g_attn, g + 1)
                pe.wait_ge(S.g_state, g + 1)
                if g >= 1:
                    pe.wait_ge(S.g_ocp, g)
                for tb in range(TB):
                    o = PS[:, 7, tb * P:tb * P + P]
                    pe.matmul(o, AT[:, g % 2, tb, :], G_V[:, tb, g * DH:(g + 1) * DH], start=True, stop=True,
                              skip_group_check=True)
                    for c in range(2 * tb, 2 * tb + 2):
                        if c == 0:
                            continue
                        r = slice((c % 2) * CHUNK, (c % 2) * CHUNK + CHUNK)
                        m = pe.matmul(o[r, :], G_Q[:, g, c * CHUNK:(c + 1) * CHUNK], ST[:, c - 1, :],
                                      start=False, stop=True, skip_group_check=True)
                m.then_inc(S.g_o, 1)
            if n < H:
                if n == 0:
                    pe.wait_ge(S.k_decayed, 2)
                else:
                    pe.wait_ge(S.g_attn, n)
                    pe.wait_ge(S.g_ke, n)
                for tb in range(TB):
                    y = slice(tb * P, tb * P + P)
                    pe.matmul(PS[:, 4, y], G_K[:, n, y], G_Q[:, n, y], start=True, stop=True)
                for tb in range(TB):
                    y = slice(tb * P, tb * P + P)
                    m = pe.transpose(PS[:, 5, y], G_E[:, n, y], ident[:])
                m.then_inc(S.g_keT, 1)

        def a_step(n):
            if 2 <= n < H + 2:
                g = n - 2
                pe.wait_ge(S.a_prob, g + 1)
                if g >= 1:
                    pe.wait_ge(S.a_pTcp, g)
                for k in range(3):
                    m = pe.transpose(PS[:, 5, k * P:k * P + P], E2[:, g % 2, k * P:k * P + P], ident[:])
                m.then_inc(S.a_pT, 1)
            if n < H:
                if n == 0:
                    pe.wait_ge(evac[0], S_IN2 // 2 + 5)
                    pe.wait_ge(evac[1], S_IN2 // 2 + 5)
                else:
                    pe.wait_ge(S.a_max, n)
                for tb, (a, b) in enumerate(((0, P), (P, 384))):
                    y = slice(tb * P, tb * P + P)
                    pe.matmul(PS[:, 4, a:b], FQ[:, n, y], FK[:, n, 0:b - a], start=True, stop=False)
                    m = pe.matmul(PS[:, 4, a:b], bcast(ident[:, n:n + 1], [P]), RA2[:, 0:b - a], start=False, stop=True)
                m.then_inc(S.a_scores, 1)
            if n >= 3:
                g = n - 3
                e = g % 2
                pe.wait_ge(S.a_pTcp, g + 1)
                pe.wait_ge(evac[g // 4], S_IN2 // 2 + 6)
                if g >= 1:
                    pe.wait_ge(S.mix_a, g)
                v = slice(g * DH, (g + 1) * DH)
                pe.matmul(PS[:, 6, 0:T], FV[:, 0, v], PM2[:, e, 0:T], start=True, stop=True)
                pe.matmul(PS[:, 6, P:T], FV[:, 1, v], PM2[:, e, T:384], start=False, stop=True,
                          skip_group_check=True).then_inc(S.a_out, 1)

        in2_events = plan(
            [(*slot(GATES2), lambda: gate_logits(H, wf_h, wf_l, S.wf_lo)),
             (*slot(GATES2 + 1), lambda: gates_turn(1, GP2)), (*slot(GATES2 + 2), lambda: gates_return(1, BP2))],
            [(*slot(HEADS2 + n), lambda n=n: g_step(n)) for n in range(H + 2)],
            [(*divmod(ATTN + n, UNITS), lambda n=n: a_step(n)) for n in range(H + 3)],
            [(13, 2, lambda: g_turn(0))])
        for s in range(S_IN2, S_OUT2):
            n = s - S_IN2
            pe_slab(pe, s // 2, s % 2, n not in (4, 5, 10, 11, 12, 13), in2_events, n,
                    (S.xt_lo, 21) if n == 0 else None)
        for s in range(S_OUT2, S_OUT2 + 4):
            pe_slab(pe, s // 2, s % 2, False, plan([(0, 0, lambda: g_turn(1))]), s - S_OUT2,
                    (S.mix_lo, 5) if s == S_OUT2 else None)

        pe.wait_ge(S.mix_y, 4)
        turn_x(pe, 3, NRM)
        pe_slab(pe, S_FF // 2, 0, True, x_in=(S.xt_lo, 29))
        pe_slab(pe, S_FF // 2, 1, True)
        with pe.Fori(1, FPAIRS) as i:
            for k in range(2):
                pe_slab(pe, i + S_FF // 2, k, True)

        def down(j, s, first=False):
            for u in range(UNITS):
                k = u % 2
                pe.wait_ge(lo_full[k], s * 2 + u // 2 + 1)
                pe.wait_ge(S.al_full, j * UNITS + u + 1)
                for tb in range(TB):
                    y = slice(tb * P, tb * P + P)
                    for b in range(4):
                        o = PS[:, 4 * tb + b, :]
                        for n, (x, w) in enumerate(((ah, wh), (ah, wl), (al, wh))):
                            m = pe.matmul(o, x[k][:, y], w[k][:, b, :], start=first and u == 0 and n == 0,
                                          stop=False, skip_group_check=True)
                m.then_inc(w_free[k], 1)

        pe.wait_ge(evac[0], S_DOWN // 2)
        pe.wait_ge(evac[1], S_DOWN // 2)
        down(0, S_DOWN, True)
        with pe.Fori(1, NDOWN) as i:
            down(i, i + S_DOWN)
        pe.wait_ge(w_free[1], 2 * (S_DOWN + NDOWN))
        pe.nop().then_inc(S.down_done, 1)


_INS = ["x", "ln_in_g", "ln_in_b", "w_in", "b_gate", "conv_w", "conv_b", "mh_norm_g", "w_out", "ln1_g", "ln1_b",
        "peer_wq", "peer_keys", "peer_u", "peer_v", "ln2_g", "ln2_b", "norm1_gain_2", "w_in_2", "hgrn_lb_param_2",
        "hgrn_norm_gain_2", "fox_gate_bias_2", "w_out_2", "norm2_gain_2", "w_ffn_gate_2", "w_ffn_up_2",
        "ffn_conv_w_2", "ffn_conv_b_2", "w_ffn_down_2", "final_norm_gain_2"]


def kernel(**inputs):
    import concourse.bacc as bacc
    import numpy as np
    from concourse.bass_utils import run_bass_kernel_spmd

    nc = bacc.Bacc("TRN2", target_bir_lowering=False, num_devices=1)
    arrays, aps = {}, {}
    for name in _INS:
        a = np.ascontiguousarray(inputs[name])
        arrays[f"in_{name}"] = a
        aps[name] = nc.dram_tensor(f"in_{name}", a.shape, mybir.dt.from_np(a.dtype), kind="ExternalInput").ap()
    out = nc.dram_tensor("out_y", (1, T, D), F32, kind="ExternalOutput").ap()
    block_kernel(nc, aps, out)
    r = run_bass_kernel_spmd(nc, [arrays], core_ids=[0])
    return r.results[0]["out_y"]
```

```python
from contextlib import ExitStack

import concourse.bass as bass
from concourse import mybir

F32 = mybir.dt.float32
F32R = mybir.dt.float32r
I32 = mybir.dt.int32
U32 = mybir.dt.uint32
ALU = mybir.AluOpType
ACT = mybir.ActivationFunctionType
AX = mybir.AxisListType.X
ds = bass.ds

P = 128
T = 256
TB = T // P
D = 2048
DC = D // P
W = 512
UC = 4
UNITS = DC // UC
H = 8
DH = 128
HW = H * DH
CHUNK = 64
NCH = T // CHUNK
FF = 5632
FC = FF // P
FPAIRS = FF // W
NEXP = 16384
NKEY = 128
TOPK = 16
ALPHA = 2.0 ** 0.25
LN_EPS = 1e-5
RMS_EPS = 1e-6
LOWEST = -3.0e38
SCALE = float(DH) ** -0.5
RING = 4
EARLY = 8
LAST = 2 * H - 1
DVE_ROWS = (5, 7, 9, 11, 14, 15)
PE_ROWS = tuple(k for k in range(TOPK) if k not in DVE_ROWS)

S_IN, S_OUT, S_WQ, S_IN2, S_OUT2, S_FF, S_DOWN = 0, 14, 18, 22, 36, 40, 62
NDOWN = FC // UC
GATES2, HEADS2, ATTN = 7, 11, 43
GATES1, HEADS1 = 3, 24


def wait_alone(eng, sem, value, passed):
    eng.wait_ge(sem, value).then_inc(passed, 1)


class Chain:

    def __init__(self, eng, sem, passed):
        self.eng, self.sem, self.passed, self.n, self.reg, self.per = eng, sem, passed, 0, None, 0

    def __call__(self, instruction, *signals):
        self.n += 1
        instruction.then_inc(self.sem, 1)
        value = self.n if self.reg is None else self.reg * self.per + self.n
        for s in signals:
            self.eng.wait_ge(self.sem, value).then_inc(s, 1)
        if not signals and self.reg is None:
            self.eng.wait_ge(self.sem, value)
        elif not signals:
            wait_alone(self.eng, self.sem, value, self.passed)

    def enter(self, reg, first, per):
        self.reg, self.per, self.at = reg, per, self.n
        self.n -= first * per

    def leave(self, first, trips):
        made = self.n + first * self.per - self.at
        assert made == self.per, f"the loop's body makes {made} links"
        self.n = self.at + trips * self.per
        self.reg = None


def block_kernel(nc, inp, out):
    ctx = ExitStack()
    with ctx:
        build(nc, inp, out, ctx)


def build(nc, inp, out, ctx):
    def sem(name):
        return ctx.enter_context(nc.semaphore(name))

    class S:

        gain_in = sem("gain_in")
        norm_in = sem("norm_in")
        stage_clear = sem("stage_clear")
        stage_in = sem("stage_in")
        small_in = sem("small_in")
        wf_in = sem("wf_in")
        keys_in = sem("keys_in")
        stored = sem("stored")
        ident_ready = sem("ident_ready")
        consts = sem("consts")
        pool_chain = sem("pool_chain")
        pool_passed = sem("pool_passed")
        act_chain = sem("act_chain")
        act_passed = sem("act_passed")
        dve_chain = sem("dve_chain")
        dve_passed = sem("dve_passed")
        square_ready = sem("square_ready")
        root_ready = sem("root_ready")
        tm_ready = sem("tm_ready")
        xt_ps = sem("xt_ps")
        xt_hi = sem("xt_hi")
        xt_lo = sem("xt_lo")
        cols_ps = sem("cols_ps")
        cols_ready = sem("cols_ready")
        mix_y = sem("mix_y")
        mix_a = sem("mix_a")
        mix_hi = sem("mix_hi")
        mix_lo = sem("mix_lo")
        conv_done = sem("conv_done")
        wg_hi = sem("wg_hi")
        wg_lo = sem("wg_lo")
        wf_hi = sem("wf_hi")
        wf_lo = sem("wf_lo")
        gate_ps = sem("gate_ps")
        gate_abs = sem("gate_abs")
        gate_ln = sem("gate_ln")
        gates_ready = sem("gates_ready")
        gates_low = sem("gates_low")
        gates_cm = sem("gates_cm")
        gates_back = sem("gates_back")
        em_arg = sem("em_arg")
        em_ready = sem("em_ready")
        m_scores = sem("m_scores")
        m_arg = sem("m_arg")
        m_exp = sem("m_exp")
        m_prob = sem("m_prob")
        m_num = sem("m_num")
        m_numcp = sem("m_numcp")
        m_y = sem("m_y")
        m_turn = sem("m_turn")
        keyT_ps = sem("keyT_ps")
        keyT = sem("keyT")
        score_ps = sem("score_ps")
        scores_cp = sem("scores_cp")
        soft_arg = sem("soft_arg")
        soft_exp = sem("soft_exp")
        uidx_ready = sem("uidx_ready")
        dot_done = sem("dot_done")
        dots_ready = sem("dots_ready")
        gelu_ready = sem("gelu_ready")
        ew_ready = sem("ew_ready")
        diag_ready = sem("diag_ready")
        v_done = sem("v_done")
        acc_done = sem("acc_done")
        ffsum = sem("ffsum")
        v_added = sem("v_added")
        nrm_used = sem("nrm_used")
        lb_arg = sem("lb_arg")
        lb_exp = sem("lb_exp")
        f_ready = sem("f_ready")
        lnf_ready = sem("lnf_ready")
        b_ready = sem("b_ready")
        expb_ready = sem("expb_ready")
        dcay_ready = sem("dcay_ready")
        ke_arg = sem("ke_arg")
        expe_ready = sem("expe_ready")
        q_decayed = sem("q_decayed")
        expnb_ready = sem("expnb_ready")
        k_decayed = sem("k_decayed")
        c_ready = sem("c_ready")
        g_keT = sem("g_keT")
        g_ke = sem("g_ke")
        g_attn = sem("g_attn")
        g_ds = sem("g_ds")
        g_state = sem("g_state")
        g_o = sem("g_o")
        g_ocp = sem("g_ocp")
        g_y = sem("g_y")
        g_turn = sem("g_turn")
        a_scores = sem("a_scores")
        a_max = sem("a_max")
        a_exp = sem("a_exp")
        a_prob = sem("a_prob")
        a_pT = sem("a_pT")
        a_pTcp = sem("a_pTcp")
        a_out = sem("a_out")
        ff_y = sem("ff_y")
        ff_conv = sem("ff_conv")
        ff_silu = sem("ff_silu")
        ff_up = sem("ff_up")
        ah_full = sem("ah_full")
        al_full = sem("al_full")
        down_done = sem("down_done")
        summed = sem("summed")
        squares = sem("squares")
        final = sem("final")

    base = (nc.sbuf_base + 63) // 64 * 64
    total = nc.sbuf_usable_end - base
    ctx.enter_context(nc.sbuf_tensor("arena", [P, total // 4 - 32], F32))
    K = 1024

    def at(name, kb, shape, dt=F32):
        return nc.alloc_sbuf_tensor_at(name, [P, *shape], dt, offset=base + int(kb * K))

    raw = [at(f"raw{k}", 8 * k, [UC, W]) for k in range(UNITS)]
    wh = [at(f"wh{k}", 32 + 8 * k, [UC, W], F32R) for k in range(2)]
    wl = [at(f"wl{k}", 48 + 8 * k, [UC, W], F32R) for k in range(2)]
    XH = at("XH", 64, [DC, T], F32R)
    XL = at("XL", 80, [DC, T], F32R)
    RES = at("RES", 96, [TB, D])
    MIX = at("MIX", 112, [DC, T])
    GAIN = at("GAIN", 112, [D])
    BIAS = at("BIAS", 120, [D])
    ident = at("ident", 128, [P])
    mask01 = at("mask01", 128.5, [384])
    maskneg = at("maskneg", 130, [384])
    hmask = at("hmask", 131.5, [P])
    smask = at("smask", 132, [T])
    ones = at("ones", 133, [T])
    iota_i = at("iota_i", 134, [TOPK], I32)
    iota_f = at("iota_f", 134.125, [TOPK])
    stage = at("stage", 134.25, [3, P])
    cols = at("cols", 135.75, [3, P])
    SM = 137.25
    bgate = at("bgate", SM, [1])
    fbias = at("fbias", SM + 0.0625, [1])
    hgain = at("hgain", SM + 0.125, [DH])
    mv = at("mv", SM + 0.75, [TB, 2])
    rstd = at("rstd", SM + 0.8125, [TB])
    msq = at("msq", SM + 0.84375, [TB])
    lb0 = at("lb0", SM + 1.25, [H])
    lb1 = at("lb1", SM + 1.28125, [H])
    lbm = at("lbm", SM + 1.3125, [H])
    lbs = at("lbs", SM + 1.34375, [H])
    lb = at("lb", SM + 1.375, [H])
    omlb = at("omlb", SM + 1.40625, [H])
    dcay = at("dcay", SM + 1.4375, [H, NCH])
    PH = 139
    ZC = at("ZC", PH, [H, T + 2])
    QT = at("QT", PH + 8.25, [H, T])
    KT = at("KT", PH + 16.25, [H, T])
    VX = at("VX", PH + 24.25, [TB, H, DH + 2])
    OG = at("OG", PH + 32.5, [TB, HW])
    mhg = at("mhg", PH + 40.5, [HW])
    wg_raw = at("wg_raw", PH + 44.5, [DC, 16])
    wg_h = at("wg_h", PH + 45.5, [DC, 16], F32R)
    wg_l = at("wg_l", PH + 46.5, [DC, 16], F32R)
    HN = at("HN", PH + 47.5, [TB, H, DH + 2])
    E1 = at("E1", PH + 55.75, [384])
    PM1 = at("PM1", PH + 57.25, [384])
    LG1 = at("LG1", PH + 58.75, [T])
    BP1 = at("BP1", PH + 59.75, [T])
    RA1 = at("RA1", PH + 60.75, [T])
    LS1 = at("LS1", PH + 61.75, [T])
    LA1 = at("LA1", PH + 62.75, [T])
    FS = at("FS", PH + 63.75, [T])
    CM = at("CM", PH + 64.75, [T])
    HS = PH + 66.5
    bcol = at("bcol", HS, [TB, H])
    emcol = at("emcol", HS + 0.0625, [TB, H])
    den = at("den", HS + 0.125, [TB, H])
    hstat = at("hstat", HS + 0.25, [H, 6])
    hmv = at("hmv", HS + 0.5, [H, 2])
    hr = at("hr", HS + 0.625, [H])
    nmax = at("nmax", HS + 0.75, [2, TB])
    psum_ = at("psum_", HS + 0.8125, [2, TB])
    stats = at("stats", HS + 0.875, [TB, 4, 6])
    G_F = at("G_F", PH, [H, T])
    G_B = at("G_B", PH + 8, [H, T])
    G_Q = at("G_Q", PH + 16, [H, T])
    GO = at("GO", PH + 16, [H, TB, DH])
    G_E = at("G_E", PH + 24, [H, T])
    G_K = at("G_K", PH + 32, [H, T])
    G_V = at("G_V", PH + 40, [TB, HW])
    G_G = at("G_G", PH + 48, [TB, HW])
    FQ = at("FQ", PH, [H, T])
    FK = at("FK", PH + 8, [H, T])
    FV = at("FV", PH + 56, [TB, HW])
    wf_raw = at("wf_raw", PH + 64, [DC, H])
    wf_h = at("wf_h", PH + 64.5, [DC, H], F32R)
    wf_l = at("wf_l", PH + 65, [DC, H], F32R)
    RA2 = at("RA2", PH + 65.5, [T])
    LG2 = at("LG2", PH + 48, [T])
    BP2 = at("BP2", PH + 49, [T])
    LS2 = at("LS2", PH + 50, [T])
    LA2 = at("LA2", PH + 53, [T])
    AT = at("AT", PH + 51, [2, TB, P])
    ST = at("ST", PH + 53, [3, P])
    KE = at("KE", PH + 54.5, [NCH - 1, DH])
    E2 = at("E2", PH + 24, [2, 384])
    PM2 = at("PM2", PH + 27, [2, 384])
    PQ = at("PQ", 112, [DC, T])
    KR = at("KR", PH, [DC, P])
    KX = at("KX", PH + 50.5, [DC, P])
    SC = at("SC", PH + 32, [TB, H, 2, NKEY])
    TK = PH + 58.5
    sc = at("sc", TK, [2, NKEY])
    sc2 = at("sc2", TK + 1, [2, NKEY])
    best = at("best", TK + 2, [2, TOPK])
    bidx = at("bidx", TK + 2.125, [2, TOPK], U32)
    bidf = at("bidf", TK + 2.25, [2, TOPK])
    tops = at("tops", TK + 2.375, [TOPK])
    topj = at("topj", TK + 2.4375, [TOPK], U32)
    tij = at("tij", TK + 2.5, [2, TOPK], U32)
    tijf = at("tijf", TK + 2.625, [2, TOPK])
    eids = at("eids", TK + 2.75, [2, TOPK])
    eidf = at("eidf", TK + 2.875, [TOPK])
    nmx = at("nmx", TK + 2.9375, [1])
    esum = at("esum", TK + 2.96875, [1])
    rsum = at("rsum", TK + 3, [1])
    eexp = at("eexp", TK + 3.0625, [TOPK])
    gate = at("gate", TK + 3.125, [2, TOPK])
    uidx = at("uidx", TK + 3.25, [2, TOPK], U32)
    vidx = at("vidx", TK + 3.375, [2, TOPK], U32)
    dots = at("dots", TK + 3.5, [2, TOPK])
    acts = at("acts", TK + 3.625, [2, TOPK])
    ew = at("ew", TK + 3.75, [2, TOPK])
    cand = at("cand", TK + 4, [TOPK, TOPK])
    cand2 = at("cand2", TK + 5, [TOPK, TOPK])
    hot = at("hot", TK + 6, [2, TOPK, TOPK])
    diag = at("diag", PH + 50.5, [TOPK, P])
    GAIN3 = at("GAIN3", 56, [D])
    ub = [at(f"ub{k}", PH + 8 * k, [D]) for k in range(RING)]
    vb = [at(f"vb{k}", 64 + 8 * k, [D]) for k in range(RING)]
    NRM = at("NRM", PH + 32, [TB, D])
    FA = at("FA", PH, [FC, T])
    FY = at("FY", PH + 44, [4, T])
    ah = [at(f"ah{k}", PH + 48 + k, [T], F32R) for k in range(2)]
    al = [at(f"al{k}", PH + 50 + k, [T], F32R) for k in range(2)]

    PS = ctx.enter_context(nc.psum_tensor("PS", [P, 8, 512], F32))

    raw_full = [sem(f"raw_full{k}") for k in range(UNITS)]
    hi_full = [sem(f"hi_full{k}") for k in range(2)]
    lo_full = [sem(f"lo_full{k}") for k in range(2)]
    w_free = [sem(f"w_free{k}") for k in range(2)]
    evac = [sem(f"evac{k}") for k in range(2)]
    u_full = [sem(f"u_full{k}") for k in range(RING)]
    x_in = [sem(f"x_in{tb}") for tb in range(TB)]
    v_full = [sem(f"v_full{k}") for k in range(RING)]
    last_full = [sem(f"last_full{k}") for k in range(RING)]

    def w_view(w):
        return w[0].rearrange("(c p) n -> p c n", p=P)

    def load_unit(sp, s, u, src):
        if not (isinstance(s, int) and s == 0):
            sp.wait_ge(lo_full[u % 2], (s - 1) * 2 + u // 2 + 1)
        sp.dma_start(raw[u][:], src).then_inc(raw_full[u], 16)

    def split_hi(act, s, u):
        act.wait_ge(raw_full[u], (s + 1) * 16)
        if not (isinstance(s, int) and s == 0 and u < 2):
            act.wait_ge(w_free[u % 2], s * 2 + u // 2)
        act.copy(wh[u % 2][:], raw[u][:]).then_inc(hi_full[u % 2], 1)

    def split_lo(dve, s, u):
        dve.wait_ge(hi_full[u % 2], s * 2 + u // 2 + 1)
        dve.tensor_tensor(wl[u % 2][:], raw[u][:], wh[u % 2][:].bitcast(F32),
                          ALU.subtract).then_inc(lo_full[u % 2], 1)

    def slab_ready(eng, s):
        eng.wait_ge(w_free[1], s * 2 + 2)

    def lead(eng, split, s0):
        split(eng, s0, 0)
        split(eng, s0, 1)

    def run_slabs(eng, split, s0, n, events, ahead=False):
        for i in range(2, 4 * n + 2):
            if i < 4 * n + ahead:
                split(eng, s0 + i // 4, i % 4)
            for f in events.get(((i - 2) // 4, (i - 2) % 4), ()):
                f()

    def slot(n):
        return n // 2, 2 * (n % 2) + 1

    def plan(*parts):
        events = {}
        for part in parts:
            for slab, unit, f in part:
                events.setdefault((slab, unit), []).append(f)
        return events

    def each(f, s0, n):
        return [(j, 3, lambda j=j: f(s0 + j)) for j in range(n)]

    def cm_out(buf):
        return PS[:, 2 * buf:2 * buf + 2, :].rearrange("p b (t n) -> p (b t) n", n=T)

    def tm_out(buf):
        return PS[:, 2 * buf:2 * buf + 2, :]

    def pe_slab(pe, half, buf, cm, events=None, slab=None, x_in=None):
        if not (isinstance(half, int) and half == 0):
            pe.wait_ge(evac[buf], half)
        for u in range(UNITS):
            pe.wait_ge(lo_full[u % 2], half * 4 + buf * 2 + u // 2 + 1)
            if x_in:
                pe.wait_ge(x_in[0], x_in[1] + u)
            mm_unit(pe, u, buf, cm).then_inc(w_free[u % 2], 1)
            for f in (events or {}).get((slab, u), ()):
                f()

    def mm_unit(pe, u, buf, cm):
        k = u % 2
        if cm:
            o = cm_out(buf)
            for t in range(4):
                for c in range(UC):
                    x = slice(t * P, t * P + P)
                    d = u * UC + c
                    first = u == 0 and c == 0 and t % 2 == 0
                    pe.matmul(o[:, t, :], wh[k][:, c, x], XH[:, d, :], start=first, stop=False,
                              skip_group_check=True)
                    pe.matmul(o[:, t, :], wh[k][:, c, x], XL[:, d, :], start=False, stop=False,
                              skip_group_check=True)
                    m = pe.matmul(o[:, t, :], wl[k][:, c, x], XH[:, d, :], start=False,
                                  stop=d == DC - 1, skip_group_check=True)
            return m
        o = tm_out(buf)
        for tb in range(TB):
            y = slice(tb * P, tb * P + P)
            for c in range(UC):
                d = u * UC + c
                pe.matmul(o[:, tb, :], XH[:, d, y], wh[k][:, c, :], start=d == 0, stop=False,
                          skip_group_check=True)
                pe.matmul(o[:, tb, :], XH[:, d, y], wl[k][:, c, :], start=False, stop=False,
                          skip_group_check=True)
                m = pe.matmul(o[:, tb, :], XL[:, d, y], wh[k][:, c, :], start=False,
                              stop=d == DC - 1, skip_group_check=True)
        return m

    def bank4(b):
        return PS[:, b, :].rearrange("p (c n) -> p c n", n=P)

    def turn_x(pe, n, src, tbs=(0, 1)):
        for tb in tbs:
            pe.wait_ge(S.tm_ready, 2 * n + tb + 1)
            for q in range(4):
                for c in range(4):
                    m = pe.transpose(bank4(4 * tb + q)[:, c, :], src[:, tb, (4 * q + c) * P:(4 * q + c + 1) * P],
                                     ident[:])
                m.then_inc(S.xt_ps, 1)

    def x_part(x, g):
        return x[:, 4 * (g % 4):4 * (g % 4) + 4, (g // 4) * P:(g // 4 + 1) * P]

    def x_hi(act, n, g0=0, g1=8):
        for g in range(g0, g1):
            act.wait_ge(S.xt_ps, 8 * n + g + 1)
            act.copy(x_part(XH, g), bank4(g)).then_inc(S.xt_hi, 1)

    def x_lo(dve, n, g0=0, g1=8):
        for g in range(g0, g1):
            dve.wait_ge(S.xt_hi, 8 * n + g + 1)
            dve.tensor_tensor(x_part(XL, g), bank4(g), x_part(XH, g).bitcast(F32),
                              ALU.subtract).then_inc(S.xt_lo, 1)

    def mix_hi(act, g):
        act.copy(XH[:, 4 * g:4 * g + 4, :], MIX[:, 4 * g:4 * g + 4, :]).then_inc(S.mix_hi, 1)

    def mix_lo(dve, n, g):
        dve.wait_ge(S.mix_hi, 4 * n + g + 1)
        dve.tensor_tensor(XL[:, 4 * g:4 * g + 4, :], MIX[:, 4 * g:4 * g + 4, :],
                          XH[:, 4 * g:4 * g + 4, :].bitcast(F32), ALU.subtract).then_inc(S.mix_lo, 1)

    def bcast(v, shape):
        return v.to_broadcast([P, *shape])

    block = ctx.enter_context(nc.Block())

    @block.sync
    def _(sp):
        def row(v, n):
            return v.partition_broadcast(P)

        def load_x(tb):
            sp.dma_start(RES[:, tb, :], inp["x"][0].rearrange("(b p) d -> b p d", p=P)[tb]).then_inc(x_in[tb], 16)

        def load_first(u):
            load_unit(sp, 0, u, w_in[:, u * UC:(u + 1) * UC, 6 * W:7 * W])

        load_x(0)
        load_x(1)
        sp.dma_start(GAIN[:], row(inp["ln_in_g"], D)).then_inc(S.gain_in, 16)
        sp.dma_start(BIAS[:], row(inp["ln_in_b"], D)).then_inc(S.norm_in, 16)
        w_in = w_view(inp["w_in"])
        for u in range(UNITS):
            load_first(u)
        sp.wait_ge(S.stage_clear, 1)
        sp.dma_start(stage[0:24, 0, :], inp["conv_w"][0].rearrange("j (c p) -> (j c) p", p=P)).then_inc(S.stage_in, 16)
        sp.dma_start(stage[24:32, 0, :], inp["conv_b"][0].rearrange("(c p) -> c p", p=P)).then_inc(S.stage_in, 16)
        sp.dma_start(stage[32:48, 0, :], inp["hgrn_lb_param_2"].rearrange("l (c p) -> (l c) p", p=P)).then_inc(S.stage_in, 16)
        fw = inp["ffn_conv_w_2"][0].rearrange("j (c p) -> j c p", p=P)
        sp.dma_start(stage[0:FC, 1, :], fw[0]).then_inc(S.stage_in, 16)
        sp.dma_start(stage[FC:2 * FC, 1, :], fw[1]).then_inc(S.stage_in, 16)
        sp.dma_start(stage[0:FC, 2, :], fw[2]).then_inc(S.stage_in, 16)
        sp.dma_start(stage[FC:2 * FC, 2, :], inp["ffn_conv_b_2"][0].rearrange("(c p) -> c p", p=P)).then_inc(S.stage_in, 16)
        sp.dma_start(bgate[0:16, :], inp["b_gate"].rearrange("o p -> p o")).then_inc(S.small_in, 16)
        sp.dma_start(fbias[0:H, :], inp["fox_gate_bias_2"].rearrange("o p -> p o")).then_inc(S.small_in, 16)
        sp.dma_start(hgain[:], row(inp["hgrn_norm_gain_2"][0], DH)).then_inc(S.small_in, 16)
        sp.dma_start(mhg[:], row(inp["mh_norm_g"][0], HW)).then_inc(S.small_in, 16)
        sp.dma_start(wg_raw[:], w_in[:, :, 14 * W:14 * W + 16]).then_inc(S.small_in, 16)

        def stream(s0, w, c0, n):
            with sp.Fori(0, n) as i:
                for u in range(UNITS):
                    load_unit(sp, i + s0, u, w[:, u * UC:(u + 1) * UC, ds(i * W + c0, W)])

        stream(1, w_in, 7 * W, 5)
        stream(6, w_in, 2 * W, 4)
        stream(10, w_in, 0, 2)
        stream(12, w_in, 12 * W, 2)
        stream(S_OUT, w_view(inp["w_out"]), 0, 2)
        sp.wait_ge(S.mix_lo, 4)
        sp.dma_start(GAIN[:], row(inp["ln1_g"][0], D)).then_inc(S.norm_in, 16)
        sp.dma_start(BIAS[:], row(inp["ln1_b"][0], D)).then_inc(S.norm_in, 16)
        keys = inp["peer_keys"][0].rearrange("h q n c -> (h q) n c")
        for n in range(2 * H):
            sp.dma_start(KR[:, n, :], keys[n]).then_inc(S.keys_in, 16)
        stream(S_OUT + 2, w_view(inp["w_out"]), 2 * W, 2)
        stream(S_WQ, w_view(inp["peer_wq"]), 0, 4)
        sp.wait_ge(S.scores_cp, 8)
        sp.dma_start(GAIN[:], row(inp["ln2_g"][0], D)).then_inc(S.norm_in, 16)
        sp.dma_start(BIAS[:], row(inp["ln2_b"][0], D)).then_inc(S.norm_in, 16)
        sp.wait_ge(w_free[1], 2 * S_IN2)
        sp.dma_start(GAIN3[:], row(inp["norm1_gain_2"][0], D)).then_inc(S.norm_in, 16)
        sp.wait_ge(last_full[1], 16 * (TOPK // RING))
        w_in2 = w_view(inp["w_in_2"])
        for u in range(UNITS):
            load_unit(sp, S_IN2, u, w_in2[:, u * UC:(u + 1) * UC, 2 * W:3 * W])
        sp.wait_ge(S.ffsum, 8)
        sp.dma_start(wf_raw[:], w_in2[:, :, 14 * W:14 * W + H]).then_inc(S.wf_in, 16)
        with sp.Fori(0, 1) as i:
            for u in range(UNITS):
                load_unit(sp, i + S_IN2 + 1, u, w_in2[:, u * UC:(u + 1) * UC, ds(i * W + 3 * W, W)])
        stream(S_IN2 + 2, w_in2, 0, 2)
        stream(S_IN2 + 4, w_in2, 4 * W, 2)
        stream(S_IN2 + 6, w_in2, 8 * W, 6)
        stream(S_IN2 + 12, w_in2, 6 * W, 2)
        w_out2 = w_view(inp["w_out_2"])

        def load_out(j):
            for u in range(UNITS):
                r = (u + UNITS // 2) % UNITS * UC
                load_unit(sp, S_OUT2 + j, u, w_out2[:, r:r + UC, j * W:(j + 1) * W])

        load_out(0)
        load_out(1)
        sp.wait_ge(S.mix_lo, 8)
        sp.dma_start(GAIN[:], row(inp["norm2_gain_2"][0], D)).then_inc(S.norm_in, 16)
        load_out(2)
        load_out(3)
        wgt, wup = w_view(inp["w_ffn_gate_2"]), w_view(inp["w_ffn_up_2"])
        with sp.Fori(0, FPAIRS) as i:
            for k, w in enumerate((wgt, wup)):
                for u in range(UNITS):
                    load_unit(sp, i * 2 + S_FF + k, u, w[:, u * UC:(u + 1) * UC, ds(i * W, W)])
        wdn = inp["w_ffn_down_2"][0].rearrange("(c p) (b n) -> c p b n", p=P, n=W)
        with sp.Fori(0, NDOWN) as i:
            for u in range(UNITS):
                load_unit(sp, i + S_DOWN, u, wdn[ds(i * UNITS + u, 1)].rearrange("o p b n -> (o p) b n"))
        sp.wait_ge(S.tm_ready, 8)
        sp.dma_start(GAIN[:], row(inp["final_norm_gain_2"], D)).then_inc(S.norm_in, 16)
        for tb in range(TB):
            sp.wait_ge(S.final, tb + 1)
            sp.dma_start(out[0].rearrange("(b p) d -> b p d", p=P)[tb], RES[:, tb, :]).then_inc(S.stored, 16)
        sp.wait_ge(S.stored, 16 * TB)

    @block.gpsimd
    def _(pool):
        link = Chain(pool, S.pool_chain, S.pool_passed)
        pool.memset(stage[:], 0.0).then_inc(S.stage_clear, 1)
        link(pool.memset(ident[:], 0.0))
        pool.affine_select(ident[:], ident[:], [[1, P]], ALU.not_equal, 1.0, base=0,
                           channel_multiplier=-1).then_inc(S.ident_ready, 1)
        pool.memset(smask[:], 1.0)
        pool.memset(ones[:], 1.0)
        pool.memset(maskneg[:], 0.0)
        pool.memset(hmask[:], 1.0)
        link(pool.memset(mask01[:], 1.0))
        for a in (0, 256):
            pool.affine_select(mask01[:, a:a + P], mask01[:, a:a + P], [[1, P]], ALU.is_ge, 0.0, base=0,
                               channel_multiplier=-1)
            pool.affine_select(maskneg[:, a:a + P], maskneg[:, a:a + P], [[-1, P]], ALU.is_ge, LOWEST,
                               base=0, channel_multiplier=1)
        pool.memset(smask[:].rearrange("p (c n) -> p c n", n=CHUNK)[:, :, 0:1], 0.0)
        link(pool.affine_select(hmask[:], hmask[:], [[1, P]], ALU.is_ge, 0.0, base=0, channel_multiplier=-1))
        pool.memset(hmask[0:CHUNK, CHUNK:P], 0.0)
        pool.iota(iota_i[:], [[1, TOPK]], base=0, channel_multiplier=0).then_inc(S.consts, 1)


        def gather(buf, idx, k, table, sem):
            pool.indirect_dma_start(buf[:], None, table, bass.IndirectOffsetOnAxis(ap=idx[:, k:k + 1], axis=0),
                                    ).then_inc(sem, 16)

        def u_row(s, tb, k, first):
            if not (first and k < RING):
                wait_alone(pool, S.dot_done, s * TOPK + k - RING + 1, S.pool_passed)
            gather(ub[k % RING], uidx[:, tb, :], k, inp["peer_u"][0], u_full[k % RING])

        def v_row(s, tb, k, first):
            if first and k == 0:
                pool.wait_ge(w_free[1], 2 * S_WQ + 8)
            if not (first and k < RING):
                wait_alone(pool, S.v_done, s * TOPK + k - RING + 1, S.pool_passed)
            gather(vb[k % RING], vidx[:, tb, :], k, inp["peer_v"][0], v_full[k % RING])

        def step(s, tb, first=False):
            wait_alone(pool, S.uidx_ready, s + 1, S.pool_passed)
            for k in range(TOPK):
                u_row(s, tb, k, first)
                if not first:
                    v_row(s - 1, 1 - tb, k, isinstance(s, int) and s == 1)

        step(0, 0, True)
        step(1, 1)
        with pool.Fori(1, H) as i:
            for tb in range(TB):
                step(i * 2 + tb, tb)
        for k in range(TOPK):
            if k < RING:
                wait_alone(pool, S.dot_done, (LAST + 1) * TOPK - RING + k + 1, S.pool_passed)
            elif k - RING in DVE_ROWS:
                wait_alone(pool, S.v_added, DVE_ROWS.index(k - RING) + 1, S.pool_passed)
            else:
                wait_alone(pool, S.v_done, LAST * TOPK + PE_ROWS.index(k - RING) + 1, S.pool_passed)
            gather(ub[k % RING], vidx[:, LAST % 2, :], k, inp["peer_v"][0], last_full[k % RING])

    @block.scalar
    def _(act):
        link = Chain(act, S.act_chain, S.act_passed)

        def root(n, x):
            act.wait_ge(S.square_ready, n + 1)
            act.activation(x, x, ACT.Sqrt).then_inc(S.root_ready, 1)

        root(0, rstd[:, 0:1])
        root(1, rstd[:, 1:2])
        x_hi(act, 0, 0, 4)
        lead(act, split_hi, S_IN)
        x_hi(act, 0, 4, 8)

        def wg_split():
            act.wait_ge(S.small_in, 80)
            act.copy(wg_h[:], wg_raw[:]).then_inc(S.wg_hi, 1)

        def q_out(dst, scale):
            def f(s):
                slab_ready(act, s)
                act.activation(dst[:, 4 * (s % 2):4 * (s % 2) + 4, :], cm_out(s % 2), ACT.Copy,
                               scale=scale).then_inc(evac[s % 2], 1)
            return f

        def v_out(s):
            slab_ready(act, s)
            act.copy(VX[:, :, 4 * (s % 2):4 * (s % 2) + 4, 0:DH],
                     tm_out(s % 2).rearrange("p b (h d) -> p b h d", d=DH)).then_inc(evac[s % 2], 1)

        def o_out(s):
            slab_ready(act, s)
            act.activation(OG[:, :, W * (s % 2):W * (s % 2) + W], tm_out(s % 2),
                           ACT.Sigmoid).then_inc(evac[s % 2], 1)

        def gate_log(n, x):
            act.wait_ge(S.gate_abs, n + 1)
            link(act.activation(x, x, ACT.Exp, scale=-1.0))
            act.activation(x, x, ACT.Ln, bias=1.0).then_inc(S.gate_ln, 1)

        def m_floor():
            act.wait_ge(S.em_arg, 1)
            act.activation(emcol[:], emcol[:], ACT.Exp).then_inc(S.em_ready, 1)

        def m_head(h):
            if h < H:
                act.wait_ge(S.m_arg, h + 1)
                act.activation(E1[:], E1[:], ACT.Exp).then_inc(S.m_exp, 1)
            if h >= 1:
                act.wait_ge(S.m_num, h)
                act.copy(HN[:, :, h - 1, 0:DH + 1],
                         PS[:, 7, 0:TB * (DH + 1)].rearrange("p (b d) -> p b d", b=TB)).then_inc(S.m_numcp, 1)

        def turned_out(turned, half):
            act.wait_ge(turned, half + 1)
            for tb in range(TB):
                a = act.copy(MIX[:, H + 4 * half:H + 4 * half + 4, tb * P:(tb + 1) * P],
                             PS[:, 6 + tb, :].rearrange("p (h t) -> p h t", t=P))
            a.then_inc(S.mix_y, 1)

        outs = [q_out(QT, 1.0)] * 2 + [q_out(KT, SCALE)] * 2 + [v_out] * 2 + [None] * 6 + [o_out]
        run_slabs(act, split_hi, S_IN, 14, plan(
            [(j, 3, lambda j=j: outs[j](S_IN + j)) for j in range(13) if outs[j]],
            [(1, 0, wg_split), (*slot(GATES1), lambda: gate_log(0, LA1[0:16, :])), (*slot(GATES1 + 2), m_floor)],
            [(*divmod(HEADS1 + 2 * h, UNITS), lambda h=h: m_head(h)) for h in range(H + 1)],
            [(10, 1, lambda: root(2, hr[:])), (11, 1, lambda: root(3, hr[:]))],
            [(13, 2, lambda: turned_out(S.m_turn, 0))]))
        split_hi(act, S_OUT, 0)
        slab_ready(act, S_OUT - 1)
        act.wait_ge(S.conv_done, 2)
        mix_hi(act, 0)
        split_hi(act, S_OUT, 1)
        o_out(S_OUT - 1)
        mix_hi(act, 1)
        act.wait_ge(S.mix_y, 1)
        mix_hi(act, 2)
        turned_out(S.m_turn, 1)
        act.wait_ge(S.mix_y, 2)
        mix_hi(act, 3)

        def keys_turned():
            for n in range(4):
                act.wait_ge(S.keyT_ps, n + 1)
                act.copy(KX[:, 4 * n:4 * n + 4, :],
                         PS[:, 4 + n, :].rearrange("p (a k) -> p a k", k=P)).then_inc(S.keyT, 1)

        def bound_exp():
            act.wait_ge(S.lb_arg, 1)
            act.activation(lb0[:], lb0[:], ACT.Exp).then_inc(S.lb_exp, 1)
            act.activation(lb1[:], lb1[:], ACT.Exp).then_inc(S.lb_exp, 1)

        run_slabs(act, split_hi, S_OUT, 4, plan([(1, 2, bound_exp), (3, 2, keys_turned)]), True)
        split_hi(act, S_WQ, 1)
        root(4, rstd[:])

        x_hi(act, 1)

        def pq_out(s):
            slab_ready(act, s)
            j = s - S_WQ
            act.copy(PQ[:, 4 * j:4 * j + 4, :], cm_out(s % 2)).then_inc(evac[s % 2], 1)

        def scores_out(q):
            for tb in range(TB):
                n = TB * q + tb
                act.wait_ge(S.score_ps, n + 1)
                act.copy(SC[:, tb, 2 * q:2 * q + 2, :, :],
                         PS[:, 4 + n % 4, :].rearrange("p (h c k) -> p h c k", h=2, c=2)).then_inc(S.scores_cp, 1)

        def soft(n, par):
            act.wait_ge(S.soft_arg, n + 1)
            act.activation(eexp[:], tops[:], ACT.Exp, bias=nmx[:, 0:1], accum_out=esum[:]).then_inc(S.soft_exp, 1)

        act.wait_ge(S.tm_ready, 4)
        run_slabs(act, split_hi, S_WQ, 4, plan(
            each(pq_out, S_WQ, 4),
            [(q + 1, 0, lambda q=q: scores_out(q)) for q in range(3)],
            [(1, 2, lambda: soft(0, 0))]))
        scores_out(3)

        def weigh(n, tb, first=False, rows=range(TOPK)):
            act.wait_ge(S.dots_ready, n + 1)
            act.activation(acts[:, tb, :], dots[:, tb, :], ACT.Gelu).then_inc(S.gelu_ready, 1)
            act.wait_ge(S.ew_ready, n + 1)
            for k in rows:
                if not first:
                    act.wait_ge(S.v_done, (n - 1) * TOPK + k + 1)
                act.activation(diag[:, k, :], ident[:], ACT.Copy, scale=ew[:, tb, k:k + 1]).then_inc(S.diag_ready, 1)

        soft(1, 1)
        weigh(0, 0, True)
        soft(2, 0)
        weigh(1, 1)
        with act.Fori(1, H - 1) as i:
            for tb in range(TB):
                soft(i * 2 + tb + 1, 1 - tb)
                weigh(i * 2 + tb, tb)
        soft(LAST, 1)
        weigh(LAST - 1, 0)
        weigh(LAST, 1, rows=PE_ROWS)

        root(5, rstd[:, 0:1])
        root(6, rstd[:, 0:1])
        x_hi(act, 2, 0, 4)
        split_hi(act, S_IN2, 0)
        root(7, rstd[:, 1:2])
        split_hi(act, S_IN2, 1)
        root(8, rstd[:, 1:2])
        x_hi(act, 2, 4, 8)

        def wf_split():
            act.wait_ge(S.wf_in, 16)
            act.copy(wf_h[:], wf_raw[:]).then_inc(S.wf_hi, 1)

        def part(x, j):
            return x[:, 4 * j:4 * j + 4, :]

        def f_out(s):
            slab_ready(act, s)
            act.wait_ge(S.nrm_used, 1)
            act.activation(part(G_F, s % 2), cm_out(s % 2), ACT.Sigmoid).then_inc(evac[s % 2], 1)

        def f_log(j):
            act.wait_ge(S.f_ready, j + 1)
            act.activation(part(G_E, j), part(G_F, j), ACT.Ln).then_inc(S.lnf_ready, 1)

        def b_exp(j):
            act.wait_ge(S.b_ready, j + 1)
            act.activation(part(G_K, j), part(G_B, j), ACT.Exp).then_inc(S.expb_ready, 1)
            act.activation(dcay[:, 4 * j:4 * j + 4, :],
                           part(G_B, j).rearrange("p h (c n) -> p h c n", n=CHUNK)[:, :, :, CHUNK - 1],
                           ACT.Exp).then_inc(S.dcay_ready, 1)

        def gq_out(s):
            slab_ready(act, s)
            j = s % 2
            act.activation(part(G_Q, j), cm_out(j), ACT.Copy, scale=SCALE).then_inc(evac[j], 1)
            act.wait_ge(S.ke_arg, j + 1)
            act.activation(part(G_E, j), part(G_E, j), ACT.Exp).then_inc(S.expe_ready, 1)

        def nb_exp(j):
            act.wait_ge(S.q_decayed, j + 1)
            act.activation(part(G_K, j), part(G_B, j), ACT.Exp, scale=-1.0).then_inc(S.expnb_ready, 1)

        def fqk_out(dst, scale):
            def f(s):
                slab_ready(act, s)
                act.wait_ge(S.k_decayed, 2)
                act.activation(part(dst, s % 2), cm_out(s % 2), ACT.Copy, scale=scale).then_inc(evac[s % 2], 1)
            return f

        def tm_copy(dst):
            def f(s):
                slab_ready(act, s)
                act.copy(dst[:, :, W * (s % 2):W * (s % 2) + W], tm_out(s % 2)).then_inc(evac[s % 2], 1)
            return f

        def g_out(s):
            slab_ready(act, s)
            act.wait_ge(S.g_ocp, H)
            act.activation(G_G[:, :, W * (s % 2):W * (s % 2) + W], tm_out(s % 2),
                           ACT.Silu).then_inc(evac[s % 2], 1)

        def g_step(n):
            if n < H:
                act.wait_ge(S.g_keT, n + 1)
                if n >= 1:
                    act.wait_ge(S.g_ds, n)
                kt = PS[:, 5, 0:T].rearrange("p (b d) -> p b d", b=TB)
                act.copy(KE[0:CHUNK, 0:NCH - 1:2, :], kt[0:CHUNK])
                act.copy(KE[CHUNK:P, 1, :], kt[CHUNK:P, 0, :]).then_inc(S.g_ke, 1)
            if n >= 2:
                act.wait_ge(S.g_o, n - 1)
                act.copy(GO[:, n - 2, :, :], PS[:, 7, 0:T].rearrange("p (b d) -> p b d", b=TB)).then_inc(S.g_ocp, 1)

        def a_step(n):
            if 2 <= n < H + 2:
                g = n - 2
                act.wait_ge(S.a_pT, g + 1)
                if g >= 2:
                    act.wait_ge(S.a_out, g - 1)
                act.copy(PM2[:, g % 2, :], PS[:, 5, 0:384]).then_inc(S.a_pTcp, 1)
            if n < H:
                e = n % 2
                act.wait_ge(S.a_max, n + 1)
                act.activation(E2[:, e, 0:P], E2[:, e, 0:P], ACT.Exp, bias=nmax[:, e, 0:1],
                               accum_out=psum_[:, e, 0:1])
                act.activation(E2[:, e, P:384], E2[:, e, P:384], ACT.Exp, bias=nmax[:, e, 1:2],
                               accum_out=psum_[:, e, 1:2]).then_inc(S.a_exp, 1)

        outs2 = [f_out] * 2 + [gq_out] * 2 + [tm_copy(G_V)] * 2 + [fqk_out(FQ, SCALE)] * 2 \
            + [fqk_out(FK, 1.0)] * 2 + [tm_copy(FV)] * 2 + [g_out]
        run_slabs(act, split_hi, S_IN2, 14, plan(
            [(j, 3, lambda j=j: outs2[j](S_IN2 + j)) for j in range(13)],
            [(0, 1, wf_split), (*slot(GATES2), lambda: gate_log(1, LA2[0:H, :]))],
            [(1 + j, 0, lambda j=j: f_log(j)) for j in range(2)],
            [(2 + j, 1, lambda j=j: b_exp(j)) for j in range(2)],
            [(3 + j, 0, lambda j=j: nb_exp(j)) for j in range(2)],
            [(*slot(HEADS2 + n), lambda n=n: g_step(n)) for n in range(H + 2)],
            [(*divmod(ATTN + n, UNITS), lambda n=n: a_step(n)) for n in range(H + 2)],
            [(10, 2, lambda: root(9, hr[:])), (11, 2, lambda: root(10, hr[:]))],
            [(13, 2, lambda: turned_out(S.g_turn, 0))]))
        split_hi(act, S_OUT2, 0)
        slab_ready(act, S_OUT2 - 1)
        act.wait_ge(S.mix_a, H)
        mix_hi(act, 0)
        split_hi(act, S_OUT2, 1)
        g_out(S_OUT2 - 1)
        mix_hi(act, 1)
        act.wait_ge(S.mix_y, 3)
        mix_hi(act, 2)
        turned_out(S.g_turn, 1)
        act.wait_ge(S.mix_y, 4)
        mix_hi(act, 3)
        run_slabs(act, split_hi, S_OUT2, 4, {}, True)
        split_hi(act, S_FF, 1)
        root(11, rstd[:])

        x_hi(act, 3)

        def gate_conv(n, s):
            slab_ready(act, s)
            if not (isinstance(n, int) and n == 0):
                act.wait_ge(S.ff_up, n)
            for t in range(4):
                w2 = cols[:, 2, ds(n * 4 + t, 1)] if not isinstance(n, int) else cols[:, 2, 4 * n + t:4 * n + t + 1]
                b = cols[:, 2, ds(n * 4 + t + FC, 1)] if not isinstance(n, int) else cols[:, 2, FC + 4 * n + t:FC + 4 * n + t + 1]
                a = act.activation(FY[:, t, :], cm_out(0)[:, t, :], ACT.Identity, bias=b, scale=w2)
            a.then_inc(S.ff_y, 1)

        def gate_silu(n):
            act.wait_ge(S.ff_conv, n + 1)
            act.activation(FY[:], FY[:], ACT.Silu).then_inc(S.ff_silu, 1)

        def ff_pair(n, s, first=False):
            for u in range(2 if first else 0, UNITS):
                split_hi(act, s, u)
            split_hi(act, s + 1, 0)
            split_hi(act, s + 1, 1)
            gate_conv(n, s)
            split_hi(act, s + 1, 2)
            gate_silu(n)
            split_hi(act, s + 1, 3)

        ff_pair(0, S_FF, True)
        with act.Fori(1, FPAIRS) as i:
            ff_pair(i, i * 2 + S_FF)
        def down_hi(j, s):
            for u in range(UNITS):
                split_hi(act, s, u)
                act.copy(ah[u % 2][:], FA[:, ds(j * UNITS + u, 1), :].rearrange("p o n -> p (o n)")
                         if not isinstance(j, int) else FA[:, j * UNITS + u, :]).then_inc(S.ah_full, 1)

        down_hi(0, S_DOWN)
        act.wait_ge(S.ff_up, FPAIRS)
        with act.Fori(1, NDOWN) as i:
            down_hi(i, i + S_DOWN)
        for tb in range(TB):
            act.wait_ge(S.summed, tb + 1)
            act.activation(NRM[:, tb, :], RES[:, tb, :], ACT.Square, accum_out=msq[:, tb:tb + 1]).then_inc(S.squares, 1)
            root(12 + tb, rstd[:, tb:tb + 1])

    @block.vector
    def _(dve):
        link = Chain(dve, S.dve_chain, S.dve_passed)

        def inverse_root(n, x, src, eps):
            dve.tensor_scalar(x, src, eps, None, ALU.add).then_inc(S.square_ready, 1)
            dve.wait_ge(S.root_ready, n + 1)
            link(dve.reciprocal(x, x))

        def row_stats(tb, q):
            return dve.bn_stats(stats[:, tb, q, :], RES[:, tb, q * W:(q + 1) * W])

        def moments():
            for tb in range(TB):
                a = dve.bn_aggr(mv[:, tb, :], stats[:, tb, :, :])
            link(a)

        def layer_norm(n, norms_in, ready):
            moments()
            inverse_root(n, rstd[:], mv[:, :, 1], LN_EPS)
            dve.wait_ge(S.norm_in, norms_in)
            for tb in range(TB):
                link(dve.scalar_tensor_tensor(RES[:, tb, :], RES[:, tb, :], mv[:, tb, 0:1], GAIN[:],
                                              ALU.subtract, ALU.mult))
                link(dve.scalar_tensor_tensor(RES[:, tb, :], RES[:, tb, :], rstd[:, tb:tb + 1], BIAS[:],
                                              ALU.mult, ALU.add), ready)

        def rms_norm(n, dst, norms_in, ready):
            moments()
            link(dve.tensor_tensor(msq[:], mv[:, :, 0], mv[:, :, 0], ALU.mult))
            link(dve.tensor_tensor(msq[:], msq[:], mv[:, :, 1], ALU.add))
            inverse_root(n, rstd[:], msq[:], RMS_EPS)
            dve.wait_ge(S.norm_in, norms_in)
            for tb in range(TB):
                dve.scalar_tensor_tensor(dst[:, tb, :], RES[:, tb, :], rstd[:, tb:tb + 1], GAIN[:],
                                         ALU.mult, ALU.mult).then_inc(ready, 1)

        def x_lead(n, s0):
            x_lo(dve, n, 0, 5)
            split_lo(dve, s0, 1)
            x_lo(dve, n, 5, 8)

        for tb in range(TB):
            dve.wait_ge(x_in[tb], 16)
            for q in range(4):
                a = row_stats(tb, q)
            link(a)
            link(dve.bn_aggr(mv[:, tb, :], stats[:, tb, :, :]))
            inverse_root(tb, rstd[:, tb:tb + 1], mv[:, tb, 1:2], LN_EPS)
        dve.wait_ge(S.gain_in, 16)
        for tb in range(TB):
            link(dve.scalar_tensor_tensor(RES[:, tb, :], RES[:, tb, :], mv[:, tb, 0:1], GAIN[:],
                                          ALU.subtract, ALU.mult))
            dve.wait_ge(S.norm_in, 16)
            link(dve.scalar_tensor_tensor(RES[:, tb, :], RES[:, tb, :], rstd[:, tb:tb + 1], BIAS[:],
                                          ALU.mult, ALU.add), S.tm_ready)
        split_lo(dve, S_IN, 0)
        x_lead(0, S_IN)

        def c_out(s):
            slab_ready(dve, s)
            link(dve.tensor_copy(ZC[:, 4 * (s % 2):4 * (s % 2) + 4, 2:], cm_out(s % 2)), evac[s % 2])

        def h_out(s):
            slab_ready(dve, s)
            j = s % 2
            z = ZC[:, 4 * j:4 * j + 4, :]
            link(dve.tensor_tensor(z[:, :, 2:], z[:, :, 2:], cm_out(j), ALU.mult), evac[j])
            for t in range(4 * j, 4 * j + 4):
                dve.tensor_scalar(MIX[:, t, :], ZC[:, t, 2:], cols[:, 0, 16 + t:17 + t], cols[:, 0, 24 + t:25 + t],
                                  ALU.mult, ALU.add)
            for tap in (1, 0):
                link(dve.engine_nop())
                for t in range(4 * j, 4 * j + 4):
                    dve.scalar_tensor_tensor(MIX[:, t, :], ZC[:, t, tap:tap + T],
                                             cols[:, 0, 8 * tap + t:8 * tap + t + 1], MIX[:, t, :],
                                             ALU.mult, ALU.add)
            link(dve.engine_nop())

        def b_out(s):
            slab_ready(dve, s)
            j = s % 2
            m = MIX[:, 4 * j:4 * j + 4, :]
            link(dve.tensor_tensor(m, m, cm_out(j), ALU.mult), evac[j], S.conv_done)

        bt = PS[:, 6, 0:T].rearrange("p (b n) -> p b n", b=TB)

        def m_clear():
            dve.memset(ZC[:, :, 0:2], 0.0)
            dve.memset(BP1[:], 0.0)
            dve.memset(RA1[:], 0.0)
            link(dve.memset(VX[:, :, :, DH:DH + 1], 1.0))

        def wg_split():
            dve.wait_ge(S.wg_hi, 1)
            dve.tensor_tensor(wg_l[:], wg_raw[:], wg_h[:].bitcast(F32), ALU.subtract).then_inc(S.wg_lo, 1)
            dve.wait_ge(S.consts, 1)
            dve.tensor_copy(iota_f[:], iota_i[:])

        def columns_out():
            dve.wait_ge(S.cols_ps, 1)
            link(dve.tensor_copy(cols[:], PS[:, 7, 0:384].rearrange("p (a n) -> p a n", n=P)), S.cols_ready)

        def gate_sigmoid(n, rows, lg, la, ls, bias):
            dve.wait_ge(S.gate_ps, n + 1)
            dve.wait_ge(S.small_in, 80)
            link(dve.tensor_scalar(lg[0:rows, :], PS[0:rows, 6, 0:T], bias[0:rows, :], None, ALU.add))
            dve.scalar_tensor_tensor(la[0:rows, :], lg[0:rows, :], -1.0, lg[0:rows, :], ALU.mult,
                                     ALU.max).then_inc(S.gate_abs, 1)
            dve.wait_ge(S.gate_ln, n + 1)
            link(dve.scalar_tensor_tensor(ls[0:rows, :], lg[0:rows, :], 0.0, la[0:rows, :], ALU.min,
                                          ALU.subtract), *([S.gates_ready] if n == 0 else []))

        def m_cumulate():
            dve.wait_ge(S.gates_low, 1)
            link(dve.tensor_copy(LS1[0:H, :], PS[0:H, 7, 0:T]))
            link(dve.tensor_tensor_scan(FS[0:H, :], ones[0:H, :], LS1[0:H, :], 0.0, ALU.mult, ALU.add))
            link(dve.tensor_tensor(BP1[0:H, :], LG1[0:H, :], FS[0:H, :], ALU.subtract))
            link(dve.tensor_tensor_scan(CM[0:H, :], BP1[0:H, :], BP1[0:H, :], 0.0, ALU.max, ALU.max))
            link(dve.tensor_scalar(RA1[0:H, :], CM[0:H, :], -1.0, None, ALU.mult))
            link(dve.tensor_tensor(LS1[0:H, :], RA1[0:H, :], FS[0:H, :], ALU.subtract))
            dve.tensor_copy(BP1[32:32 + H, :], LS1[0:H, :]).then_inc(S.gates_cm, 1)

        def m_columns():
            dve.wait_ge(S.gates_back, 1)
            link(dve.tensor_copy(bcol[:], bt[:, :, 0:H]))
            dve.tensor_copy(emcol[:], bt[:, :, 32:32 + H]).then_inc(S.em_arg, 1)

        def m_head(h):
            dve.wait_ge(S.m_scores, h + 1)
            if h >= 1:
                dve.wait_ge(S.m_prob, h)
            dve.tensor_scalar(E1[:, 0:T], PS[:, 5, 0:T], bcol[:, 0, h:h + 1], 0.0, ALU.add, ALU.min)
            dve.tensor_scalar(E1[:, T:384], PS[:, 5, P:T], bcol[:, 1, h:h + 1], 0.0, ALU.add,
                              ALU.min).then_inc(S.m_arg, 1)
            dve.wait_ge(S.m_exp, h + 1)
            link(dve.tensor_tensor(E1[:], E1[:], mask01[:], ALU.mult))
            if h >= 1:
                dve.wait_ge(S.m_num, h)
            dve.tensor_tensor(PM1[:], E1[:], PS[:, 4, 0:384], ALU.mult).then_inc(S.m_prob, 1)

        def m_stats(tb):
            if tb == 0:
                dve.wait_ge(S.m_numcp, H)
                dve.wait_ge(S.em_ready, 1)
                link(dve.scalar_tensor_tensor(den[:], HN[:, :, :, DH], -1.0, HN[:, :, :, DH], ALU.mult, ALU.max))
                link(dve.tensor_tensor(den[:], den[:], emcol[:], ALU.max))
                link(dve.reciprocal(den[:], den[:]))
            hh = HN[:, tb, :, 0:DH]
            link(dve.tensor_tensor(hh, hh, bcast(den[:, tb, :].unsqueeze(2), [H, DH]), ALU.mult))
            for h in range(H):
                b = dve.bn_stats(hstat[:, h, :], HN[:, tb, h, 0:DH])
            link(b)
            for h in range(H):
                b = dve.bn_aggr(hmv[:, h, :], hstat[:, h, :])
            link(b)
            inverse_root(2 + tb, hr[:], hmv[:, :, 1], LN_EPS)

        def m_norm(tb):
            hh = HN[:, tb, :, 0:DH]
            for h in range(H):
                a = dve.tensor_scalar(HN[:, tb, h, 0:DH], HN[:, tb, h, 0:DH], hmv[:, h, 0:1], hr[:, h:h + 1],
                                      ALU.subtract, ALU.mult)
            link(a)
            link(dve.tensor_tensor(hh, hh, mhg[:].rearrange("p (h d) -> p h d", d=DH), ALU.mult))

        def m_gate(half):
            dve.wait_ge(evac[half], 7)
            for tb in range(TB):
                hh = HN[:, tb, 4 * half:4 * half + 4, 0:DH]
                og = OG[:, tb, half * W:(half + 1) * W].rearrange("p (h d) -> p h d", d=DH)
                a = dve.tensor_tensor(hh, hh, og, ALU.mult)
            link(a, S.m_y)

        run_slabs(dve, split_lo, S_IN, 14, plan(
            [(6 + j, 3, lambda j=j: (c_out, h_out, b_out)[j // 2](6 + j)) for j in range(6)],
            [(0, 1, m_clear), (1, 0, wg_split), (1, 1, columns_out)],
            [(*slot(GATES1), lambda: gate_sigmoid(0, 16, LG1, LA1, LS1, bgate)), (*slot(GATES1 + 1), m_cumulate),
             (*slot(GATES1 + 2), m_columns)],
            [(*divmod(HEADS1 + 2 * h, UNITS), lambda h=h: m_head(h)) for h in range(H)],
            [(10, 1, lambda: m_stats(0)), (10, 2, lambda: m_norm(0)), (11, 1, lambda: m_stats(1)), (11, 2, lambda: m_norm(1)),
             (13, 1, lambda: m_gate(0))]))
        split_lo(dve, S_OUT, 0)
        mix_lo(dve, 0, 0)
        split_lo(dve, S_OUT, 1)
        m_gate(1)
        mix_lo(dve, 0, 1)
        mix_lo(dve, 0, 2)
        mix_lo(dve, 0, 3)

        def res_add(scale):
            def f(s):
                slab_ready(dve, s)
                q = s - (S_OUT if s < S_OUT2 else S_OUT2)
                r = RES[:, :, q * W:(q + 1) * W]
                link(dve.scalar_tensor_tensor(r, r, scale, tm_out(s % 2), ALU.mult, ALU.add), evac[s % 2])
                dve.wait_ge(evac[s % 2], s // 2 + 1)
                for tb in range(TB):
                    a = row_stats(tb, q)
                if q == 3:
                    link(a)
            return f

        def bound_arg():
            link(dve.tensor_tensor(lbm[:], cols[:, 0, 32:40], cols[:, 0, 40:48], ALU.max))
            dve.tensor_tensor(lb0[:], cols[:, 0, 32:40], lbm[:], ALU.subtract)
            link(dve.tensor_tensor(lb1[:], cols[:, 0, 40:48], lbm[:], ALU.subtract), S.lb_arg)

        def bound():
            dve.wait_ge(S.lb_exp, 2)
            link(dve.tensor_tensor(lbs[:], lb0[:], lb1[:], ALU.add))
            link(dve.reciprocal(lbs[:], lbs[:]))
            link(dve.tensor_tensor(lb[:], lb0[:], lbs[:], ALU.mult))
            link(dve.tensor_scalar(omlb[:], lb[:], -1.0, 1.0, ALU.mult, ALU.add))

        run_slabs(dve, split_lo, S_OUT, 4, plan(each(res_add(ALPHA), S_OUT, 4), [(1, 1, bound_arg), (2, 1, bound)]), True)
        layer_norm(4, 48, S.tm_ready)
        x_lead(1, S_WQ)

        def top16(vals, spare, dst, idx):
            link(dve.max(dst[:, 0:8], vals))
            dve.max_index(idx[:, 0:8], dst[:, 0:8], vals)
            link(dve.match_replace(spare, dst[:, 0:8], vals, LOWEST))
            link(dve.max(dst[:, 8:16], spare))
            link(dve.max_index(idx[:, 8:16], dst[:, 8:16], spare))

        def route_keys(n, tb, h):
            src = SC[:, tb, ds(h, 1), :, :].rearrange("p o a k -> p (o a) k") if not isinstance(h, int) else SC[:, tb, h, :, :]
            link(dve.tensor_copy(sc[:], src))
            for a in range(2):
                top16(sc[:, a, :], sc2[:, a, :], best[:, a, :], bidx[:, a, :])
            link(dve.tensor_copy(bidf[:], bidx[:]))
            link(dve.tensor_tensor(cand[:], bcast(best[:, 0, :].unsqueeze(2), [TOPK, TOPK]),
                                   bcast(best[:, 1, :].unsqueeze(1), [TOPK, TOPK]), ALU.add))

        def route_pairs(n, tb):
            if not (isinstance(n, int) and n == 0):
                wait_alone(dve, S.soft_exp, n, S.dve_passed)
            c1, c2 = cand[:].rearrange("p a b -> p (a b)"), cand2[:].rearrange("p a b -> p (a b)")
            top16(c1, c2, tops[:], topj[:])
            dve.tensor_scalar(nmx[:], tops[:, 0:1], -1.0, None, ALU.mult).then_inc(S.soft_arg, 1)
            dve.tensor_scalar(tij[:, 0, :], topj[:], 4, None, ALU.logical_shift_right)
            link(dve.tensor_scalar(tij[:, 1, :], topj[:], 15, None, ALU.bitwise_and))
            link(dve.tensor_copy(tijf[:], tij[:]))
            for a in range(2):
                link(dve.tensor_tensor(hot[:, a, :, :], bcast(iota_f[:].unsqueeze(1), [TOPK, TOPK]),
                                       bcast(tijf[:, a, :].unsqueeze(2), [TOPK, TOPK]), ALU.is_equal))
                link(dve.tensor_tensor(hot[:, a, :, :], hot[:, a, :, :],
                                       bcast(bidf[:, a, :].unsqueeze(1), [TOPK, TOPK]), ALU.mult))
            link(dve.tensor_reduce(eids[:], hot[:], AX, ALU.add))
            link(dve.scalar_tensor_tensor(eidf[:], eids[:, 0, :], float(NKEY), eids[:, 1, :], ALU.mult, ALU.add))
            dve.tensor_copy(uidx[:, tb, :], eidf[:]).then_inc(S.uidx_ready, 1)
            dve.wait_ge(S.soft_exp, n + 1)
            link(dve.reciprocal(rsum[:], esum[:]))
            link(dve.tensor_scalar(gate[:, tb, :], eexp[:], rsum[:, 0:1], None, ALU.mult))

        def dot_rows(n, tb, k0=0, k1=TOPK):
            if k0 == 0:
                dve.tensor_copy(vidx[:, tb, :], uidx[:, tb, :])
            for k in range(k0, k1):
                dve.wait_ge(u_full[k % RING], (n * (TOPK // RING) + k // RING + 1) * 16)
                dve.tensor_tensor_reduce(ub[k % RING][:], ub[k % RING][:], RES[:, tb, :], 1.0, 0.0, ALU.mult,
                                         ALU.add, dots[:, tb, k:k + 1]).then_inc(S.dot_done, 1)
            if k1 == TOPK:
                dve.wait_ge(S.dot_done, (n + 1) * TOPK).then_inc(S.dots_ready, 1)

        def weights(n, tb):
            dve.wait_ge(S.gelu_ready, n + 1)
            dve.tensor_tensor(ew[:, tb, :], acts[:, tb, :], gate[:, tb, :], ALU.mult).then_inc(S.ew_ready, 1)

        def expert_step(n, tb, h_next, done=0):
            if h_next is not None:
                route_keys(n + 1, 1 - tb, h_next)
                route_pairs(n + 1, 1 - tb)
            dot_rows(n, tb, done)
            weights(n, tb)

        def first_keys():
            dve.wait_ge(S.scores_cp, 1)
            route_keys(0, 0, 0)

        run_slabs(dve, split_lo, S_WQ, 4, plan(
            [(1, 1, first_keys), (1, 2, lambda: route_pairs(0, 0))],
            [(2 + k // 4, k % 4, lambda k=k: dot_rows(0, 0, k, k + 1)) for k in range(EARLY)]))
        dve.wait_ge(S.scores_cp, 2)
        expert_step(0, 0, 0, EARLY)
        dve.wait_ge(S.scores_cp, 8)
        expert_step(1, 1, 1)
        with dve.Fori(1, H - 1) as i:
            link.enter(i, 1, 50)
            for tb in range(TB):
                expert_step(i * 2 + tb, tb, i + tb)
        link.leave(1, H - 2)
        expert_step(LAST - 1, 0, H - 1)
        dve.wait_ge(S.v_done, (LAST - 1) * TOPK)
        expert_step(LAST, 1, None)

        def last_row(k):
            dve.wait_ge(last_full[k % RING], (k // RING + 1) * 16)
            link(dve.scalar_tensor_tensor(RES[:, 1, :], ub[k % RING][:], ew[:, 1, k:k + 1], RES[:, 1, :],
                                          ALU.mult, ALU.add), S.v_added)

        def add_sums(tb, scale):
            for b in range(4):
                r = RES[:, tb, b * W:(b + 1) * W]
                dve.scalar_tensor_tensor(r, r, scale, PS[:, 4 * tb + b, :], ALU.mult, ALU.add).then_inc(S.ffsum, 1)
            dve.wait_ge(S.ffsum, 4 * tb + 4)

        def second_norms(tb):
            for b in range(4):
                a = row_stats(tb, b)
            link(a)
            link(dve.bn_aggr(mv[:, tb, :], stats[:, tb, :, :]))
            r1 = rstd[:, tb:tb + 1]
            inverse_root(5 + 2 * tb, r1, mv[:, tb, 1:2], LN_EPS)
            dve.wait_ge(S.norm_in, 96)
            link(dve.scalar_tensor_tensor(RES[:, tb, :], RES[:, tb, :], mv[:, tb, 0:1], GAIN[:],
                                          ALU.subtract, ALU.mult))
            link(dve.scalar_tensor_tensor(RES[:, tb, :], RES[:, tb, :], r1, BIAS[:], ALU.mult, ALU.add))
            for b in range(4):
                a = row_stats(tb, b)
            link(a)
            link(dve.bn_aggr(mv[:, tb, :], stats[:, tb, :, :]))
            m1 = msq[:, tb:tb + 1]
            link(dve.tensor_tensor(m1, mv[:, tb, 0:1], mv[:, tb, 0:1], ALU.mult))
            link(dve.tensor_tensor(m1, m1, mv[:, tb, 1:2], ALU.add))
            inverse_root(6 + 2 * tb, r1, m1, RMS_EPS)
            dve.scalar_tensor_tensor(NRM[:, tb, :], RES[:, tb, :], r1, GAIN3[:], ALU.mult,
                                     ALU.mult).then_inc(S.tm_ready, 1)

        link(dve.tensor_scalar(RES[:, 1, :], RES[:, 1, :], ALPHA, None, ALU.mult))
        dve.wait_ge(S.v_done, LAST * TOPK)
        add_sums(0, ALPHA)
        second_norms(0)
        for k in DVE_ROWS[:2]:
            last_row(k)
        x_lo(dve, 2, 0, 4)
        for k in DVE_ROWS[2:-1]:
            last_row(k)
        dve.wait_ge(S.acc_done, 1)
        add_sums(1, 1.0)
        last_row(DVE_ROWS[-1])
        second_norms(1)

        split_lo(dve, S_IN2, 0)
        x_lo(dve, 2, 4, 5)
        dve.wait_ge(S.tm_ready, 6)
        split_lo(dve, S_IN2, 1)
        x_lo(dve, 2, 5, 8)
        dve.wait_ge(S.xt_lo, 24)
        dve.engine_nop().then_inc(S.nrm_used, 1)

        def wf_split():
            dve.wait_ge(S.wf_hi, 1)
            dve.tensor_tensor(wf_l[:], wf_raw[:], wf_h[:].bitcast(F32), ALU.subtract).then_inc(S.wf_lo, 1)

        def clear():
            dve.memset(BP2[:], 0.0)
            dve.memset(RA2[:], 0.0)
            dve.memset(KE[:], 0.0)
            link(dve.memset(AT[:], 0.0))

        def f_fix(j):
            dve.wait_ge(evac[j], S_IN2 // 2 + 1)
            for h in range(4 * j, 4 * j + 4):
                a = dve.tensor_scalar(G_F[:, h, :], G_F[:, h, :], omlb[:, h:h + 1], lb[:, h:h + 1], ALU.mult, ALU.add)
            link(a, S.f_ready)

        def f_cumulate(j):
            dve.wait_ge(S.lnf_ready, j + 1)
            for h in range(4 * j, 4 * j + 4):
                a = dve.tensor_tensor_scan(G_B[:, h, :], smask[:], G_E[:, h, :], 0.0, ALU.mult, ALU.add)
            link(a, S.b_ready)

        def q_fix(j):
            hs = slice(4 * j, 4 * j + 4)
            bc = G_B[:, hs, :].rearrange("p h (c n) -> p (h c) n", n=CHUNK)
            ec = G_E[:, hs, :].rearrange("p h (c n) -> p (h c) n", n=CHUNK)
            last = bc[:, :, CHUNK - 1:CHUNK]
            dve.wait_ge(S.b_ready, j + 1)
            link(dve.tensor_tensor(ec, bcast(last, [4 * NCH, CHUNK]), bc, ALU.subtract), S.ke_arg)
            link(dve.tensor_scalar(G_F[:, hs, :], G_F[:, hs, :], -1.0, 1.0, ALU.mult, ALU.add))
            dve.wait_ge(evac[j], S_IN2 // 2 + 2)
            dve.wait_ge(S.expb_ready, j + 1)
            link(dve.tensor_tensor(G_Q[:, hs, :], G_Q[:, hs, :], G_K[:, hs, :], ALU.mult), S.q_decayed)

        def k_fix(j):
            hs = slice(4 * j, 4 * j + 4)
            dve.wait_ge(S.expe_ready, j + 1)
            link(dve.tensor_tensor(G_E[:, hs, :], G_E[:, hs, :], G_F[:, hs, :], ALU.mult))
            dve.wait_ge(S.expnb_ready, j + 1)
            link(dve.tensor_tensor(G_K[:, hs, :], G_K[:, hs, :], G_F[:, hs, :], ALU.mult), S.k_decayed)

        def a_cumulate():
            dve.wait_ge(S.gate_ln, 2)
            link(dve.tensor_tensor_scan(BP2[0:H, :], ones[0:H, :], LS2[0:H, :], 0.0, ALU.mult, ALU.add))
            dve.tensor_scalar(RA2[0:H, :], BP2[0:H, :], -1.0, None, ALU.mult).then_inc(S.gates_cm, 1)

        def a_columns():
            dve.wait_ge(S.gates_back, 2)
            link(dve.tensor_copy(bcol[:], bt[:, :, 0:H]), S.c_ready)

        def g_step(n):
            if n >= 1:
                h = n - 1
                dve.wait_ge(S.g_ds, h + 1)
                dve.wait_ge(S.dcay_ready, 2)
                if h >= 1:
                    dve.wait_ge(S.g_o, h)
                link(dve.tensor_copy(ST[:, 0, :], PS[:, 6, 0:P]))
                for c in (1, 2):
                    link(dve.scalar_tensor_tensor(ST[:, c, :], ST[:, c - 1, :], dcay[:, h, c:c + 1],
                                                  PS[:, 6, c * P:c * P + P], ALU.mult, ALU.add))
                dve.engine_nop().then_inc(S.g_state, 1)
            if n < H:
                dve.wait_ge(S.g_keT, n + 1)
                for tb in range(TB):
                    a = dve.copy_predicated(AT[:, n % 2, tb, :], hmask[:].bitcast(I32), PS[:, 4, tb * P:tb * P + P])
                link(a, S.g_attn)

        def g_norm(tb):
            dve.wait_ge(S.g_ocp, H)
            for h in range(H):
                b = dve.bn_stats(hstat[:, h, :], GO[:, h, tb, :])
            link(b)
            for h in range(H):
                b = dve.bn_aggr(hmv[:, h, :], hstat[:, h, :])
            link(b)
            link(dve.tensor_tensor(hr[:], hmv[:, :, 0], hmv[:, :, 0], ALU.mult))
            link(dve.tensor_tensor(hr[:], hr[:], hmv[:, :, 1], ALU.add))
            inverse_root(9 + tb, hr[:], hr[:], RMS_EPS)
            for h in range(H):
                a = dve.scalar_tensor_tensor(GO[:, h, tb, :], GO[:, h, tb, :], hr[:, h:h + 1], hgain[:],
                                             ALU.mult, ALU.mult)
            link(a)

        def g_gate(half):
            dve.wait_ge(evac[half], S_OUT2 // 2)
            for tb in range(TB):
                hh = GO[:, 4 * half:4 * half + 4, tb, :]
                gg = G_G[:, tb, half * W:(half + 1) * W].rearrange("p (h d) -> p h d", d=DH)
                a = dve.tensor_tensor(hh, hh, gg, ALU.mult)
            link(a, S.g_y)

        def a_step(n):
            if n < H:
                h, e = n, n % 2
                dve.wait_ge(S.a_scores, h + 1)
                if h >= 2:
                    dve.wait_ge(S.a_pT, h - 1)
                for a, tb in ((0, 0), (P, 1), (2 * P, 1)):
                    b = dve.scalar_tensor_tensor(E2[:, e, a:a + P], PS[:, 4, a:a + P], bcol[:, tb, h:h + 1],
                                                 maskneg[:, a:a + P], ALU.add, ALU.add)
                link(b)
                dve.tensor_reduce(nmax[:, e, 0:1], E2[:, e, 0:P], AX, ALU.max, negate=True)
                link(dve.tensor_reduce(nmax[:, e, 1:2], E2[:, e, P:384], AX, ALU.max, negate=True), S.a_max)
            if 1 <= n <= H:
                e = (n - 1) % 2
                dve.wait_ge(S.a_exp, n)
                link(dve.reciprocal(psum_[:, e, :], psum_[:, e, :]))
                dve.tensor_scalar(E2[:, e, 0:P], E2[:, e, 0:P], psum_[:, e, 0:1], None, ALU.mult)
                link(dve.tensor_scalar(E2[:, e, P:384], E2[:, e, P:384], psum_[:, e, 1:2], None, ALU.mult), S.a_prob)
            if n >= 3:
                dve.wait_ge(S.a_out, n - 2)
                dve.tensor_copy(MIX[:, n - 3, :], PS[:, 6, 0:T]).then_inc(S.mix_a, 1)

        run_slabs(dve, split_lo, S_IN2, 14, plan(
            [(0, 1, wf_split), (0, 2, clear)],
            [(j, 3, lambda j=j: f_fix(j)) for j in range(2)],
            [(1 + j, 1, lambda j=j: f_cumulate(j)) for j in range(2)],
            [(2 + j, 3, lambda j=j: q_fix(j)) for j in range(2)],
            [(3 + j, 1, lambda j=j: k_fix(j)) for j in range(2)],
            [(*slot(GATES2), lambda: gate_sigmoid(1, H, LG2, LA2, LS2, fbias)),
             (*slot(GATES2 + 1), a_cumulate), (*slot(GATES2 + 2), a_columns)],
            [(*slot(HEADS2 + n), lambda n=n: g_step(n)) for n in range(H + 1)],
            [(*divmod(ATTN + n, UNITS), lambda n=n: a_step(n)) for n in range(H + 3)],
            [(10, 2, lambda: g_norm(0)), (11, 2, lambda: g_norm(1))],
            [(13, 1, lambda: g_gate(0))]))
        split_lo(dve, S_OUT2, 0)
        mix_lo(dve, 1, 0)
        split_lo(dve, S_OUT2, 1)
        g_gate(1)
        mix_lo(dve, 1, 1)
        mix_lo(dve, 1, 2)
        mix_lo(dve, 1, 3)
        run_slabs(dve, split_lo, S_OUT2, 4, plan(each(res_add(1.0), S_OUT2, 4)), True)
        rms_norm(11, NRM, 112, S.tm_ready)
        x_lead(3, S_FF)

        def col(a, n, t):
            return cols[:, a[0], ds(n * 4 + (t + a[1]), 1)] if not isinstance(n, int) else \
                cols[:, a[0], 4 * n + t + a[1]:4 * n + t + a[1] + 1]

        def gate_taps(n):
            dve.wait_ge(S.ff_y, n + 1)
            for back, place in ((1, (1, FC)), (2, (1, 0))):
                for t in range(4):
                    a = dve.scalar_tensor_tensor(FY[:, t, back:], cm_out(0)[:, t, 0:T - back], col(place, n, t),
                                                 FY[:, t, back:], ALU.mult, ALU.add)
                link(a)
            dve.engine_nop().then_inc(S.ff_conv, 1)
            dve.engine_nop().then_inc(evac[0], 1)

        def up_out(n, s):
            slab_ready(dve, s)
            dve.wait_ge(S.ff_silu, n + 1)
            dst = FA[:, ds(n * 4, 4), :] if not isinstance(n, int) else FA[:, 4 * n:4 * n + 4, :]
            link(dve.tensor_tensor(dst, FY[:], cm_out(1), ALU.mult), evac[1], S.ff_up)

        def ff_pair(n, s, first=False):
            if not first:
                split_lo(dve, s, 0)
                split_lo(dve, s, 1)
                up_out(n - 1, s - 1)
            split_lo(dve, s, 2)
            split_lo(dve, s, 3)
            split_lo(dve, s + 1, 0)
            split_lo(dve, s + 1, 1)
            gate_taps(n)
            split_lo(dve, s + 1, 2)
            split_lo(dve, s + 1, 3)

        ff_pair(0, S_FF, True)
        with dve.Fori(1, FPAIRS) as i:
            link.enter(i, 1, 3)
            ff_pair(i, i * 2 + S_FF)
        link.leave(1, FPAIRS - 1)

        def down_lo(j, s, u0=0, u1=UNITS):
            for u in range(u0, u1):
                split_lo(dve, s, u)
                dve.wait_ge(S.ah_full, j * UNITS + u + 1)
                dve.tensor_tensor(al[u % 2][:], FA[:, ds(j * UNITS + u, 1), :].rearrange("p o n -> p (o n)")
                                  if not isinstance(j, int) else FA[:, j * UNITS + u, :],
                                  ah[u % 2][:].bitcast(F32), ALU.subtract).then_inc(S.al_full, 1)

        down_lo(0, S_DOWN, 0, 1)
        up_out(FPAIRS - 1, S_FF + 2 * FPAIRS - 1)
        down_lo(0, S_DOWN, 1)
        with dve.Fori(1, NDOWN) as i:
            down_lo(i, i + S_DOWN)
        for tb in range(TB):
            dve.wait_ge(S.down_done, tb + 1)
            for b in range(4):
                r = RES[:, tb, b * W:(b + 1) * W]
                a = dve.tensor_tensor(r, r, PS[:, 4 * tb + b, :], ALU.add)
            link(a, S.summed)
        dve.wait_ge(S.norm_in, 128)
        for tb in range(TB):
            r1 = rstd[:, tb:tb + 1]
            dve.wait_ge(S.squares, tb + 1)
            link(dve.tensor_scalar(msq[:, tb:tb + 1], msq[:, tb:tb + 1], 1.0 / D, None, ALU.mult))
            inverse_root(12 + tb, r1, msq[:, tb:tb + 1], RMS_EPS)
            dve.scalar_tensor_tensor(RES[:, tb, :], RES[:, tb, :], r1, GAIN[:], ALU.mult, ALU.mult).then_inc(S.final, 1)

    @block.tensor
    def _(pe):
        pe.wait_ge(S.ident_ready, 1)
        turn_x(pe, 0, RES)

        def turn_columns():
            pe.wait_ge(S.stage_in, 7 * 16)
            pe.wait_ge(S.xt_lo, 8)
            for a in range(3):
                m = pe.transpose(PS[:, 7, a * P:a * P + P], stage[:, a, :], ident[:])
            m.then_inc(S.cols_ps, 1)

        def gate_logits(width, h, l, ready):
            pe.wait_ge(ready, 1)
            o = PS[0:width, 6, 0:T]
            for d in range(DC):
                pe.matmul(o, h[:, d, :], XH[:, d, :], start=d == 0, stop=False)
                pe.matmul(o, l[:, d, :], XH[:, d, :], start=False, stop=False)
                m = pe.matmul(o, h[:, d, :], XL[:, d, :], start=False, stop=d == DC - 1)
            m.then_inc(S.gate_ps, 1)

        def forgets_down():
            pe.wait_ge(S.gates_ready, 1)
            pe.wait_ge(S.cols_ready, 1)
            pe.matmul(PS[0:H, 7, 0:T], ident[0:16, H:16], LS1[0:16, :], start=True, stop=True).then_inc(S.gates_low, 1)

        def gates_return(n, src):
            pe.wait_ge(S.gates_cm, n + 1)
            for tb in range(TB):
                m = pe.transpose(PS[:, 6, tb * P:tb * P + P], src[:, tb * P:tb * P + P], ident[:])
            m.then_inc(S.gates_back, 1)

        def m_head(h):
            if h >= 1:
                pe.wait_ge(S.m_prob, h)
            if h < H:
                if h == 0:
                    pe.wait_ge(evac[0], 2)
                    pe.wait_ge(evac[1], 2)
                pe.matmul(PS[:, 4, 0:T], KT[:, h, 0:P], QT[:, h, :], start=True, stop=True)
                pe.matmul(PS[:, 4, T:384], KT[:, h, P:T], QT[:, h, P:T], start=True, stop=True)
                pe.matmul(PS[:, 5, 0:T], bcast(ident[:, h:h + 1], [P]), RA1[:], start=True,
                          stop=True).then_inc(S.m_scores, 1)
            if h >= 1:
                g = h - 1
                if g == 0:
                    pe.wait_ge(evac[0], 3)
                    pe.wait_ge(evac[1], 3)
                else:
                    pe.wait_ge(S.m_numcp, g)
                o = PS[:, 7, 0:TB * (DH + 1)].rearrange("p (b d) -> p b d", b=TB)
                pe.matmul(o[:, 0, :], PM1[:, 0:P], VX[:, 0, g, 0:DH + 1], start=True, stop=True)
                pe.matmul(o[:, 1, :], PM1[:, P:T], VX[:, 0, g, 0:DH + 1], start=True, stop=False)
                pe.matmul(o[:, 1, :], PM1[:, T:384], VX[:, 1, g, 0:DH + 1], start=False,
                          stop=True).then_inc(S.m_num, 1)

        def turn_heads(half, src, y, turned, mix):
            pe.wait_ge(y, half + 1)
            if half == 1:
                pe.wait_ge(S.mix_y, mix + 1)
            for tb in range(TB):
                for k in range(4):
                    m = pe.transpose(PS[:, 6 + tb, k * P:k * P + P], src(tb, 4 * half + k), ident[:])
            m.then_inc(turned, 1)

        def m_turn(half):
            pe.wait_ge(S.m_numcp, H)
            turn_heads(half, lambda tb, h: HN[:, tb, h, 0:DH], S.m_y, S.m_turn, 0)

        def g_turn(half):
            pe.wait_ge(S.mix_a, H)
            turn_heads(half, lambda tb, h: GO[:, h, tb, :], S.g_y, S.g_turn, 2)

        def turn_keys():
            pe.wait_ge(S.keys_in, 16 * 2 * H)
            pe.wait_ge(S.mix_y, 2)
            for n in range(4):
                for k in range(4):
                    m = pe.transpose(PS[:, 4 + n, k * P:k * P + P], KR[:, 4 * n + k, :], ident[:])
                m.then_inc(S.keyT_ps, 1)

        m_events = plan(
            [(1, 1, turn_columns)],
            [(*slot(GATES1), lambda: gate_logits(16, wg_h, wg_l, S.wg_lo)), (*slot(GATES1 + 1), forgets_down),
             (*slot(GATES1 + 2), lambda: gates_return(0, BP1))],
            [(*divmod(HEADS1 + 2 * h, UNITS), lambda h=h: m_head(h)) for h in range(H + 1)],
            [(13, 2, lambda: m_turn(0))])
        for s in range(S_IN, S_OUT):
            pe_slab(pe, s // 2, s % 2, s not in (4, 5, 12, 13), m_events, s, (S.xt_lo, 5) if s == 0 else None)
        out_events = plan([(0, 0, lambda: m_turn(1)), (3, 2, turn_keys)])
        for s in range(S_OUT, S_OUT + 4):
            pe_slab(pe, s // 2, s % 2, False, out_events, s - S_OUT, (S.mix_lo, 1) if s == S_OUT else None)

        pe.wait_ge(S.keyT, 4)
        turn_x(pe, 1, RES)

        def scores(q):
            pe.wait_ge(evac[q % 2], (S_WQ + q) // 2 + 1)
            for tb in range(TB):
                n = TB * q + tb
                if n >= 4:
                    pe.wait_ge(S.scores_cp, n - 3)
                for k in range(4):
                    m = pe.matmul(PS[:, 4 + n % 4, k * P:k * P + P], PQ[:, 4 * q + k, tb * P:tb * P + P],
                                  KX[:, 4 * q + k, :], start=True, stop=True)
                m.then_inc(S.score_ps, 1)

        wq_events = plan([(q + 1, 0, lambda q=q: scores(q)) for q in range(3)])
        for s in range(S_WQ, S_WQ + 4):
            pe_slab(pe, s // 2, s % 2, True, wq_events, s - S_WQ, (S.xt_lo, 13) if s == S_WQ else None)
        scores(3)
        pe.wait_ge(S.scores_cp, 8)

        def v_rows(n, tb, start=False):
            for k in range(TOPK):
                pe.wait_ge(v_full[k % RING], (n * (TOPK // RING) + k // RING + 1) * 16)
                pe.wait_ge(S.diag_ready, n * TOPK + k + 1)
                for b in range(4):
                    m = pe.matmul(PS[:, 4 * tb + b, :], diag[:, k, :], vb[k % RING][:, b * W:(b + 1) * W],
                                  start=start and k == 0, stop=False, skip_group_check=True)
                m.then_inc(S.v_done, 1)

        v_rows(0, 0, True)
        v_rows(1, 1, True)
        with pe.Fori(1, H - 1) as i:
            for tb in range(TB):
                v_rows(i * 2 + tb, tb)
        v_rows(LAST - 1, 0)
        for j, k in enumerate(PE_ROWS):
            if j == 6:
                turn_x(pe, 2, NRM, (0,))
            pe.wait_ge(last_full[k % RING], (k // RING + 1) * 16)
            pe.wait_ge(S.diag_ready, LAST * TOPK + j + 1)
            for b in range(4):
                m = pe.matmul(PS[:, 4 + b, :], diag[:, k, :], ub[k % RING][:, b * W:(b + 1) * W],
                              start=False, stop=False, skip_group_check=True)
            m.then_inc(S.v_done, 1)
        pe.wait_ge(S.v_done, LAST * TOPK + len(PE_ROWS))
        pe.nop().then_inc(S.acc_done, 1)

        turn_x(pe, 2, NRM, (1,))
        def g_step(n):
            if 1 <= n <= H:
                h = n - 1
                pe.wait_ge(S.g_ke, h + 1)
                if h == 0:
                    pe.wait_ge(S.c_ready, 1)
                    pe.wait_ge(evac[0], S_IN2 // 2 + 3)
                    pe.wait_ge(evac[1], S_IN2 // 2 + 3)
                else:
                    pe.wait_ge(S.g_state, h)
                for c in range(NCH - 1):
                    m = pe.matmul(PS[:, 6, c * P:c * P + P], KE[:, c, :],
                                  G_V[:, c // 2, h * DH:(h + 1) * DH], start=True, stop=True)
                m.then_inc(S.g_ds, 1)
            if n >= 2:
                g = n - 2
                pe.wait_ge(S.g_attn, g + 1)
                pe.wait_ge(S.g_state, g + 1)
                if g >= 1:
                    pe.wait_ge(S.g_ocp, g)
                for tb in range(TB):
                    o = PS[:, 7, tb * P:tb * P + P]
                    pe.matmul(o, AT[:, g % 2, tb, :], G_V[:, tb, g * DH:(g + 1) * DH], start=True, stop=True,
                              skip_group_check=True)
                    for c in range(2 * tb, 2 * tb + 2):
                        if c == 0:
                            continue
                        r = slice((c % 2) * CHUNK, (c % 2) * CHUNK + CHUNK)
                        m = pe.matmul(o[r, :], G_Q[:, g, c * CHUNK:(c + 1) * CHUNK], ST[:, c - 1, :],
                                      start=False, stop=True, skip_group_check=True)
                m.then_inc(S.g_o, 1)
            if n < H:
                if n == 0:
                    pe.wait_ge(S.k_decayed, 2)
                else:
                    pe.wait_ge(S.g_attn, n)
                    pe.wait_ge(S.g_ke, n)
                for tb in range(TB):
                    y = slice(tb * P, tb * P + P)
                    pe.matmul(PS[:, 4, y], G_K[:, n, y], G_Q[:, n, y], start=True, stop=True)
                for tb in range(TB):
                    y = slice(tb * P, tb * P + P)
                    m = pe.transpose(PS[:, 5, y], G_E[:, n, y], ident[:])
                m.then_inc(S.g_keT, 1)

        def a_step(n):
            if 2 <= n < H + 2:
                g = n - 2
                pe.wait_ge(S.a_prob, g + 1)
                if g >= 1:
                    pe.wait_ge(S.a_pTcp, g)
                for k in range(3):
                    m = pe.transpose(PS[:, 5, k * P:k * P + P], E2[:, g % 2, k * P:k * P + P], ident[:])
                m.then_inc(S.a_pT, 1)
            if n < H:
                if n == 0:
                    pe.wait_ge(evac[0], S_IN2 // 2 + 5)
                    pe.wait_ge(evac[1], S_IN2 // 2 + 5)
                else:
                    pe.wait_ge(S.a_max, n)
                for tb, (a, b) in enumerate(((0, P), (P, 384))):
                    y = slice(tb * P, tb * P + P)
                    pe.matmul(PS[:, 4, a:b], FQ[:, n, y], FK[:, n, 0:b - a], start=True, stop=False)
                    m = pe.matmul(PS[:, 4, a:b], bcast(ident[:, n:n + 1], [P]), RA2[:, 0:b - a], start=False, stop=True)
                m.then_inc(S.a_scores, 1)
            if n >= 3:
                g = n - 3
                e = g % 2
                pe.wait_ge(S.a_pTcp, g + 1)
                pe.wait_ge(evac[g // 4], S_IN2 // 2 + 6)
                if g >= 1:
                    pe.wait_ge(S.mix_a, g)
                v = slice(g * DH, (g + 1) * DH)
                pe.matmul(PS[:, 6, 0:T], FV[:, 0, v], PM2[:, e, 0:T], start=True, stop=True)
                pe.matmul(PS[:, 6, P:T], FV[:, 1, v], PM2[:, e, T:384], start=False, stop=True,
                          skip_group_check=True).then_inc(S.a_out, 1)

        in2_events = plan(
            [(*slot(GATES2), lambda: gate_logits(H, wf_h, wf_l, S.wf_lo)),
             (*slot(GATES2 + 2), lambda: gates_return(1, BP2))],
            [(*slot(HEADS2 + n), lambda n=n: g_step(n)) for n in range(H + 2)],
            [(*divmod(ATTN + n, UNITS), lambda n=n: a_step(n)) for n in range(H + 3)],
            [(13, 2, lambda: g_turn(0))])
        for s in range(S_IN2, S_OUT2):
            n = s - S_IN2
            pe_slab(pe, s // 2, s % 2, n not in (4, 5, 10, 11, 12, 13), in2_events, n,
                    (S.xt_lo, 21) if n == 0 else None)
        for s in range(S_OUT2, S_OUT2 + 4):
            pe_slab(pe, s // 2, s % 2, False, plan([(0, 0, lambda: g_turn(1))]), s - S_OUT2,
                    (S.mix_lo, 5) if s == S_OUT2 else None)

        pe.wait_ge(S.mix_y, 4)
        turn_x(pe, 3, NRM)
        pe_slab(pe, S_FF // 2, 0, True, x_in=(S.xt_lo, 29))
        pe_slab(pe, S_FF // 2, 1, True)
        with pe.Fori(1, FPAIRS) as i:
            for k in range(2):
                pe_slab(pe, i + S_FF // 2, k, True)

        def down(j, s, first=False, last=False):
            for u in range(UNITS):
                k = u % 2
                pe.wait_ge(lo_full[k], s * 2 + u // 2 + 1)
                pe.wait_ge(S.al_full, j * UNITS + u + 1)
                for tb in range(TB):
                    y = slice(tb * P, tb * P + P)
                    for b in range(4):
                        o = PS[:, 4 * tb + b, :]
                        for n, (x, w) in enumerate(((ah, wh), (ah, wl), (al, wh))):
                            m = pe.matmul(o, x[k][:, y], w[k][:, b, :], start=first and u == 0 and n == 0,
                                          stop=last and u == UNITS - 1 and n == 2, skip_group_check=True)
                    if last and u == UNITS - 1:
                        m.then_inc(S.down_done, 1)
                if not (last and u == UNITS - 1):
                    m.then_inc(w_free[k], 1)

        pe.wait_ge(evac[0], S_DOWN // 2)
        pe.wait_ge(evac[1], S_DOWN // 2)
        down(0, S_DOWN, True)
        with pe.Fori(1, NDOWN - 1) as i:
            down(i, i + S_DOWN)
        down(NDOWN - 1, S_DOWN + NDOWN - 1, last=True)


_INS = ["x", "ln_in_g", "ln_in_b", "w_in", "b_gate", "conv_w", "conv_b", "mh_norm_g", "w_out", "ln1_g", "ln1_b",
        "peer_wq", "peer_keys", "peer_u", "peer_v", "ln2_g", "ln2_b", "norm1_gain_2", "w_in_2", "hgrn_lb_param_2",
        "hgrn_norm_gain_2", "fox_gate_bias_2", "w_out_2", "norm2_gain_2", "w_ffn_gate_2", "w_ffn_up_2",
        "ffn_conv_w_2", "ffn_conv_b_2", "w_ffn_down_2", "final_norm_gain_2"]


def kernel(**inputs):
    import concourse.bacc as bacc
    import numpy as np
    from concourse.bass_utils import run_bass_kernel_spmd

    nc = bacc.Bacc("TRN2", target_bir_lowering=False, num_devices=1)
    arrays, aps = {}, {}
    for name in _INS:
        a = np.ascontiguousarray(inputs[name])
        arrays[f"in_{name}"] = a
        aps[name] = nc.dram_tensor(f"in_{name}", a.shape, mybir.dt.from_np(a.dtype), kind="ExternalInput").ap()
    out = nc.dram_tensor("out_y", (1, T, D), F32, kind="ExternalOutput").ap()
    block_kernel(nc, aps, out)
    r = run_bass_kernel_spmd(nc, [arrays], core_ids=[0])
    return r.results[0]["out_y"]
```
